# Optimizing a Trainium2 kernel written in Bass

```python
import jax, jax.numpy as jnp
from jax import lax
import numpy as np

D_MODEL = 1024
BATCH = 1
SEQ = 1024
DEPTH = 1
DEC_BATCH = 8
DEC_SEQ = 16
PAST_LEN = 256

CHUNK = 64
MIX_WIDTH = D_MODEL
POOL_WIDTH = MIX_WIDTH // 2
POOL_GROUPS = 4
POOL_GROUP_DIM = POOL_WIDTH // POOL_GROUPS
POOL_WINDOWS = (2, 4, 8, 16)
POOL_HIST = max(POOL_WINDOWS) - 1
GMLP_WIDTH = MIX_WIDTH - POOL_WIDTH
GMLP_HEADS = 4
GMLP_HEAD_DIM = GMLP_WIDTH // GMLP_HEADS
GMLP_CHUNK = 128
PEER_HEADS = 8
PEER_NKEYS = 128
PEER_EXPERTS = PEER_NKEYS * PEER_NKEYS
PEER_TOPK = 16
PEER_DKEY = 256
PEER_DHALF = PEER_DKEY // 2
PEER_BLOCK = 256
N_MOD = 6
EPS = 1e-6

kernel_name = "hybrid_pool_gmlp_peer_stream_step"

def rmsnorm(x, g):
    xf = x.astype(jnp.float32)
    y = xf * lax.rsqrt(jnp.mean(xf * xf, axis=-1, keepdims=True) + EPS)
    return (y * g.astype(jnp.float32)).astype(x.dtype)

def modulate(h, shift, scale):
    return h * (1 + scale[:, None, :]) + shift[:, None, :]

def pool_mixer(p, hist, pos0, pool_w, pool_scale):
    B, T, _ = p.shape
    padded = jnp.concatenate([hist, p], axis=1).astype(jnp.float32)
    csum = jnp.cumsum(padded, axis=1)
    csum = jnp.concatenate([jnp.zeros_like(csum[:, :1]), csum], axis=1)
    end = csum[:, POOL_HIST + 1:]
    pos = pos0 + jnp.arange(T)
    means = []
    for g, w in enumerate(POOL_WINDOWS):
        sl = slice(g * POOL_GROUP_DIM, (g + 1) * POOL_GROUP_DIM)
        start = csum[:, POOL_HIST + 1 - w:POOL_HIST + 1 - w + T, sl]
        cnt = jnp.minimum(pos + 1, w).astype(jnp.float32)[None, :, None]
        means.append((end[..., sl] - start) / cnt)
    diff = jnp.concatenate(means, axis=-1) - p.astype(jnp.float32)
    diff = diff.reshape(B, T, POOL_GROUPS, POOL_GROUP_DIM).astype(p.dtype)
    out = jnp.einsum('btgc,gcd->btgd', diff, pool_w).reshape(B, T, POOL_WIDTH)
    return out * pool_scale

def gmlp_mixer(u, v, norm_g, ws, bs):
    B, T, _ = v.shape
    vn = rmsnorm(v.reshape(B, T, GMLP_HEADS, GMLP_HEAD_DIM), norm_g.reshape(GMLP_HEADS, GMLP_HEAD_DIM))
    n_chunk = -(-T // GMLP_CHUNK)
    pad = n_chunk * GMLP_CHUNK - T
    vp = jnp.pad(vn, ((0, 0), (0, pad), (0, 0), (0, 0))).reshape(B, n_chunk, GMLP_CHUNK, GMLP_HEADS, GMLP_HEAD_DIM)
    mask = jnp.tril(jnp.ones((GMLP_CHUNK, GMLP_CHUNK), dtype=bool))
    wm = jnp.where(mask[None], ws, jnp.zeros_like(ws))
    s = jnp.einsum('hij,bnjhc->bnihc', wm, vp) + bs.T[None, None, :, :, None]
    s = s.reshape(B, n_chunk * GMLP_CHUNK, GMLP_HEADS, GMLP_HEAD_DIM)[:, :T].reshape(B, T, GMLP_WIDTH)
    return u * s, vn.reshape(B, T, GMLP_WIDTH)

def peer_retrieve(h, wq, keys):
    N = h.shape[0]
    q = (h @ wq).reshape(N, PEER_HEADS, 2, PEER_DHALF).astype(jnp.float32)
    s = jnp.einsum('nhpc,hpkc->nhpk', q, keys.astype(jnp.float32))
    sv, si = lax.top_k(s, PEER_TOPK)
    comb = sv[:, :, 0, :, None] + sv[:, :, 1, None, :]
    cv, ci = lax.top_k(comb.reshape(N, PEER_HEADS, PEER_TOPK * PEER_TOPK), PEER_TOPK)
    i1 = jnp.take_along_axis(si[:, :, 0], ci // PEER_TOPK, axis=-1)
    i2 = jnp.take_along_axis(si[:, :, 1], ci % PEER_TOPK, axis=-1)
    expert = i1 * PEER_NKEYS + i2
    gate = jax.nn.softmax(cv, axis=-1)
    return expert, gate

def peer_apply(h, expert, gate, u_tab, v_tab):
    N, D = h.shape
    blk = min(PEER_BLOCK, N)
    nb = -(-N // blk)
    pad = nb * blk - N
    hp = jnp.pad(h, ((0, pad), (0, 0))).reshape(nb, blk, D)
    ep = jnp.pad(expert, ((0, pad), (0, 0), (0, 0))).reshape(nb, blk, PEER_HEADS, PEER_TOPK)
    gp = jnp.pad(gate.astype(h.dtype), ((0, pad), (0, 0), (0, 0))).reshape(nb, blk, PEER_HEADS, PEER_TOPK)

    def one(args):
        hb, eb, gb = args
        ub = jnp.take(u_tab, eb, axis=0)
        vb = jnp.take(v_tab, eb, axis=0)
        a = jax.nn.gelu(jnp.einsum('nd,nhkd->nhk', hb, ub), approximate=False)
        return jnp.einsum('nhk,nhkd->nd', gb * a, vb)

    out = lax.map(one, (hp, ep, gp))
    return out.reshape(nb * blk, D)[:N]

def block(x, c, pool_hist, pos0, w_ada, b_ada, g1, w_in, pool_w, pool_scale,
          gmlp_g, gmlp_ws, gmlp_bs, w_out, g2, peer_wq, peer_keys, peer_u, peer_v):
    B, T, D = x.shape
    mod = (jax.nn.silu(c) @ w_ada + b_ada).reshape(B, N_MOD, D)
    shift1, scale1, gate1, shift2, scale2, gate2 = (mod[:, i] for i in range(N_MOD))
    h = modulate(rmsnorm(x, g1), shift1, scale1)
    z = h @ w_in
    p = z[..., :POOL_WIDTH]
    u = jax.nn.gelu(z[..., POOL_WIDTH:POOL_WIDTH + GMLP_WIDTH], approximate=False)
    v = jax.nn.gelu(z[..., POOL_WIDTH + GMLP_WIDTH:], approximate=False)
    pool_out = pool_mixer(p, pool_hist, pos0, pool_w, pool_scale)
    gm_out, vn = gmlp_mixer(u, v, gmlp_g, gmlp_ws, gmlp_bs)
    mix = jnp.concatenate([pool_out, gm_out], axis=-1) @ w_out
    x = x + gate1[:, None, :] * mix
    h2 = modulate(rmsnorm(x, g2), shift2, scale2).reshape(B * T, D)
    expert, gate = peer_retrieve(h2, peer_wq, peer_keys)
    ff = peer_apply(h2, expert, gate, peer_u, peer_v).reshape(B, T, D)
    x = x + gate2[:, None, :] * ff
    new_hist = jnp.concatenate([pool_hist, p], axis=1)[:, -POOL_HIST:]
    return x, new_hist, vn

def setup_inputs(seed: int = 0) -> dict:
    key = jax.random.key(seed)
    ks = jax.random.split(key, 24)
    f32 = jnp.float32
    nrm = lambda k, shape, s: (jax.random.normal(k, shape, f32) * s).astype(f32)
    D = D_MODEL
    return {
        "x_prompt": nrm(ks[0], (BATCH, SEQ, D), 1.0),
        "x_sample": nrm(ks[1], (DEC_BATCH, DEC_SEQ, D), 1.0),
        "cache_pool": nrm(ks[2], (DEPTH, DEC_BATCH, POOL_HIST, POOL_WIDTH), 1.0),
        "c_prompt": nrm(ks[3], (BATCH, D), 1.0),
        "c_sample": nrm(ks[4], (DEC_BATCH, D), 1.0),
        "w_ada": nrm(ks[5], (DEPTH, D, N_MOD * D), 0.5 * D ** -0.5),
        "b_ada": nrm(ks[6], (DEPTH, N_MOD * D), 0.01),
        "g_norm1": 1.0 + nrm(ks[7], (DEPTH, D), 0.02),
        "w_in": nrm(ks[8], (DEPTH, D, POOL_WIDTH + 2 * GMLP_WIDTH), D ** -0.5),
        "pool_w": nrm(ks[9], (DEPTH, POOL_GROUPS, POOL_GROUP_DIM, POOL_GROUP_DIM), POOL_GROUP_DIM ** -0.5),
        "pool_scale": 1.0 + nrm(ks[10], (DEPTH, POOL_WIDTH), 0.02),
        "gmlp_norm_g": 1.0 + nrm(ks[11], (DEPTH, GMLP_WIDTH), 0.02),
        "gmlp_ws": nrm(ks[12], (DEPTH, GMLP_HEADS, GMLP_CHUNK, GMLP_CHUNK), GMLP_CHUNK ** -0.5),
        "gmlp_bs": nrm(ks[13], (DEPTH, GMLP_HEADS, GMLP_CHUNK), 0.02),
        "w_out": nrm(ks[14], (DEPTH, MIX_WIDTH, D), MIX_WIDTH ** -0.5),
        "g_norm2": 1.0 + nrm(ks[15], (DEPTH, D), 0.02),
        "peer_wq": nrm(ks[16], (DEPTH, D, PEER_HEADS * PEER_DKEY), D ** -0.5),
        "peer_keys": nrm(ks[17], (DEPTH, PEER_HEADS, 2, PEER_NKEYS, PEER_DHALF), PEER_DHALF ** -0.5),
        "peer_u": nrm(ks[18], (DEPTH, PEER_EXPERTS, D), D ** -0.5),
        "peer_v": nrm(ks[19], (DEPTH, PEER_EXPERTS, D), PEER_HEADS ** -0.5),
        "g_final": 1.0 + nrm(ks[20], (D,), 0.02),
    }

def reference(x_prompt, x_sample, cache_pool, c_prompt, c_sample, w_ada, b_ada, g_norm1, w_in,
              pool_w, pool_scale, gmlp_norm_g, gmlp_ws, gmlp_bs, w_out, g_norm2, peer_wq,
              peer_keys, peer_u, peer_v, g_final):
    xp, xs = x_prompt, x_sample
    pool_prompt_new, pool_sample_new, gmlp_v_sample_new = [], [], []
    for l in range(DEPTH):
        weights = (w_ada[l], b_ada[l], g_norm1[l], w_in[l], pool_w[l], pool_scale[l],
                   gmlp_norm_g[l], gmlp_ws[l], gmlp_bs[l], w_out[l], g_norm2[l],
                   peer_wq[l], peer_keys[l], peer_u[l], peer_v[l])
        hist0 = jnp.zeros((xp.shape[0], POOL_HIST, POOL_WIDTH), xp.dtype)
        xp, hp, _ = block(xp, c_prompt, hist0, 0, *weights)
        xs, hs, vs = block(xs, c_sample, cache_pool[l], PAST_LEN, *weights)
        pool_prompt_new.append(hp)
        pool_sample_new.append(hs)
        gmlp_v_sample_new.append(vs)
    y_prompt = rmsnorm(xp, g_final)
    y_sample = rmsnorm(xs, g_final)
    return (y_prompt, y_sample, jnp.stack(pool_prompt_new), jnp.stack(pool_sample_new), jnp.stack(gmlp_v_sample_new))


_drawn_inputs = setup_inputs


def setup_inputs(seed=0):
    import zlib

    import numpy as np

    out = dict(_drawn_inputs(seed))
    spreads = {}
    factors = {'b_ada': 4.083,
     'g_norm1': 2.884,
     'pool_scale': 8.0,
     'gmlp_norm_g': 7.663,
     'gmlp_bs': 22.408,
     'g_norm2': 24.644,
     'g_final': 8.916}
    for name, (base, spread) in spreads.items():
        noise = np.random.default_rng([zlib.crc32(name.encode()), seed]).standard_normal(out[name].shape)
        drawn = base * np.exp(spread * noise) if base else spread * noise
        out[name] = __import__('jax').numpy.asarray(drawn.astype(out[name].dtype))
    for name, factor in factors.items():
        out[name] = (out[name] * factor).astype(out[name].dtype)
    return out
```

```python
import concourse.bass as bass
from concourse import mybir
from contextlib import ExitStack

F32 = mybir.dt.float32
F32R = mybir.dt.float32r
BF16 = mybir.dt.bfloat16
U32 = mybir.dt.uint32
ALU = mybir.AluOpType
ACT = mybir.ActivationFunctionType
AX = mybir.AxisListType

P = 128
D = 1024
KD = D // P
HALF = 512
PROMPT_TILES = 8
TILES = 9
STREAMS, STEP = 8, 16
HIST = 15
ZW = 1536
GROUPS = 4
HEADS = 8
TOPK = 16
NKEYS = 128
BLOCK = 64
BLOCKS = TILES * P // BLOCK
BATCH = 8
NEG = -3.0e38
EPS = 1e-6
MODS = 6
SHIFT1, SCALE1, GATE1, SHIFT2, SCALE2, GATE2 = range(MODS)


class Order:

    def __init__(self, eng, sem):
        self.eng, self.sem, self.base, self.n = eng, sem, 0, 0

    def loop(self, base):
        self.base, self.n = base, 0

    def mark(self, ins):
        ins.then_inc(self.sem, 1)
        self.n += 1

    def settle(self):
        self.eng.wait_ge(self.sem, self.base + self.n)

    def then(self, ins):
        self.mark(ins)
        self.settle()


def sems(nc, ctx, stage, names):
    made = {n: ctx.enter_context(nc.semaphore(f"{stage}_{n}")) for n in names.split()}
    return type("Sems", (), made)


def wait(eng, sem, value):
    if not isinstance(value, int) or value > 0:
        eng.wait_ge(sem, value)


def sbuf(nc, ctx, name, shape, dtype=F32):
    return ctx.enter_context(nc.sbuf_tensor(name, shape, dtype))


def psum(nc, ctx, name, shape, dtype=F32):
    return ctx.enter_context(nc.psum_tensor(name, shape, dtype))


def modulation(nc, ctx, c_prompt, c_sample, w_ada, b_ada, g1, g2, selector_in, ident_in, mod_rows):
    S = sems(nc, ctx, "mod", "consts silu cT_ps cT w0 w1 w2 rows_ps rows spread_ps spread norm_g stored")
    NC = 1 + STREAMS
    CHUNKS = MODS * D // HALF
    with ExitStack() as mem:
        c_rows = sbuf(nc, mem, "c_rows", [NC, D])
        c_silu = sbuf(nc, mem, "c_silu", [NC, D])
        cT = sbuf(nc, mem, "cT", [P, KD, 16])
        ident = sbuf(nc, mem, "ident_a", [P, P])
        selector = sbuf(nc, mem, "selector", [NC, 2, P])
        bias = sbuf(nc, mem, "bias", [NC, MODS * D])
        norm_g = sbuf(nc, mem, "norm_g", [P, 2, D])
        w = [sbuf(nc, mem, f"w_ada{s}", [P, KD, HALF]) for s in range(3)]
        rows = [sbuf(nc, mem, f"mod_row{s}", [NC, HALF]) for s in range(2)]
        spread = sbuf(nc, mem, "mod_spread", [P, 2, MODS, D])
        cT_ps = psum(nc, mem, "cT_ps", [P, KD, 16])
        rows_ps = [psum(nc, mem, f"rows_ps{s}", [NC, HALF]) for s in range(2)]
        spread_ps = [psum(nc, mem, f"spread_ps{s}", [P, 2, HALF]) for s in range(2)]
        w_loaded = [S.w0, S.w1, S.w2]
        w_view = w_ada.rearrange("(k p) n -> p k n", p=P)
        CONSTS = 16 * 5
        block = mem.enter_context(nc.Block())

        @block.sync
        def _(sp):
            sp.dma_start(c_rows[0:1, :], c_prompt).then_inc(S.consts, 16)
            sp.dma_start(c_rows[1:NC, :], c_sample).then_inc(S.consts, 16)
            sp.dma_start(ident[:, :], ident_in).then_inc(S.consts, 16)
            sp.dma_start(selector[:, :, :], selector_in).then_inc(S.consts, 16)
            sp.dma_start(bias[:, :], b_ada.partition_broadcast(NC)).then_inc(S.consts, 16)
            for c in range(CHUNKS):
                if c >= 3:
                    sp.wait_ge(S.rows_ps, c - 2)
                sp.dma_start(w[c % 3][:, :, :], w_view[:, :, c * HALF:(c + 1) * HALF]).then_inc(w_loaded[c % 3], 16)
                if c == 0:
                    sp.dma_start(norm_g[:, 0, :], g1.partition_broadcast(P)).then_inc(S.norm_g, 16)
                    sp.dma_start(norm_g[:, 1, :], g2.partition_broadcast(P)).then_inc(S.norm_g, 16)

        @block.scalar
        def _(act):
            act.wait_ge(S.consts, CONSTS)
            nc.scalar.activation(c_silu[:, :], c_rows[:, :], ACT.Silu).then_inc(S.silu, 1)
            for m in range(MODS):
                act.wait_ge(S.spread, 2 * m + 2)
                act.dma_start(mod_rows[:, m, :, :].rearrange("k p n -> p k n"), spread[:, :, m, :])\
                    .then_inc(S.stored, 16)
            act.wait_ge(S.stored, 16 * MODS)

        @block.vector
        def _(dve):
            dve.wait_ge(S.cT_ps, 1)
            nc.vector.tensor_copy(cT[:, :, 0:NC], cT_ps[:, :, 0:NC]).then_inc(S.cT, 1)

            def finish(c):
                m, half = c // 2, slice(c % 2 * HALF, (c % 2 + 1) * HALF)
                dve.wait_ge(S.spread_ps, c + 1)
                if m in (SCALE1, SCALE2):
                    for kind in range(2):
                        last = nc.vector.scalar_tensor_tensor(
                            out=spread[:, kind, m, half], in0=spread_ps[c % 2][:, kind, :], scalar=1.0,
                            in1=norm_g[:, m // 3, half], op0=ALU.add, op1=ALU.mult)
                else:
                    last = nc.vector.tensor_copy(spread[:, :, m, half], spread_ps[c % 2][:, :, :])
                last.then_inc(S.spread, 1)

            for c in range(CHUNKS):
                dve.wait_ge(S.rows_ps, c + 1)
                if c >= 2:
                    dve.wait_ge(S.spread_ps, c - 1)
                nc.vector.tensor_tensor(rows[c % 2][:, :], rows_ps[c % 2][:, :], bias[:, c * HALF:(c + 1) * HALF],
                                        ALU.add).then_inc(S.rows, 1)
                if c == 2:
                    dve.wait_ge(S.norm_g, 32)
                if c:
                    finish(c - 1)
            finish(CHUNKS - 1)

        @block.tensor
        def _(pe):
            pe.wait_ge(S.consts, CONSTS)
            pe.wait_ge(S.silu, 1)
            for k in range(KD):
                last = nc.tensor.transpose(cT_ps[:, k, 0:NC], c_silu[:, k * P:(k + 1) * P], ident[0:NC, 0:NC])
            last.then_inc(S.cT_ps, 1)
            pe.wait_ge(S.cT, 1)

            def spread_rows(c):
                pe.wait_ge(S.rows, c + 1)
                if c >= 2:
                    pe.wait_ge(S.spread, c - 1)
                for kind in range(2):
                    last = nc.tensor.matmul(spread_ps[c % 2][:, kind, :], selector[:, kind, :], rows[c % 2][:, :],
                                            start=True, stop=True)
                last.then_inc(S.spread_ps, 1)

            for c in range(CHUNKS):
                pe.wait_ge(w_loaded[c % 3], (c // 3 + 1) * 16)
                if c >= 2:
                    pe.wait_ge(S.rows, c - 1)
                for k in range(KD):
                    last = nc.tensor.matmul(rows_ps[c % 2][:, :], cT[:, k, 0:NC], w[c % 3][:, k, :],
                                            start=k == 0, stop=k == KD - 1)
                last.then_inc(S.rows_ps, 1)
                if c:
                    spread_rows(c - 1)
            spread_rows(CHUNKS - 1)


def mixing(nc, ctx, x_prompt, x_sample, cache_pool, w_in, pool_w, pool_scale, gmlp_g, gmlp_ws, gmlp_bs,
           w_out, ident_in, bands_in, mod_rows, x1_rows, h2T_tiles, pool_prompt_out, pool_sample_out, v_sample_out):
    S = sems(nc, ctx, "mix", "passed consts x0 x1 ws_ps ws_sb wm mods sumsq mean rstd h hT_ps hT z_ps zp zu zv "
                             "vmean vrstd vn gmlp_ps diff diffT pool mixT mix h2T_ps h2T x1_out h2T_out "
                             "x1_ready outs zero dve")
    x_loaded = [S.x0, S.x1]
    with ExitStack() as mem:
        w_in_sb = sbuf(nc, mem, "w_in_sb", [P, KD, ZW])
        w_out_sb = sbuf(nc, mem, "w_out_sb", [P, KD, D])
        mods = sbuf(nc, mem, "mods", [P, 5, D])
        ident = sbuf(nc, mem, "ident_b", [P, P])
        bands = sbuf(nc, mem, "bands", [P, 5, GROUPS, P])
        BAND_FIRST, BAND_NEXT, BAND_SAMPLE, BAND_BEFORE, BAND_HIST = range(5)
        hist = sbuf(nc, mem, "hist", [STREAMS * HIST, HALF])
        pool_w_sb = sbuf(nc, mem, "pool_w_sb", [P, GROUPS, P])
        pool_scale_sb = sbuf(nc, mem, "pool_scale_sb", [P, GROUPS])
        gmlp_g_sb = sbuf(nc, mem, "gmlp_g_sb", [P, HALF])
        ws = sbuf(nc, mem, "ws", [P, 2, GROUPS, P])
        wmT = sbuf(nc, mem, "wmT", [P, 2, GROUPS, P])
        bs = sbuf(nc, mem, "bs", [P, 2, GROUPS, P])
        power = sbuf(nc, mem, "power", [P, GROUPS])
        x = [sbuf(nc, mem, f"x_in{s}", [P, D]) for s in range(2)]
        squares = sbuf(nc, mem, "squares", [P, D])
        sumsq = sbuf(nc, mem, "sumsq", [P, 1])
        mean = sbuf(nc, mem, "mean", [P, 1])
        rstd = sbuf(nc, mem, "rstd", [P, 1])
        h = sbuf(nc, mem, "h", [P, D])
        hT = sbuf(nc, mem, "hT", [P, KD, P])
        p = [sbuf(nc, mem, f"p{s}", [P, HALF]) for s in range(2)]
        u = sbuf(nc, mem, "u", [P, HALF])
        v = sbuf(nc, mem, "v", [P, GROUPS, P])
        vsq = sbuf(nc, mem, "vsq", [P, GROUPS, P])
        vsum = sbuf(nc, mem, "vsum", [P, GROUPS])
        vrstd = sbuf(nc, mem, "vrstd", [P, GROUPS])
        diffT = sbuf(nc, mem, "diffT", [P, GROUPS, P])
        mixT = sbuf(nc, mem, "mixT", [P, KD, P])
        x1 = sbuf(nc, mem, "x1", [P, D])
        t_ps = psum(nc, mem, "t_ps", [P, KD, P])
        z_ps = psum(nc, mem, "z_ps", [P, 3, HALF])
        mix_ps = psum(nc, mem, "mix_ps", [P, 2, HALF])
        uT_ps, sT_ps = t_ps[:, 0:4, :], t_ps[:, 4:8, :]
        diff_ps = mix_ps[:, 0, :].rearrange("p (g t) -> p g t", g=GROUPS)
        pool_ps = mix_ps[:, 1, :].rearrange("p (g t) -> p g t", g=GROUPS)
        CONSTS = 16 * 19
        block = mem.enter_context(nc.Block())

        def tiles(eng, tile):
            tile(0, 0, 0)
            tile(1, 0, 1)
            with eng.Fori(1, PROMPT_TILES // 2) as i:
                for s in range(2):
                    tile(i * 2 + s, i, s)
            tile(PROMPT_TILES, PROMPT_TILES // 2, 0, sample=True)

        @block.sync
        def _(sp):
            c = S.consts
            sp.dma_start(w_in_sb[:, :, :], w_in.rearrange("(k p) n -> p k n", p=P)).then_inc(c, 16)
            sp.dma_start(w_out_sb[:, :, :], w_out.rearrange("(k p) n -> p k n", p=P)).then_inc(c, 16)
            sp.dma_start(ident[:, :], ident_in).then_inc(c, 16)
            sp.dma_start(bands[:, :, :, :], bands_in).then_inc(c, 16)
            sp.dma_start(hist[:, :], cache_pool.rearrange("l b r c -> (l b r) c")).then_inc(c, 16)
            sp.dma_start(pool_w_sb[:, :, :], pool_w.rearrange("g c d -> c g d")).then_inc(c, 16)
            sp.dma_start(pool_scale_sb[:, :], pool_scale.rearrange("(g c) -> c g", g=GROUPS),
                         allow_slow_non_contiguous=True).then_inc(c, 16)
            sp.dma_start(gmlp_g_sb[:, :], gmlp_g.partition_broadcast(P)).then_inc(c, 16)
            sp.dma_start(ws[:, 0, :, :], gmlp_ws.rearrange("h i j -> i h j")).then_inc(c, 16)
            sp.wait_ge(S.zero, 1)
            for b in range(STREAMS):
                span = slice(b * STEP, (b + 1) * STEP)
                sp.dma_start(ws[span, 1, :, span], gmlp_ws[:, 0:STEP, 0:STEP].rearrange("h i j -> i h j"))\
                    .then_inc(c, 16)
            sp.dma_start(bs[:, 0, :, :].rearrange("p h i -> p (h i)"),
                         gmlp_bs.rearrange("h i -> (h i)").partition_broadcast(P)).then_inc(c, 16)
            sp.dma_start(mods[:, :, :], mod_rows[0, 0:5, :, :].rearrange("m p n -> p m n")).then_inc(c, 16)
            def tile(t, i, s, sample=False):
                if not sample:
                    src = x_prompt[0, bass.ds(t * P, P), :]
                else:
                    src = x_sample.rearrange("b t d -> (b t) d")
                if not (isinstance(t, int) and t < 2):
                    sp.wait_ge(S.x1_ready, t - 1)
                sp.dma_start(x[s][:, :], src).then_inc(x_loaded[s], 16)
            tiles(sp, tile)
            sp.wait_ge(S.h2T_ps, TILES - 1)
            sp.dma_start(mods[:, :, :], mod_rows[1, 0:5, :, :].rearrange("m p n -> p m n")).then_inc(S.mods, 16)

        @block.gpsimd
        def _(pool):
            pool.memset(ws[:, 1, :, :], 0.0).then_inc(S.zero, 1)
            pool.memset(power[:, :], -0.5).then_inc(S.zero, 1)
            pool.wait_ge(S.ws_sb, 2)
            pool.affine_select(out=wmT[:, :, :, :], in_=wmT[:, :, :, :], compare_op=ALU.is_ge, fill=0.0, base=0,
                               pattern=[[0, 2 * GROUPS], [1, P]], channel_multiplier=-1).then_inc(S.wm, 1)
            pool.wait_ge(S.zero, 2)

            def tile(t, i, s, sample=False):
                pool.wait_ge(S.mean, t * 2 + 1)
                pool.tensor_tensor(rstd[:, :], mean[:, :], power[:, 0:1], ALU.pow).then_inc(S.rstd, 1)
                pool.wait_ge(S.vmean, t + 1)
                pool.tensor_tensor(vrstd[:, :], vsum[:, :], power[:, :], ALU.pow).then_inc(S.vrstd, 1)
                pool.wait_ge(S.zp, t + 1)
                if sample:
                    for b in range(STREAMS):
                        pool.dma_start(pool_sample_out[0, b, :, :], p[0][b * STEP + 1:(b + 1) * STEP, :])\
                            .then_inc(S.outs, 16)
                    pool.wait_ge(S.vn, t + 1)
                    pool.dma_start(v_sample_out.rearrange("l b t c -> (l b t) c"),
                                   v[:, :, :].rearrange("p g c -> p (g c)")).then_inc(S.outs, 16)
                pool.wait_ge(S.mean, t * 2 + 2)
                pool.tensor_tensor(rstd[:, :], mean[:, :], power[:, 0:1], ALU.pow).then_inc(S.rstd, 1)
                pool.wait_ge(S.x1_ready, t + 1)
                pool.sem_inc(S.passed, 1)
                pool.dma_start(x1_rows[bass.ds(t, 1), :, :].rearrange("a p d -> p (a d)"), x1[:, :])\
                    .then_inc(S.x1_out, 16)
                pool.wait_ge(S.h2T, t * 2 + 2)
                pool.sem_inc(S.passed, 1)
                pool.dma_start(h2T_tiles[bass.ds(t, 1), :, :].rearrange("a p d -> p (a d)"),
                               hT[:, :, :].rearrange("p k t -> p (k t)")).then_inc(S.h2T_out, 16)
            tiles(pool, tile)
            pool.wait_ge(S.x1_out, 16 * TILES)
            pool.wait_ge(S.h2T_out, 16 * TILES)
            pool.dma_start(pool_prompt_out[0, 0, :, :], p[1][P - HIST:P, :]).then_inc(S.outs, 16)
            pool.wait_ge(S.outs, 16 * (STREAMS + 2))

        @block.scalar
        def _(act):
            def tile(t, i, s, sample=False):
                act.wait_ge(x_loaded[s], (i + 1) * 16)
                wait(act, S.mean, t * 2)
                nc.scalar.activation(squares[:, :], x[s][:, :], ACT.Square, accum_out=sumsq[:, :]).then_inc(S.sumsq, 1)
                act.wait_ge(S.hT_ps, t + 1)
                wait(act, S.h2T_out, t * 16)
                for half in (slice(0, 4), slice(4, 8)):
                    nc.scalar.activation(hT[:, half, :], t_ps[:, half, :], ACT.Copy).then_inc(S.hT, 1)
                act.wait_ge(S.z_ps, t * 3 + 1)
                nc.scalar.activation(p[s][:, :], z_ps[:, 0, :], ACT.Copy).then_inc(S.zp, 1)
                act.wait_ge(S.z_ps, t * 3 + 2)
                nc.scalar.activation(u[:, :], z_ps[:, 1, :], ACT.Gelu).then_inc(S.zu, 1)
                act.wait_ge(S.z_ps, t * 3 + 3)
                nc.scalar.activation(v[:, :, :].rearrange("p g c -> p (g c)"), z_ps[:, 2, :], ACT.Gelu)\
                    .then_inc(S.zv, 1)
                act.wait_ge(S.diff, t + 1)
                nc.scalar.activation(diffT[:, :, :], diff_ps, ACT.Copy).then_inc(S.diffT, 1)
                act.wait_ge(S.x1_ready, t + 1)
                nc.scalar.activation(squares[:, :], x1[:, :], ACT.Square, accum_out=sumsq[:, :]).then_inc(S.sumsq, 1)
                act.wait_ge(S.h2T_ps, t + 1)
                for half in (slice(0, 4), slice(4, 8)):
                    nc.scalar.activation(hT[:, half, :], t_ps[:, half, :], ACT.Copy).then_inc(S.h2T, 1)
            tiles(act, tile)

        @block.vector
        def _(dve):
            own = Order(dve, S.dve)
            FIRST, PER_TILE = 2, 7
            dve.wait_ge(S.consts, CONSTS)
            dve.wait_ge(S.ws_ps, 1)
            nc.vector.tensor_copy(wmT[:, 0, :, :], t_ps[:, 0:4, :]).then_inc(S.ws_sb, 1)
            nc.vector.tensor_copy(wmT[:, 1, :, :], t_ps[:, 4:8, :]).then_inc(S.ws_sb, 1)
            own.mark(nc.vector.tensor_copy(
                bs[:, 1, :, :].rearrange("p h (b i) -> p h b i", b=STREAMS),
                bs[:, 0, :, 0:STEP].rearrange("p h (b i) -> p h b i", b=1)
                .to_broadcast([P, GROUPS, STREAMS, STEP])))
            own.then(nc.vector.memset(vsq[:, :, :], 0.0))

            def tile(t, i, s, sample=False):
                kind = int(sample)
                own.loop(FIRST + t * PER_TILE)

                def normed(src, shift, scale, n):
                    dve.wait_ge(S.sumsq, t * 2 + n)
                    nc.vector.tensor_scalar(mean[:, :], sumsq[:, :], 1.0 / D, EPS, ALU.mult, ALU.add)\
                        .then_inc(S.mean, 1)
                    dve.wait_ge(S.rstd, t * 2 + n)
                    own.then(nc.vector.scalar_tensor_tensor(out=h[:, :], in0=src, scalar=rstd[:, :],
                                                            in1=mods[:, scale, :], op0=ALU.mult, op1=ALU.mult))
                    nc.vector.tensor_tensor(h[:, :], h[:, :], mods[:, shift, :], ALU.add).then_inc(S.h, 1)

                if sample:
                    dve.wait_ge(S.mods, 16)
                wait(dve, S.h2T_ps, t)
                normed(x[s][:, :], SHIFT1, SCALE1, 1)
                dve.wait_ge(S.zv, t + 1)
                own.then(nc.vector.tensor_tensor(vsq[:, :, :], v[:, :, :], v[:, :, :], ALU.mult))
                own.then(nc.vector.tensor_reduce(vsum[:, :], vsq[:, :, :], AX.X, ALU.add))
                nc.vector.tensor_scalar(vsum[:, :], vsum[:, :], 1.0 / P, EPS, ALU.mult, ALU.add)\
                    .then_inc(S.vmean, 1)
                dve.wait_ge(S.vrstd, t + 1)
                own.then(nc.vector.tensor_tensor(v[:, :, :], v[:, :, :],
                                                 vrstd[:, :].rearrange("p (g c) -> p g c", c=1)
                                                 .to_broadcast([P, GROUPS, P]), ALU.mult))
                nc.vector.tensor_tensor(v[:, :, :], v[:, :, :],
                                        gmlp_g_sb[:, :].rearrange("p (g c) -> p g c", g=GROUPS), ALU.mult)\
                    .then_inc(S.vn, 1)
                dve.wait_ge(S.gmlp_ps, t + 1)
                own.then(nc.vector.tensor_tensor(vsq[:, :, :], sT_ps, bs[:, kind, :, :], ALU.add))
                nc.vector.tensor_tensor(mixT[:, 4:8, :], uT_ps, vsq[:, :, :], ALU.mult).then_inc(S.mixT, 1)
                dve.wait_ge(S.pool, t + 1)
                nc.vector.tensor_tensor(mixT[:, 0:4, :], pool_ps,
                                        pool_scale_sb[:, :].rearrange("p (g c) -> p g c", c=1)
                                        .to_broadcast([P, GROUPS, P]), ALU.mult).then_inc(S.mixT, 1)
                dve.wait_ge(S.mix, t + 1)
                wait(dve, S.x1_out, t * 16)
                own.then(nc.vector.tensor_tensor(x1[:, :], mix_ps[:, :, :].rearrange("p a n -> p (a n)"),
                                                 mods[:, GATE1, :], ALU.mult))
                nc.vector.tensor_tensor(x1[:, :], x1[:, :], x[s][:, :], ALU.add).then_inc(S.x1_ready, 1)
                dve.wait_ge(S.x1_ready, t + 1)
                normed(x1[:, :], SHIFT2, SCALE2, 2)
                assert own.n == PER_TILE, own.n
            tiles(dve, tile)

        @block.tensor
        def _(pe):
            pe.wait_ge(S.consts, CONSTS)
            for kind in range(2):
                for g in range(GROUPS):
                    last = nc.tensor.transpose(t_ps[:, kind * 4 + g, :], ws[:, kind, g, :], ident[:, :])
            last.then_inc(S.ws_ps, 1)
            pe.wait_ge(S.wm, 1)

            def tile(t, i, s, sample=False):
                pe.wait_ge(S.h, t * 2 + 1)
                wait(pe, S.h2T, t * 2)
                for k in range(KD):
                    last = nc.tensor.transpose(t_ps[:, k, :], h[:, k * P:(k + 1) * P], ident[:, :])
                last.then_inc(S.hT_ps, 1)
                pe.wait_ge(S.hT, t * 2 + 2)
                for b in range(3):
                    for k in range(KD):
                        last = nc.tensor.matmul(z_ps[:, b, :], hT[:, k, :], w_in_sb[:, k, b * HALF:(b + 1) * HALF],
                                                start=k == 0, stop=k == KD - 1)
                    last.then_inc(S.z_ps, 1)
                pe.wait_ge(S.zp, t + 1)
                now = BAND_SAMPLE if sample else BAND_NEXT
                before = bands[:, BAND_BEFORE]
                rows = p[1 - s]
                if sample:
                    before, rows = bands[0:STREAMS * HIST, BAND_HIST], hist
                first = isinstance(t, int) and t == 0
                if first:
                    now = BAND_FIRST
                for g in range(GROUPS):
                    chan = slice(g * P, (g + 1) * P)
                    last = nc.tensor.matmul(diff_ps[:, g, :], p[s][:, chan], bands[:, now, g, :],
                                            start=True, stop=first)
                    if not first:
                        last = nc.tensor.matmul(diff_ps[:, g, :], rows[:, chan], before[:, g, :],
                                                start=False, stop=True)
                last.then_inc(S.diff, 1)
                pe.wait_ge(S.zu, t + 1)
                for g in range(GROUPS):
                    nc.tensor.transpose(uT_ps[:, g, :], u[:, g * P:(g + 1) * P], ident[:, :])
                pe.wait_ge(S.diffT, t + 1)
                for g in range(GROUPS):
                    last = nc.tensor.matmul(pool_ps[:, g, :], pool_w_sb[:, g, :], diffT[:, g, :],
                                            start=True, stop=True)
                last.then_inc(S.pool, 1)
                pe.wait_ge(S.vn, t + 1)
                for g in range(GROUPS):
                    last = nc.tensor.matmul(sT_ps[:, g, :], v[:, g, :], wmT[:, int(sample), g, :],
                                            start=True, stop=True)
                last.then_inc(S.gmlp_ps, 1)
                pe.wait_ge(S.mixT, t * 2 + 2)
                for b in range(2):
                    for k in range(KD):
                        last = nc.tensor.matmul(mix_ps[:, b, :], mixT[:, k, :], w_out_sb[:, k, b * HALF:(b + 1) * HALF],
                                                start=k == 0, stop=k == KD - 1)
                last.then_inc(S.mix, 1)
                pe.wait_ge(S.h, t * 2 + 2)
                for k in range(KD):
                    last = nc.tensor.transpose(t_ps[:, k, :], h[:, k * P:(k + 1) * P], ident[:, :])
                last.then_inc(S.h2T_ps, 1)
            tiles(pe, tile)


def routing(nc, ctx, wq, keys, ident_in, h2T_tiles, gate_blocks):
    S = sems(nc, ctx, "route", "passed consts iota h2 keys_ps keysT q_ps q qT_ps qT scores scores_used shifted exp "
                               "slots slotsT_ps slotsT left right_hot gated_vector gated_pool place_ps placed out0 out1 dve")
    HP = HEADS * 2
    with ExitStack() as mem:
        wq_sb = sbuf(nc, mem, "wq_sb", [P, KD, HP * P])
        keysT = sbuf(nc, mem, "keysT", [P, HP, NKEYS])
        ident = sbuf(nc, mem, "ident_c", [P, P])
        h2T = sbuf(nc, mem, "h2T", [P, KD, P])
        q = sbuf(nc, mem, "q", [P, 4, P])
        qT = sbuf(nc, mem, "qT", [P, HP, P])
        work = sbuf(nc, mem, "work", [P, HP * NKEYS])
        best = sbuf(nc, mem, "best", [P, HP, TOPK])
        best_at = sbuf(nc, mem, "best_at", [P, HP, TOPK], U32)
        best_key = sbuf(nc, mem, "best_key", [P, HP, TOPK], BF16)
        pair = sbuf(nc, mem, "pair", [P, HEADS, TOPK])
        pair_at = sbuf(nc, mem, "pair_at", [P, HEADS, TOPK], U32)
        rank_int = sbuf(nc, mem, "rank_int", [P, 2, HEADS, TOPK], U32)
        rank = sbuf(nc, mem, "rank", [P, 2, HEADS, TOPK], BF16)
        hit = sbuf(nc, mem, "hit", [P, HEADS, TOPK, TOPK], BF16)
        total = sbuf(nc, mem, "total", [P, HEADS])
        slots = sbuf(nc, mem, "slots", [P, 3, HEADS, TOPK])
        keyT = sbuf(nc, mem, "keyT", [P, 2, P], BF16)
        gateT = sbuf(nc, mem, "gateT", [P, P])
        left = [sbuf(nc, mem, f"left{s}", [P, BATCH, NKEYS]) for s in range(2)]
        right_hot = [sbuf(nc, mem, f"right_hot{s}", [P, NKEYS, BATCH], BF16) for s in range(2)]
        right = [sbuf(nc, mem, f"right{s}", [P, BATCH, NKEYS]) for s in range(2)]
        dense = [sbuf(nc, mem, f"dense{s}", [P, NKEYS, BLOCK]) for s in range(2)]
        iota_rank = sbuf(nc, mem, "iota_rank", [P, TOPK, TOPK], BF16)
        iota_key = sbuf(nc, mem, "iota_key", [P, NKEYS], BF16)
        iota_keys = sbuf(nc, mem, "iota_keys", [P, NKEYS, BATCH], BF16)
        s_ps = psum(nc, mem, "s_ps", [P, HP, NKEYS])
        q_ps = psum(nc, mem, "q_ps", [P, HALF])
        x_ps = psum(nc, mem, "x_ps", [P, 4, P])
        place_ps = psum(nc, mem, "place_ps", [P, 2, 4, NKEYS])
        stored = [S.out0, S.out1]
        BATCHES = P // BATCH
        block = mem.enter_context(nc.Block())

        def on_vector(b):
            return b % 4 == 3
        ON_POOL = sum(not on_vector(b) for b in range(BATCHES))

        def gated(eng, b):
            return eng.tensor_tensor(
                right[b % 2][:, :, :], right_hot[b % 2][:, :, :].rearrange("p i t -> p t i"),
                gateT[:, b * BATCH:(b + 1) * BATCH].rearrange("p (t o) -> p t o", o=1)
                .to_broadcast([P, BATCH, NKEYS]), ALU.mult)

        def wait_for_gated(eng, t, b):
            if on_vector(b):
                eng.wait_ge(S.gated_vector, t * (BATCHES - ON_POOL) + sum(on_vector(n) for n in range(b + 1)))
            else:
                eng.wait_ge(S.gated_pool, t * ON_POOL + sum(not on_vector(n) for n in range(b + 1)))

        def wait_for_room(eng, sem, t, b, per):
            wait(eng, sem, t * (BATCHES * per) + max(b - 1, 0) * per)

        def tiles(eng, tile):
            tile(0, True)
            with eng.Fori(1, TILES - 1) as t:
                tile(t, True)
            tile(TILES - 1, False)

        @block.sync
        def _(sp):
            sp.dma_start(work[:, :].rearrange("k (n c) -> k n c", n=HP), keys.rearrange("h s k c -> k (h s) c"))\
                .then_inc(S.consts, 16)
            sp.dma_start(ident[:, :], ident_in).then_inc(S.consts, 16)
            sp.dma_start(h2T[:, :, :].rearrange("p k t -> p (k t)"), h2T_tiles[0, :, :]).then_inc(S.h2, 16)
            sp.dma_start(wq_sb[:, :, :], wq.rearrange("(k p) n -> p k n", p=P)).then_inc(S.consts, 16)

            def load_h2(t):
                sp.wait_ge(S.q_ps, t * 4)
                sp.dma_start(h2T[:, :, :].rearrange("p k t -> p (k t)"),
                             h2T_tiles[bass.ds(t, 1), :, :].rearrange("a p d -> p (a d)")).then_inc(S.h2, 16)

            def tile(t, ahead):
                if ahead:
                    load_h2(t + 2)
                for half in range(2):
                    sp.wait_ge(S.placed, t * 32 + 2 + 16 * (half + 1))
                    sp.dma_start(gate_blocks[bass.ds(t * 2 + half, 1), :, :, :].rearrange("a p i j -> p (a i j)"),
                                 dense[half][:, :, :].rearrange("p i j -> p (i j)")).then_inc(stored[half], 16)
            load_h2(1)
            with sp.Fori(0, TILES - 2) as t:
                tile(t, True)
            tile(TILES - 2, False)
            tile(TILES - 1, False)
            for half in range(2):
                sp.wait_ge(stored[half], TILES * 16)

        @block.gpsimd
        def _(pool):
            pool.iota(iota_rank[:, :, :], pattern=[[1, TOPK], [0, TOPK]], base=0, channel_multiplier=0,
                      allow_small_or_imprecise_dtypes=True).then_inc(S.iota, 1)
            pool.iota(iota_key[:, :], pattern=[[1, NKEYS]], base=0, channel_multiplier=0,
                      allow_small_or_imprecise_dtypes=True).then_inc(S.iota, 1)
            pool.iota(iota_keys[:, :, :], pattern=[[1, NKEYS], [0, BATCH]], base=0, channel_multiplier=0,
                      allow_small_or_imprecise_dtypes=True).then_inc(S.iota, 1)

            def tile(t, ahead):
                pool.wait_ge(S.slotsT, t * 2 + 2)
                for b in range(BATCHES):
                    if not on_vector(b):
                        wait_for_room(pool, S.place_ps, t, b, 2)
                        pool.wait_ge(S.right_hot, t * BATCHES + b + 1)
                        gated(nc.gpsimd, b).then_inc(S.gated_pool, 1)
            tiles(pool, tile)

        @block.scalar
        def _(act):
            act.sem_inc(S.placed, 2)
            act.wait_ge(S.keys_ps, 1)
            nc.scalar.activation(keysT[:, :, :], s_ps[:, :, :], ACT.Copy).then_inc(S.keysT, 1)

            def queries(t):
                for b in range(4):
                    n = t * 4 + b
                    act.wait_ge(S.q_ps, n + 1)
                    wait(act, S.qT_ps, n)
                    nc.scalar.activation(q[:, :, :].rearrange("p a c -> p (a c)"), q_ps[:, :], ACT.Copy)\
                        .then_inc(S.q, 1)
                    act.wait_ge(S.qT_ps, n + 1)
                    wait(act, S.scores, t * 4)
                    nc.scalar.activation(qT[:, b * 4:b * 4 + 4, :], x_ps[:, :, :], ACT.Copy).then_inc(S.qT, 1)

            def tile(t, ahead):
                if ahead:
                    queries(t + 1)
                act.wait_ge(S.shifted, t + 1)
                nc.scalar.activation(slots[:, 2, :, :], slots[:, 2, :, :], ACT.Exp).then_inc(S.exp, 1)
                for half in range(2):
                    wait(act, stored[half], t * 16)
                    for g in range(16):
                        act.wait_ge(S.place_ps, t * 32 + half * 16 + g + 1)
                        nc.scalar.activation(dense[half][:, :, g * 4:g * 4 + 4].rearrange("p i t -> p t i"),
                                             place_ps[:, g % 2, :, :], ACT.Copy).then_inc(S.placed, 1)
            queries(0)
            tiles(act, tile)

        @block.vector
        def _(dve):
            own = Order(dve, S.dve)
            PER_TILE = 138
            dve.wait_ge(S.iota, 3)
            dve.wait_ge(S.keysT, 1)
            best4 = best[:, :, :].rearrange("p (h s) k -> p h s k", s=2)
            key4 = best_key[:, :, :].rearrange("p (h s) k -> p h s k", s=2)
            sums = work[:, :].rearrange("p (h a b) -> p h a b", h=HEADS, a=TOPK)
            work3 = work[:, :].rearrange("p (n k) -> p n k", n=HP)
            low, high = slice(0, 8), slice(8, 16)

            def two_lists(t):
                for n in range(HP):
                    if n % 4 == 0:
                        dve.wait_ge(S.scores, t * 4 + n // 4 + 1)
                        dve.sem_inc(S.passed, 1)
                    own.mark(nc.vector.max(best[:, n, low], s_ps[:, n, :]))
                own.settle()
                dve.sem_inc(S.passed, 1)
                for n in range(HP):
                    own.mark(nc.vector.max_index(best_at[:, n, low], best[:, n, low], s_ps[:, n, :]))
                    own.mark(nc.vector.match_replace(work3[:, n, :], best[:, n, low], s_ps[:, n, :], NEG))
                own.settle()
                nc.vector.memset(total[:, :], 0.0).then_inc(S.scores_used, 1)
                for n in range(HP):
                    own.mark(nc.vector.max(best[:, n, high], work3[:, n, :]))
                own.settle()
                dve.sem_inc(S.passed, 1)
                for n in range(HP):
                    own.mark(nc.vector.max_index(best_at[:, n, high], best[:, n, high], work3[:, n, :]))
                own.settle()
                dve.sem_inc(S.passed, 1)
                own.then(nc.vector.tensor_copy(best_key[:, :, :], best_at[:, :, :]))

            def best_pairs(t):
                own.then(nc.vector.tensor_tensor(
                    sums, best4[:, :, 0, :].rearrange("p h (a o) -> p h a o", o=1)
                    .to_broadcast([P, HEADS, TOPK, TOPK]),
                    best4[:, :, 1, :].rearrange("p h (o b) -> p h o b", o=1)
                    .to_broadcast([P, HEADS, TOPK, TOPK]), ALU.add))
                dve.sem_inc(S.passed, 1)
                for part in (low, high):
                    for h in range(HEADS):
                        own.mark(nc.vector.max(pair[:, h, part], sums[:, h].rearrange("p a b -> p (a b)")))
                    own.settle()
                    dve.sem_inc(S.passed, 1)
                    for h in range(HEADS):
                        own.mark(nc.vector.max_index(pair_at[:, h, part], pair[:, h, part],
                                                     sums[:, h].rearrange("p a b -> p (a b)")))
                    own.settle()
                    dve.sem_inc(S.passed, 1)
                    if part is low:
                        for h in range(HEADS):
                            flat = sums[:, h].rearrange("p a b -> p (a b)")
                            own.mark(nc.vector.match_replace(flat, pair[:, h, low], flat, NEG))
                        own.settle()
                        dve.sem_inc(S.passed, 1)

            def gates(t):
                wait(dve, S.slotsT_ps, t)
                nc.vector.tensor_tensor(slots[:, 2, :, :], pair[:, :, :],
                                        pair[:, :, 0:1].to_broadcast([P, HEADS, TOPK]), ALU.subtract)\
                    .then_inc(S.shifted, 1)
                own.mark(nc.vector.tensor_scalar(rank_int[:, 0, :, :], pair_at[:, :, :], 4, None,
                                                 ALU.logical_shift_right))
                own.then(nc.vector.tensor_scalar(rank_int[:, 1, :, :], pair_at[:, :, :], TOPK - 1, None,
                                                 ALU.bitwise_and))
                own.then(nc.vector.tensor_copy(rank[:, :, :, :], rank_int[:, :, :, :]))
                dve.wait_ge(S.exp, t + 1)
                own.then(nc.vector.tensor_reduce(total[:, :], slots[:, 2, :, :], AX.X, ALU.add))
                own.then(nc.vector.reciprocal(total[:, :], total[:, :]))
                own.then(nc.vector.tensor_tensor(slots[:, 2, :, :], slots[:, 2, :, :],
                                                 total[:, :].rearrange("p (h o) -> p h o", o=1)
                                                 .to_broadcast([P, HEADS, TOPK]), ALU.mult))

            def chosen_keys(t):
                for s in range(2):
                    own.then(nc.vector.tensor_tensor(
                        hit[:, :, :, :], rank[:, s].rearrange("p h (o k) -> p h o k", o=1)
                        .to_broadcast([P, HEADS, TOPK, TOPK]),
                        iota_rank[:, :, :].rearrange("p (o a) k -> p o a k", o=1)
                        .to_broadcast([P, HEADS, TOPK, TOPK]), ALU.is_equal))
                    own.then(nc.vector.tensor_tensor(
                        hit[:, :, :, :], hit[:, :, :, :], key4[:, :, s, :].rearrange("p h (a o) -> p h a o", o=1)
                        .to_broadcast([P, HEADS, TOPK, TOPK]), ALU.mult))
                    for n in (8, 4, 2):
                        own.then(nc.vector.tensor_tensor(hit[:, :, 0:n, :], hit[:, :, 0:n, :], hit[:, :, n:2 * n, :],
                                                         ALU.add))
                    nc.vector.tensor_tensor(slots[:, s, :, :], hit[:, :, 0, :], hit[:, :, 1, :], ALU.add)\
                        .then_inc(S.slots, 1)
                    dve.wait_ge(S.slots, t * 2 + s + 1)

            def one_hots(t):
                dve.wait_ge(S.slotsT_ps, t + 1)
                nc.vector.tensor_copy(keyT[:, :, :], x_ps[:, 0:2, :]).then_inc(S.slotsT, 1)
                nc.vector.tensor_copy(gateT[:, :], x_ps[:, 2, :]).then_inc(S.slotsT, 1)
                dve.wait_ge(S.slotsT, t * 2 + 2)

                def right_rows(b):
                    if b >= 2:
                        wait_for_gated(dve, t, b - 2)
                    nc.vector.tensor_tensor(
                        right_hot[b % 2][:, :, :], keyT[:, 1, b * BATCH:(b + 1) * BATCH]
                        .rearrange("p (o t) -> p o t", o=1).to_broadcast([P, NKEYS, BATCH]),
                        iota_keys[:, :, :], ALU.is_equal).then_inc(S.right_hot, 1)

                right_rows(0)
                for b in range(BATCHES):
                    if b + 1 < BATCHES:
                        right_rows(b + 1)
                    wait_for_room(dve, S.place_ps, t, b, 2)
                    nc.vector.tensor_tensor(
                        left[b % 2][:, :, :], keyT[:, 0, b * BATCH:(b + 1) * BATCH]
                        .rearrange("p (t o) -> p t o", o=1).to_broadcast([P, BATCH, NKEYS]),
                        iota_key[:, :].rearrange("p (o i) -> p o i", o=1).to_broadcast([P, BATCH, NKEYS]),
                        ALU.is_equal).then_inc(S.left, 1)
                    if on_vector(b):
                        dve.wait_ge(S.right_hot, t * BATCHES + b + 1)
                        gated(nc.vector, b).then_inc(S.gated_vector, 1)

            def tile(t, ahead):
                own.loop(t * PER_TILE)
                two_lists(t)
                best_pairs(t)
                gates(t)
                chosen_keys(t)
                one_hots(t)
                assert own.n == PER_TILE, own.n
            tiles(dve, tile)

        @block.tensor
        def _(pe):
            pe.wait_ge(S.consts, 48)
            for n in range(HP):
                last = nc.tensor.transpose(s_ps[:, n, :], work[:, n * P:(n + 1) * P], ident[:, :])
            last.then_inc(S.keys_ps, 1)

            def queries(t):
                pe.wait_ge(S.h2, t * 16 + 16)
                def product(b):
                    wait(pe, S.q, t * 4 + b)
                    for k in range(KD):
                        last = nc.tensor.matmul(q_ps[:, :], h2T[:, k, :], wq_sb[:, k, b * HALF:(b + 1) * HALF],
                                                start=k == 0, stop=k == KD - 1)
                    last.then_inc(S.q_ps, 1)
                for b in range(4):
                    product(b)
                    pe.wait_ge(S.q, t * 4 + b + 1)
                    wait(pe, S.qT, t * 4 + b)
                    for n in range(4):
                        last = nc.tensor.transpose(x_ps[:, n, :], q[:, n, :], ident[:, :])
                    last.then_inc(S.qT_ps, 1)

            def scores(t):
                pe.wait_ge(S.qT, t * 4 + 4)
                wait(pe, S.scores_used, t)
                for n in range(HP):
                    last = nc.tensor.matmul(s_ps[:, n, :], qT[:, n, :], keysT[:, n, :], start=True, stop=True)
                    if n % 4 == 3:
                        last.then_inc(S.scores, 1)

            def tile(t, ahead):
                if ahead:
                    queries(t + 1)
                    scores(t + 1)
                pe.wait_ge(S.slots, t * 2 + 2)
                wait(pe, S.slotsT, t * 2)
                for n in range(3):
                    last = nc.tensor.transpose(x_ps[:, n, :], slots[:, n, :, :].rearrange("p h k -> p (h k)"),
                                               ident[:, :])
                last.then_inc(S.slotsT_ps, 1)
                for b in range(BATCHES):
                    n = t * BATCHES + b
                    pe.wait_ge(S.left, n + 1)
                    wait_for_gated(pe, t, b)
                    for g in range(2):
                        pe.wait_ge(S.placed, n * 2 + g + 1)
                        for j in range(4):
                            last = nc.tensor.matmul(place_ps[:, g, j, :], right[b % 2][:, g * 4 + j, :],
                                                    left[b % 2][:, g * 4 + j, :], start=True, stop=True)
                        last.then_inc(S.place_ps, 1)
            pe.wait_ge(S.keysT, 1)
            queries(0)
            scores(0)
            tiles(pe, tile)


def experts(nc, ctx, u_table, v_table, ident_in, h2T_tiles, gate_blocks, ff):
    S = sems(nc, ctx, "exp", "passed consts zero h0 h1 h_split h_used u0 u1 gates vld uT_ps uT_hi uT_lo act_ps gelu "
                             "m m_hi m_lo v_hi v_lo y_ps y_free")
    EXPERTS = NKEYS * NKEYS
    EB = EXPERTS // P
    PAIRS = EB // 2
    TOKENS = TILES * P
    GROUP = TOKENS // 3
    OUTPUTS = 2 * TILES
    with ExitStack() as mem:
        ident = sbuf(nc, mem, "ident_d", [P, P])
        h_hi = sbuf(nc, mem, "h_hi", [P, KD, TOKENS], F32R)
        h_lo = sbuf(nc, mem, "h_lo", [P, KD, TOKENS], F32R)
        u = [sbuf(nc, mem, f"u_raw{s}", [P, D]) for s in range(2)]
        v = sbuf(nc, mem, "v_raw", [P, D])
        uT_hi = [sbuf(nc, mem, f"uT_hi{s}", [P, KD, P], F32R) for s in range(2)]
        uT_lo = [sbuf(nc, mem, f"uT_lo{s}", [P, KD, P], F32R) for s in range(2)]
        gates = sbuf(nc, mem, "gates", [P, BLOCKS, 2, BLOCK])
        g = sbuf(nc, mem, "g", [P, TOKENS])
        m_hi = [sbuf(nc, mem, f"m_hi{s}", [P, TOKENS], F32R) for s in range(3)]
        m_lo = [sbuf(nc, mem, f"m_lo{s}", [P, TOKENS], F32R) for s in range(3)]
        v_hi = [sbuf(nc, mem, f"v_hi{s}", [P, D], F32R) for s in range(3)]
        v_lo = [sbuf(nc, mem, f"v_lo{s}", [P, D], F32R) for s in range(3)]
        uT_ps = psum(nc, mem, "uT_ps", [P, KD, P])
        a_ps = [psum(nc, mem, f"a_ps{n}", [P, HALF]) for n in range(3)]
        y_ps = [psum(nc, mem, f"y_ps{n}", [P, HALF]) for n in range(3)]
        block = mem.enter_context(nc.Block())

        def buffer(j, parity):
            return 2 if j else parity

        def pairs(eng, first, pair, last):
            first()
            with eng.Fori(0, PAIRS // 2 - 1) as i:
                pair(i * 2 + 1, 1)
                pair(i * 2 + 2, 0)
            last()

        @block.sync
        def _(sp):
            sp.dma_start(ident[:, :], ident_in).then_inc(S.consts, 16)
            h_loaded = [S.h0, S.h1]

            def load_h(t, s):
                sp.wait_ge(S.h_used, t * 2 + 2)
                sp.dma_start(u[s][:, :], h2T_tiles[bass.ds(t, 1), :, :].rearrange("a p d -> p (a d)"))\
                    .then_inc(h_loaded[s], 16)
            with sp.Fori(0, TILES // 2) as i:
                load_h(i * 2, 0)
                load_h(i * 2 + 1, 1)
            load_h(TILES - 1, 0)
            sp.wait_ge(S.h_used, 2 + 2 * TILES)
            u_loaded = [S.u0, S.u1]

            def load_u(e, s):
                wait(sp, S.uT_ps, e)
                sp.dma_start(u[s][:, :], u_table[bass.ds(e * P, P), :]).then_inc(u_loaded[s], 16)

            def load_v(e):
                wait(sp, S.v_lo, e)
                sp.dma_start(v[:, :], v_table[bass.ds(e * P, P), :]).then_inc(S.vld, 16)

            def load(c, more=True):
                load_u(c * 2 + 1, 1)
                load_v(c * 2)
                if more:
                    load_u(c * 2 + 2, 0)
                load_v(c * 2 + 1)
            load_u(0, 0)
            load(0)
            with sp.Fori(1, PAIRS - 1) as c:
                load(c)
            load(PAIRS - 1, more=False)

        @block.gpsimd
        def _(pool):
            pool.sem_inc(S.h_used, 2)
            pool.memset(ff[:, :, :], 0.0).then_inc(S.zero, 1)

            def split_v(c, parity, j):
                e = c * 2 + j
                pool.wait_ge(S.v_hi, e + 1)
                nc.gpsimd.tensor_tensor(v_lo[buffer(j, parity)][:, :], v[:, :],
                                        v_hi[buffer(j, parity)][:, :].bitcast(F32), ALU.subtract)\
                    .then_inc(S.v_lo, 1)

            def load_gates(c):
                pool.sem_inc(S.passed, 1)
                pool.dma_start(gates[:, :, :, :],
                               gate_blocks[:, :, bass.ds(c * 2, 2), :].rearrange("n p i j -> p n (i j)"))\
                    .then_inc(S.gates, 16)

            def pair(c, parity, more=True):
                split_v(c, parity, 0)
                split_v(c, parity, 1)
                if more:
                    pool.wait_ge(S.m, c * 6 + 6)
                    load_gates(c + 1)
            load_gates(0)
            pairs(pool, lambda: pair(0, 0), pair, lambda: pair(PAIRS - 1, 1, more=False))

        @block.scalar
        def _(act):
            h_loaded = [S.h0, S.h1]

            def split_h(t, i, s):
                act.wait_ge(h_loaded[s], i * 16 + 16)
                nc.scalar.activation(h_hi[:, :, bass.ds(t * P, P)], u[s][:, :].rearrange("p (k t) -> p k t", k=KD),
                                     ACT.Copy).then_inc(S.h_split, 1)
            with act.Fori(0, TILES // 2) as i:
                split_h(i * 2, i, 0)
                split_h(i * 2 + 1, i, 1)
            split_h(TILES - 1, TILES // 2, 0)

            def uT(e, s):
                act.wait_ge(S.uT_ps, e + 2)
                wait(act, S.act_ps, e * 3 - 3)
                for n in range(2):
                    nc.scalar.activation(uT_hi[s][:, n * 4:n * 4 + 4, :], uT_ps[:, n * 4:n * 4 + 4, :], ACT.Copy)\
                        .then_inc(S.uT_hi, 1)

            def split_v(c, parity, j):
                e = c * 2 + j
                act.wait_ge(S.vld, e * 16 + 16)
                if j:
                    wait(act, S.y_ps, c * OUTPUTS)
                nc.scalar.activation(v_hi[buffer(j, parity)][:, :], v[:, :], ACT.Copy).then_inc(S.v_hi, 1)

            def weigh(c, parity, j):
                e = c * 2 + j
                wait(act, S.m_lo, e * 3)
                for n in range(3):
                    act.wait_ge(S.act_ps, e * 3 + n + 1)
                    nc.scalar.activation(g[:, n * GROUP:(n + 1) * GROUP], a_ps[n][:, 0:GROUP], ACT.Gelu)\
                        .then_inc(S.gelu, 1)
                act.wait_ge(S.m, e * 3 + 3)
                nc.scalar.activation(m_hi[buffer(j, parity)][:, :], g[:, :], ACT.Copy).then_inc(S.m_hi, 1)

            def pair(c, parity, more=True):
                uT(c * 2 + 1, 1)
                split_v(c, parity, 0)
                weigh(c, parity, 0)
                if more:
                    uT(c * 2 + 2, 0)
                split_v(c, parity, 1)
                weigh(c, parity, 1)
            act.wait_ge(S.uT_ps, 2)
            for n in range(2):
                nc.scalar.activation(uT_hi[0][:, n * 4:n * 4 + 4, :], uT_ps[:, n * 4:n * 4 + 4, :], ACT.Copy)\
                    .then_inc(S.uT_hi, 1)
            pairs(act, lambda: pair(0, 0), pair, lambda: pair(PAIRS - 1, 1, more=False))

        @block.vector
        def _(dve):
            dve.sem_inc(S.y_free, 3)

            def split_h(t, s):
                dve.wait_ge(S.h_split, t + 1)
                tok = bass.ds(t * P, P)
                nc.vector.tensor_tensor(h_lo[:, :, tok], u[s][:, :].rearrange("p (k t) -> p k t", k=KD),
                                        h_hi[:, :, tok].bitcast(F32), ALU.subtract).then_inc(S.h_used, 2)
            with dve.Fori(0, TILES // 2) as i:
                split_h(i * 2, 0)
                split_h(i * 2 + 1, 1)
            split_h(TILES - 1, 0)
            dve.wait_ge(S.zero, 1)

            def uT(e, s):
                for n in range(2):
                    dve.wait_ge(S.uT_hi, e * 2 + n + 1)
                    part = slice(n * 4, n * 4 + 4)
                    nc.vector.tensor_tensor(uT_lo[s][:, part, :], uT_ps[:, part, :], uT_hi[s][:, part, :].bitcast(F32),
                                            ALU.subtract).then_inc(S.uT_lo, 1)

            def weigh(c, j, n):
                dve.wait_ge(S.gelu, (c * 2 + j) * 3 + n + 1)
                dve.wait_ge(S.gates, c * 16 + 16)
                part = g[:, n * GROUP:(n + 1) * GROUP].rearrange("p (n j) -> p n j", j=BLOCK)
                per = GROUP // BLOCK
                nc.vector.tensor_tensor(part, part, gates[:, n * per:(n + 1) * per, j, :], ALU.mult).then_inc(S.m, 1)

            def rest(c, j, parity, n):
                b = buffer(j, parity)
                dve.wait_ge(S.m_hi, c * 2 + j + 1)
                part = slice(n * GROUP, (n + 1) * GROUP)
                nc.vector.tensor_tensor(m_lo[b][:, part], g[:, part], m_hi[b][:, part].bitcast(F32), ALU.subtract)\
                    .then_inc(S.m_lo, 1)

            def collect(c, between):
                for n in range(OUTPUTS):
                    dve.wait_ge(S.y_ps, c * OUTPUTS + n + 1)
                    part = ff[:, n // 2, (n % 2) * HALF:(n % 2 + 1) * HALF]
                    nc.vector.tensor_tensor(part, part, y_ps[n % 3][:, :], ALU.add).then_inc(S.y_free, 1)
                    if n in between:
                        between[n]()

            def pair(c, parity, more=True, before=True):
                uT(c * 2 + 1, 1)
                steps = {}
                for n in range(3):
                    steps[1 + n] = lambda n=n: weigh(c, 0, n)
                    steps[7 + n] = lambda n=n: rest(c, 0, parity, n)
                if before:
                    collect(c - 1, steps)
                else:
                    for n in sorted(steps):
                        steps[n]()
                if more:
                    uT(c * 2 + 2, 0)
                for n in range(3):
                    weigh(c, 1, n)
                for n in range(3):
                    rest(c, 1, parity, n)
            uT(0, 0)
            pairs(dve, lambda: pair(0, 0, before=False), pair, lambda: pair(PAIRS - 1, 1, more=False))
            collect(PAIRS - 1, {})

        @block.tensor
        def _(pe):
            pe.sem_inc(S.uT_ps, 1)
            pe.wait_ge(S.consts, 16)
            u_loaded = [S.u0, S.u1]

            def transpose_u(e, c, s):
                pe.wait_ge(u_loaded[s], c * 16 + 16)
                wait(pe, S.uT_lo, e * 2)
                for k in range(KD):
                    last = nc.tensor.transpose(uT_ps[:, k, :], u[s][:, k * P:(k + 1) * P], ident[:, :])
                last.then_inc(S.uT_ps, 1)

            def first_product(e, s):
                pe.wait_ge(S.uT_lo, e * 2 + 2)
                for n in range(3):
                    wait(pe, S.gelu, e * 3 - 2 + n)
                    tok = slice(n * GROUP, (n + 1) * GROUP)
                    for k in range(KD):
                        for m, (lhs, rhs) in enumerate(((uT_lo, h_hi), (uT_hi, h_lo), (uT_hi, h_hi))):
                            last = nc.tensor.matmul(a_ps[n][:, 0:GROUP], lhs[s][:, k, :], rhs[:, k, tok],
                                                    start=k == 0 and m == 0, stop=k == KD - 1 and m == 2)
                    last.then_inc(S.act_ps, 1)

            def second_product(c, parity):
                pe.wait_ge(S.m_lo, c * 6 + 6)
                pe.wait_ge(S.v_lo, c * 2 + 2)
                for n in range(OUTPUTS):
                    tok = slice(n // 2 * P, (n // 2 + 1) * P)
                    col = slice((n % 2) * HALF, (n % 2 + 1) * HALF)
                    pe.wait_ge(S.y_free, c * OUTPUTS + n + 1)
                    for j in range(2):
                        b = buffer(j, parity)
                        for m, (lhs, rhs) in enumerate(((m_lo, v_hi), (m_hi, v_lo), (m_hi, v_hi))):
                            last = nc.tensor.matmul(y_ps[n % 3][:, :], lhs[b][:, tok], rhs[b][:, col],
                                                    start=j == 0 and m == 0, stop=j == 1 and m == 2)
                    last.then_inc(S.y_ps, 1)

            def pair(c, parity, more=True, before=True):
                transpose_u(c * 2 + 1, c, 1)
                first_product(c * 2, 0)
                if before:
                    second_product(c - 1, 1 - parity)
                if more:
                    transpose_u(c * 2 + 2, c + 1, 0)
                first_product(c * 2 + 1, 1)
            transpose_u(0, 0, 0)
            pairs(pe, lambda: pair(0, 0, before=False), pair, lambda: pair(PAIRS - 1, 1, more=False))
            second_product(PAIRS - 1, 1)


def finishing(nc, ctx, g_final, mod_rows, x1_rows, ff, y_prompt, y_sample):
    S = sems(nc, ctx, "fin", "consts power x0 x1 x_free sumsq mean rstd y0 y1 dve sum")
    with ExitStack() as mem:
        gate2 = sbuf(nc, mem, "gate2", [P, 2, D])
        g = sbuf(nc, mem, "g_final_sb", [P, D])
        power = sbuf(nc, mem, "power_e", [P, 1])
        x1 = [sbuf(nc, mem, f"x1_{s}", [P, D]) for s in range(2)]
        y = [sbuf(nc, mem, f"y{s}", [P, D]) for s in range(2)]
        squares = sbuf(nc, mem, "squares_e", [P, D])
        sumsq = sbuf(nc, mem, "sumsq_e", [P, 1])
        mean = sbuf(nc, mem, "mean_e", [P, 1])
        rstd = sbuf(nc, mem, "rstd_e", [P, 1])
        loaded, stored = [S.x0, S.x1], [S.y0, S.y1]
        block = mem.enter_context(nc.Block())

        def tiles(eng, tile):
            tile(0, 0, 0)
            tile(1, 0, 1)
            with eng.Fori(1, PROMPT_TILES // 2) as i:
                for s in range(2):
                    tile(i * 2 + s, i, s)
            tile(PROMPT_TILES, PROMPT_TILES // 2, 0, sample=True)

        @block.sync
        def _(sp):
            sp.dma_start(gate2[:, :, :], mod_rows[:, GATE2, :, :].rearrange("k p n -> p k n")).then_inc(S.consts, 16)
            sp.dma_start(g[:, :], g_final.partition_broadcast(P)).then_inc(S.consts, 16)

            def tile(t, i, s, sample=False):
                sp.wait_ge(S.x_free, t + 1)
                sp.dma_start(x1[s][:, :], x1_rows[bass.ds(t, 1), :, :].rearrange("a p d -> p (a d)"))\
                    .then_inc(loaded[s], 16)
            tiles(sp, tile)

        @block.gpsimd
        def _(pool):
            pool.sem_inc(S.x_free, 2)
            pool.memset(power[:, :], -0.5).then_inc(S.power, 1)
            pool.wait_ge(S.power, 1)

            def tile(t, i, s, sample=False):
                pool.wait_ge(S.mean, t + 1)
                pool.tensor_tensor(rstd[:, :], mean[:, :], power[:, :], ALU.pow).then_inc(S.rstd, 1)
            tiles(pool, tile)

        @block.scalar
        def _(act):
            def tile(t, i, s, sample=False):
                act.wait_ge(S.sum, t + 1)
                nc.scalar.activation(squares[:, :], y[s][:, :], ACT.Square, accum_out=sumsq[:, :]).then_inc(S.sumsq, 1)
                act.wait_ge(S.dve, t * 2 + 2)
                if sample:
                    dst = y_sample.rearrange("b t d -> (b t) d")
                else:
                    dst = y_prompt[0, bass.ds(t * P, P), :]
                act.dma_start(dst, y[s][:, :]).then_inc(stored[s], 16)
            tiles(act, tile)
            act.wait_ge(S.y0, 5 * 16)
            act.wait_ge(S.y1, 4 * 16)

        @block.vector
        def _(dve):
            dve.wait_ge(S.consts, 32)

            def tile(t, i, s, sample=False):
                wait(dve, stored[s], i * 16)
                nc.vector.tensor_tensor(y[s][:, :], ff[:, bass.ds(t, 1), :].rearrange("p a d -> p (a d)"),
                                        gate2[:, int(sample), :], ALU.mult).then_inc(S.dve, 1)
                dve.wait_ge(S.dve, t * 2 + 1)
                dve.wait_ge(loaded[s], i * 16 + 16)
                nc.vector.tensor_tensor(y[s][:, :], y[s][:, :], x1[s][:, :], ALU.add).then_inc(S.sum, 1)
                dve.wait_ge(S.sumsq, t + 1)
                nc.vector.tensor_scalar(mean[:, :], sumsq[:, :], 1.0 / D, EPS, ALU.mult, ALU.add).then_inc(S.mean, 1)
                dve.wait_ge(S.sum, t + 1)
                dve.sem_inc(S.x_free, 1)
                dve.wait_ge(S.rstd, t + 1)
                nc.vector.scalar_tensor_tensor(out=y[s][:, :], in0=y[s][:, :], scalar=rstd[:, :], in1=g[:, :],
                                               op0=ALU.mult, op1=ALU.mult).then_inc(S.dve, 1)
            tiles(dve, tile)


def program(nc, a, outs):
    y_prompt, y_sample, pool_prompt_out, pool_sample_out, v_sample_out = outs
    with ExitStack() as ctx:
        mod_rows = nc.dram_tensor("mod_rows", (2, MODS, P, D), F32, kind="Internal").ap()
        x1_rows = nc.dram_tensor("x1_rows", (TILES, P, D), F32, kind="Internal").ap()
        h2T_tiles = nc.dram_tensor("h2T_tiles", (TILES, P, D), F32, kind="Internal").ap()
        gate_blocks = nc.dram_tensor("gate_blocks", (BLOCKS, P, NKEYS, BLOCK), F32, kind="Internal").ap()
        modulation(nc, ctx, a["c_prompt"], a["c_sample"], a["w_ada"][0], a["b_ada"][0], a["g_norm1"][0],
                   a["g_norm2"][0], a["selector"], a["identity"], mod_rows)
        mixing(nc, ctx, a["x_prompt"], a["x_sample"], a["cache_pool"], a["w_in"][0], a["pool_w"][0],
               a["pool_scale"][0], a["gmlp_norm_g"][0], a["gmlp_ws"][0], a["gmlp_bs"][0], a["w_out"][0],
               a["identity"], a["bands"], mod_rows, x1_rows, h2T_tiles, pool_prompt_out, pool_sample_out,
               v_sample_out)
        routing(nc, ctx, a["peer_wq"][0], a["peer_keys"][0], a["identity"], h2T_tiles, gate_blocks)
        with nc.sbuf_tensor("ff", [P, TILES, D], F32) as ff:
            experts(nc, ctx, a["peer_u"][0], a["peer_v"][0], a["identity"], h2T_tiles, gate_blocks, ff)
            finishing(nc, ctx, a["g_final"], mod_rows, x1_rows, ff, y_prompt, y_sample)


_INS = ['x_prompt', 'x_sample', 'cache_pool', 'c_prompt', 'c_sample', 'w_ada', 'b_ada', 'g_norm1', 'w_in', 'pool_w',
        'pool_scale', 'gmlp_norm_g', 'gmlp_ws', 'gmlp_bs', 'w_out', 'g_norm2', 'peer_wq', 'peer_keys', 'peer_u',
        'peer_v', 'g_final']
_OUTS = [(1, 1024, 1024), (8, 16, 1024), (1, 1, 15, 512), (1, 8, 15, 512), (1, 8, 16, 512)]


def _constants():
    import numpy as np
    selector = np.zeros((1 + STREAMS, 2, P), np.float32)
    selector[0, 0, :] = 1
    for t in range(P):
        selector[1 + t // STEP, 1, t] = 1
    bands = np.zeros((P, 5, GROUPS, P), np.float32)
    for g in range(GROUPS):
        w = 2 << g
        for t in range(P):
            for j in range(P):
                back = t - j
                if 0 <= back < w:
                    bands[j, 0, g, t] = 1 / min(t + 1, w)
                    bands[j, 1, g, t] = 1 / w
                    if j // STEP == t // STEP:
                        bands[j, 2, g, t] = 1 / w
                if back + P < w:
                    bands[j, 3, g, t] = 1 / w
                if j < STREAMS * HIST and j // HIST == t // STEP and t % STEP - (j % HIST - HIST) < w:
                    bands[j, 4, g, t] = 1 / w
            bands[t, 0:3, g, t] -= 1
    return {"identity": np.eye(P, dtype=np.float32), "selector": selector, "bands": bands}


def kernel(**inputs):
    import numpy as _np
    import concourse.bacc as _bacc
    from concourse.bass_utils import run_bass_kernel_spmd as _run

    nc = _bacc.Bacc("TRN2", target_bir_lowering=False, num_devices=1)
    arrays, args = {}, {}
    given = {name: _np.ascontiguousarray(inputs[name]) for name in _INS}
    given.update(_constants())
    for name, a in given.items():
        arrays[f"in_{name}"] = a
        args[name] = nc.dram_tensor(f"in_{name}", a.shape, F32, kind="ExternalInput").ap()
    outs = [nc.dram_tensor(f"out_{i}", shape, F32, kind="ExternalOutput").ap() for i, shape in enumerate(_OUTS)]
    program(nc, args, outs)
    r = _run(nc, [arrays], core_ids=[0])
    return tuple(r.results[0][f"out_{i}"] for i in range(len(_OUTS)))
```

```python
import concourse.bass as bass
from concourse import mybir
from contextlib import ExitStack

F32 = mybir.dt.float32
F32R = mybir.dt.float32r
BF16 = mybir.dt.bfloat16
U32 = mybir.dt.uint32
ALU = mybir.AluOpType
ACT = mybir.ActivationFunctionType
AX = mybir.AxisListType

P = 128
D = 1024
KD = D // P
HALF = 512
PROMPT_TILES = 8
TILES = 9
STREAMS, STEP = 8, 16
HIST = 15
ZW = 1536
GROUPS = 4
HEADS = 8
TOPK = 16
NKEYS = 128
BLOCK = 64
BLOCKS = TILES * P // BLOCK
BATCH = 8
NEG = -3.0e38
EPS = 1e-6
MODS = 6
SHIFT1, SCALE1, GATE1, SHIFT2, SCALE2, GATE2 = range(MODS)


class Order:

    def __init__(self, eng, sem):
        self.eng, self.sem, self.base, self.n = eng, sem, 0, 0

    def loop(self, base):
        self.base, self.n = base, 0

    def mark(self, ins):
        ins.then_inc(self.sem, 1)
        self.n += 1

    def settle(self):
        self.eng.wait_ge(self.sem, self.base + self.n)

    def then(self, ins):
        self.mark(ins)
        self.settle()


def sems(nc, ctx, stage, names):
    made = {n: ctx.enter_context(nc.semaphore(f"{stage}_{n}")) for n in names.split()}
    return type("Sems", (), made)


def wait(eng, sem, value):
    if not isinstance(value, int) or value > 0:
        eng.wait_ge(sem, value)


def sbuf(nc, ctx, name, shape, dtype=F32):
    return ctx.enter_context(nc.sbuf_tensor(name, shape, dtype))


def psum(nc, ctx, name, shape, dtype=F32):
    return ctx.enter_context(nc.psum_tensor(name, shape, dtype))


def modulation(nc, ctx, c_prompt, c_sample, w_ada, b_ada, g1, g2, selector_in, ident_in, w_in, w_in_sb, mod_rows):
    S = sems(nc, ctx, "mod", "consts silu cT_ps cT w0 w1 w2 rows_ps rows spread_ps spread norm_g stored w_in")
    NC = 1 + STREAMS
    CHUNKS = MODS * D // HALF
    with ExitStack() as mem:
        c_rows = sbuf(nc, mem, "c_rows", [NC, D])
        c_silu = sbuf(nc, mem, "c_silu", [NC, D])
        cT = sbuf(nc, mem, "cT", [P, KD, 16])
        ident = sbuf(nc, mem, "ident_a", [P, P])
        selector = sbuf(nc, mem, "selector", [NC, 2, P])
        bias = sbuf(nc, mem, "bias", [NC, MODS * D])
        norm_g = sbuf(nc, mem, "norm_g", [P, 2, D])
        w = [sbuf(nc, mem, f"w_ada{s}", [P, KD, HALF]) for s in range(3)]
        rows = [sbuf(nc, mem, f"mod_row{s}", [NC, HALF]) for s in range(2)]
        spread = sbuf(nc, mem, "mod_spread", [P, 2, MODS, D])
        cT_ps = psum(nc, mem, "cT_ps", [P, KD, 16])
        rows_ps = [psum(nc, mem, f"rows_ps{s}", [NC, HALF]) for s in range(2)]
        spread_ps = [psum(nc, mem, f"spread_ps{s}", [P, 2, HALF]) for s in range(2)]
        w_loaded = [S.w0, S.w1, S.w2]
        w_view = w_ada.rearrange("(k p) n -> p k n", p=P)
        CONSTS = 16 * 5
        block = mem.enter_context(nc.Block())

        @block.sync
        def _(sp):
            sp.dma_start(c_rows[0:1, :], c_prompt).then_inc(S.consts, 16)
            sp.dma_start(c_rows[1:NC, :], c_sample).then_inc(S.consts, 16)
            sp.dma_start(ident[:, :], ident_in).then_inc(S.consts, 16)
            sp.dma_start(selector[:, :, :], selector_in).then_inc(S.consts, 16)
            sp.dma_start(bias[:, :], b_ada.partition_broadcast(NC)).then_inc(S.consts, 16)
            for c in range(CHUNKS):
                if c >= 3:
                    sp.wait_ge(S.rows_ps, c - 2)
                sp.dma_start(w[c % 3][:, :, :], w_view[:, :, c * HALF:(c + 1) * HALF]).then_inc(w_loaded[c % 3], 16)
                if c == 0:
                    sp.dma_start(norm_g[:, 0, :], g1.partition_broadcast(P)).then_inc(S.norm_g, 16)
                    sp.dma_start(norm_g[:, 1, :], g2.partition_broadcast(P)).then_inc(S.norm_g, 16)
                if c >= CHUNKS - KD:
                    k = c - (CHUNKS - KD)
                    sp.dma_start(w_in_sb[:, k, :], w_in[k * P:(k + 1) * P, :]).then_inc(S.w_in, 16)
            sp.wait_ge(S.w_in, 16 * KD)

        @block.scalar
        def _(act):
            act.wait_ge(S.consts, CONSTS)
            nc.scalar.activation(c_silu[:, :], c_rows[:, :], ACT.Silu).then_inc(S.silu, 1)
            for m in range(MODS):
                act.wait_ge(S.spread, 2 * m + 2)
                act.dma_start(mod_rows[:, m, :, :].rearrange("k p n -> p k n"), spread[:, :, m, :])\
                    .then_inc(S.stored, 16)
            act.wait_ge(S.stored, 16 * MODS)

        @block.vector
        def _(dve):
            dve.wait_ge(S.cT_ps, 1)
            nc.vector.tensor_copy(cT[:, :, 0:NC], cT_ps[:, :, 0:NC]).then_inc(S.cT, 1)

            def finish(c):
                m, half = c // 2, slice(c % 2 * HALF, (c % 2 + 1) * HALF)
                dve.wait_ge(S.spread_ps, c + 1)
                if m in (SCALE1, SCALE2):
                    for kind in range(2):
                        last = nc.vector.scalar_tensor_tensor(
                            out=spread[:, kind, m, half], in0=spread_ps[c % 2][:, kind, :], scalar=1.0,
                            in1=norm_g[:, m // 3, half], op0=ALU.add, op1=ALU.mult)
                else:
                    last = nc.vector.tensor_copy(spread[:, :, m, half], spread_ps[c % 2][:, :, :])
                last.then_inc(S.spread, 1)

            for c in range(CHUNKS):
                dve.wait_ge(S.rows_ps, c + 1)
                if c >= 2:
                    dve.wait_ge(S.spread_ps, c - 1)
                nc.vector.tensor_tensor(rows[c % 2][:, :], rows_ps[c % 2][:, :], bias[:, c * HALF:(c + 1) * HALF],
                                        ALU.add).then_inc(S.rows, 1)
                if c == 2:
                    dve.wait_ge(S.norm_g, 32)
                if c:
                    finish(c - 1)
            finish(CHUNKS - 1)

        @block.tensor
        def _(pe):
            pe.wait_ge(S.consts, CONSTS)
            pe.wait_ge(S.silu, 1)
            for k in range(KD):
                last = nc.tensor.transpose(cT_ps[:, k, 0:NC], c_silu[:, k * P:(k + 1) * P], ident[0:NC, 0:NC])
            last.then_inc(S.cT_ps, 1)
            pe.wait_ge(S.cT, 1)

            def spread_rows(c):
                pe.wait_ge(S.rows, c + 1)
                if c >= 2:
                    pe.wait_ge(S.spread, c - 1)
                for kind in range(2):
                    last = nc.tensor.matmul(spread_ps[c % 2][:, kind, :], selector[:, kind, :], rows[c % 2][:, :],
                                            start=True, stop=True)
                last.then_inc(S.spread_ps, 1)

            for c in range(CHUNKS):
                pe.wait_ge(w_loaded[c % 3], (c // 3 + 1) * 16)
                if c >= 2:
                    pe.wait_ge(S.rows, c - 1)
                for k in range(KD):
                    last = nc.tensor.matmul(rows_ps[c % 2][:, :], cT[:, k, 0:NC], w[c % 3][:, k, :],
                                            start=k == 0, stop=k == KD - 1)
                last.then_inc(S.rows_ps, 1)
                if c:
                    spread_rows(c - 1)
            spread_rows(CHUNKS - 1)


class Tile:

    def __init__(self, j, offset=0):
        self.j, self.offset = j, offset
        self.n = j * 2 + offset
        self.half = j + offset // 2
        self.s = offset % 2
        known = isinstance(j, int)
        self.first = known and self.n == 0
        self.last = self.sample = known and self.n == TILES - 1

    def after(self, k):
        return Tile(self.j, self.offset + k)


def mixing(nc, ctx, x_prompt, x_sample, cache_pool, w_in_sb, pool_w, pool_scale, gmlp_g, gmlp_ws, gmlp_bs,
           w_out, ident_in, bands_in, mod_rows, x1_rows, h2T_tiles, pool_prompt_out, pool_sample_out, v_sample_out):
    S = sems(nc, ctx, "mix", "passed consts early mods_in mods_sample w_out_in x0 x1 r0 r1 ws_ps ws_sb wm bs_rep zero "
                             "sumsq mean rstd h_scaled h hT_ps hT z_ps zp zu zv v_squared v_summed vmean vrstd "
                             "v_scaled vn diff diffT pool pool_mixed gmlp_ps s_biased gmlp_mixed mix mix_read "
                             "x1_ready sumsq2 mean2 rstd2 h2_scaled h2 h2T_ps h2T x1_out0 x1_out1 h2T_out outs")
    x_loaded, r_loaded = [S.x0, S.x1], [S.r0, S.r1]
    x1_stored = [S.x1_out0, S.x1_out1]
    with ExitStack() as mem:
        w_out_sb = sbuf(nc, mem, "w_out_sb", [P, KD, D])
        mods = sbuf(nc, mem, "mods", [P, 2, 5, D])
        ident = sbuf(nc, mem, "ident_b", [P, P])
        bands = sbuf(nc, mem, "bands", [P, 5, GROUPS, P])
        BAND_FIRST, BAND_NEXT, BAND_SAMPLE, BAND_BEFORE, BAND_HIST = range(5)
        hist = sbuf(nc, mem, "hist", [STREAMS * HIST, HALF])
        pool_w_sb = sbuf(nc, mem, "pool_w_sb", [P, GROUPS, P])
        pool_scale_sb = sbuf(nc, mem, "pool_scale_sb", [P, GROUPS])
        gmlp_g_sb = sbuf(nc, mem, "gmlp_g_sb", [P, HALF])
        ws = sbuf(nc, mem, "ws", [P, 2, GROUPS, P])
        wmT = sbuf(nc, mem, "wmT", [P, 2, GROUPS, P])
        bs = sbuf(nc, mem, "bs", [P, 2, GROUPS, P])
        power = sbuf(nc, mem, "power", [P, GROUPS])
        x = [sbuf(nc, mem, f"x_in{s}", [P, D]) for s in range(2)]
        squares = sbuf(nc, mem, "squares", [P, D], BF16)
        squares2 = sbuf(nc, mem, "squares2", [P, D], BF16)
        sumsq = sbuf(nc, mem, "sumsq", [P, 1])
        mean = sbuf(nc, mem, "mean", [P, 1])
        rstd = sbuf(nc, mem, "rstd", [P, 1])
        sumsq2 = sbuf(nc, mem, "sumsq2", [P, 1])
        mean2 = sbuf(nc, mem, "mean2", [P, 1])
        rstd2 = sbuf(nc, mem, "rstd2", [P, 1])
        h = sbuf(nc, mem, "h", [P, D])
        hT = sbuf(nc, mem, "hT", [P, KD, P])
        p = [sbuf(nc, mem, f"p{s}", [P, HALF]) for s in range(2)]
        uT = sbuf(nc, mem, "uT", [P, GROUPS, P])
        v = sbuf(nc, mem, "v", [P, GROUPS, P])
        vsq = sbuf(nc, mem, "vsq", [P, GROUPS, P])
        vsum = sbuf(nc, mem, "vsum", [P, GROUPS])
        vrstd = sbuf(nc, mem, "vrstd", [P, GROUPS])
        sT = sbuf(nc, mem, "sT", [P, GROUPS, P])
        diffT = sbuf(nc, mem, "diffT", [P, GROUPS, P])
        mixT = sbuf(nc, mem, "mixT", [P, KD, P])
        x1 = [sbuf(nc, mem, f"x1_in{s}", [P, D]) for s in range(2)]
        gated = sbuf(nc, mem, "gated_mix", [P, D])
        h2 = sbuf(nc, mem, "h2", [P, D])
        h2T = sbuf(nc, mem, "h2T_b", [P, KD, P])
        t_ps = psum(nc, mem, "t_ps", [P, KD, P])
        z_ps = psum(nc, mem, "z_ps", [P, 3, HALF])
        mix_ps = psum(nc, mem, "mix_ps", [P, 2, HALF])
        diff_ps = psum(nc, mem, "diff_ps", [P, GROUPS, P])
        sT_ps = mix_ps[:, 0, :].rearrange("p (g t) -> p g t", g=GROUPS)
        pool_ps = mix_ps[:, 1, :].rearrange("p (g t) -> p g t", g=GROUPS)
        EARLY = 16 * (2 + STREAMS)
        CONSTS = 16 * 6
        block = mem.enter_context(nc.Block())

        def periods(eng, period):
            period(Tile(0, 0))
            period(Tile(0, 1))
            with eng.Fori(1, 3) as j:
                period(Tile(j, 0))
                period(Tile(j, 1))
            for t in range(6, TILES):
                period(Tile(3, t - 6))

        @block.sync
        def _(sp):
            def src(t):
                if t.sample:
                    return x_sample.rearrange("b t d -> (b t) d")
                return x_prompt[0, bass.ds(t.n * P, P), :]

            def load_x(t):
                wait(sp, S.h, t.n - 1)
                sp.dma_start(x[t.s][:, :], src(t)).then_inc(x_loaded[t.s], 16)

            def load_residual(t):
                wait(sp, x1_stored[t.s], t.half * 16)
                sp.dma_start(x1[t.s][:, :], src(t)).then_inc(r_loaded[t.s], 16)

            sp.dma_start(x[0][:, :], src(Tile(0))).then_inc(x_loaded[0], 16)
            sp.dma_start(mods[:, 0, 0:2, :], mod_rows[0, 0:2, :, :].rearrange("m p n -> p m n"))\
                .then_inc(S.mods_in, 16)
            sp.dma_start(ident[:, :], ident_in).then_inc(S.early, 16)
            sp.dma_start(ws[:, 0, :, :], gmlp_ws.rearrange("h i j -> i h j")).then_inc(S.early, 16)
            sp.wait_ge(S.zero, 1)
            for b in range(STREAMS):
                span = slice(b * STEP, (b + 1) * STEP)
                sp.dma_start(ws[span, 1, :, span], gmlp_ws[:, 0:STEP, 0:STEP].rearrange("h i j -> i h j"))\
                    .then_inc(S.early, 16)
            sp.dma_start(x[1][:, :], src(Tile(0, 1))).then_inc(x_loaded[1], 16)
            c = S.consts
            sp.dma_start(bs[:, 0, :, :].rearrange("p h i -> p (h i)"),
                         gmlp_bs.rearrange("h i -> (h i)").partition_broadcast(P)).then_inc(c, 16)
            sp.dma_start(gmlp_g_sb[:, :], gmlp_g.partition_broadcast(P)).then_inc(c, 16)
            sp.dma_start(pool_w_sb[:, :, :], pool_w.rearrange("g c d -> c g d")).then_inc(c, 16)
            sp.dma_start(pool_scale_sb[:, :], pool_scale.rearrange("(g c) -> c g", g=GROUPS),
                         allow_slow_non_contiguous=True).then_inc(c, 16)
            sp.dma_start(bands[:, :, :, :], bands_in).then_inc(c, 16)
            sp.dma_start(hist[:, :], cache_pool.rearrange("l b r c -> (l b r) c")).then_inc(c, 16)
            sp.dma_start(w_out_sb[:, :, :], w_out.rearrange("(k p) n -> p k n", p=P)).then_inc(S.w_out_in, 16)
            sp.dma_start(mods[:, 0, 2:5, :], mod_rows[0, 2:5, :, :].rearrange("m p n -> p m n"))\
                .then_inc(S.w_out_in, 16)
            sp.dma_start(x1[0][:, :], src(Tile(0))).then_inc(r_loaded[0], 16)
            sp.dma_start(x1[1][:, :], src(Tile(0, 1))).then_inc(r_loaded[1], 16)
            sp.dma_start(mods[:, 1, :, :], mod_rows[1, 0:5, :, :].rearrange("m p n -> p m n"))\
                .then_inc(S.mods_sample, 16)

            def period(t):
                if not (t.last or t.after(1).last):
                    load_x(t.after(2))
                if not (t.first or t.last):
                    load_residual(t.after(1))
            periods(sp, period)

        @block.gpsimd
        def _(pool):
            pool.memset(ws[:, 1, :, :], 0.0).then_inc(S.zero, 1)
            pool.memset(power[:, :], -0.5).then_inc(S.zero, 1)
            pool.wait_ge(S.zero, 2)

            def root(t):
                pool.wait_ge(S.mean, t.n + 1)
                pool.tensor_tensor(rstd[:, :], mean[:, :], power[:, 0:1], ALU.pow).then_inc(S.rstd, 1)

            def head_roots(t):
                pool.wait_ge(S.vmean, t.n + 1)
                pool.tensor_tensor(vrstd[:, :], vsum[:, :], power[:, :], ALU.pow).then_inc(S.vrstd, 1)

            def store_x1(t):
                pool.wait_ge(S.h2, t.n + 1)
                pool.sem_inc(S.passed, 1)
                pool.dma_start(x1_rows[bass.ds(t.n, 1), :, :].rearrange("a p d -> p (a d)"), x1[t.s][:, :])\
                    .then_inc(x1_stored[t.s], 16)

            def root_x1(t):
                pool.wait_ge(S.mean2, t.n + 1)
                pool.tensor_tensor(rstd2[:, :], mean2[:, :], power[:, 0:1], ALU.pow).then_inc(S.rstd2, 1)

            def store_h2T(t):
                pool.wait_ge(S.h2T, t.n * 2 + 2)
                pool.sem_inc(S.passed, 1)
                pool.dma_start(h2T_tiles[bass.ds(t.n, 1), :, :].rearrange("a p d -> p (a d)"),
                               h2T[:, :, :].rearrange("p k t -> p (k t)")).then_inc(S.h2T_out, 16)

            def period(t):
                if not t.first:
                    root_x1(t.after(-1))
                if not (t.last or t.after(1).last):
                    root(t.after(2))
                if not t.first:
                    store_x1(t.after(-1))
                    store_h2T(t.after(-1))
                if not t.last:
                    head_roots(t.after(1))

            root(Tile(0))
            pool.wait_ge(S.ws_sb, 2)
            pool.affine_select(out=wmT[:, :, :, :], in_=wmT[:, :, :, :], compare_op=ALU.is_ge, fill=0.0, base=0,
                               pattern=[[0, 2 * GROUPS], [1, P]], channel_multiplier=-1).then_inc(S.wm, 1)
            root(Tile(0, 1))
            head_roots(Tile(0))
            periods(pool, period)
            root_x1(Tile(0, TILES - 1))
            store_x1(Tile(0, TILES - 1))
            pool.wait_ge(S.zp, TILES)
            for b in range(STREAMS):
                pool.dma_start(pool_sample_out[0, b, :, :], p[0][b * STEP + 1:(b + 1) * STEP, :]).then_inc(S.outs, 16)
            pool.wait_ge(S.vn, TILES)
            pool.dma_start(v_sample_out.rearrange("l b t c -> (l b t) c"),
                           v[:, :, :].rearrange("p g c -> p (g c)")).then_inc(S.outs, 16)
            pool.dma_start(pool_prompt_out[0, 0, :, :], p[1][P - HIST:P, :]).then_inc(S.outs, 16)
            store_h2T(Tile(0, TILES - 1))
            pool.wait_ge(S.x1_out0, 16 * 5)
            pool.wait_ge(S.x1_out1, 16 * 4)
            pool.wait_ge(S.h2T_out, 16 * TILES)
            pool.wait_ge(S.outs, 16 * (STREAMS + 2))

        @block.scalar
        def _(act):
            def square_x(t):
                act.wait_ge(x_loaded[t.s], (t.half + 1) * 16)
                wait(act, S.mean, t.n)
                nc.scalar.activation(squares[:, :], x[t.s][:, :], ACT.Square, accum_out=sumsq[:, :])\
                    .then_inc(S.sumsq, 1)

            def square_x1(t):
                act.wait_ge(S.x1_ready, t.n + 1)
                wait(act, S.mean2, t.n)
                nc.scalar.activation(squares2[:, :], x1[t.s][:, :], ACT.Square, accum_out=sumsq2[:, :])\
                    .then_inc(S.sumsq2, 1)

            def copy_hT(t):
                act.wait_ge(S.hT_ps, t.n + 1)
                wait(act, S.z_ps, t.n * 3)
                for half in (slice(0, 4), slice(4, 8)):
                    nc.scalar.activation(hT[:, half, :], t_ps[:, half, :], ACT.Copy).then_inc(S.hT, 1)

            def copy_h2T(t):
                act.wait_ge(S.h2T_ps, t.n + 1)
                wait(act, S.h2T_out, t.n * 16)
                for half in (slice(0, 4), slice(4, 8)):
                    nc.scalar.activation(h2T[:, half, :], t_ps[:, half, :], ACT.Copy).then_inc(S.h2T, 1)

            def take_p(t):
                act.wait_ge(S.z_ps, t.n * 3 + 1)
                nc.scalar.activation(p[t.s][:, :], z_ps[:, 0, :], ACT.Copy).then_inc(S.zp, 1)

            def take_u(t):
                act.wait_ge(S.z_ps, t.n * 3 + 2)
                wait(act, S.gmlp_mixed, t.n)
                nc.scalar.activation(uT[:, :, :].rearrange("p g t -> p (g t)"), z_ps[:, 1, :], ACT.Gelu)\
                    .then_inc(S.zu, 1)

            def take_v(t):
                act.wait_ge(S.z_ps, t.n * 3 + 3)
                nc.scalar.activation(v[:, :, :].rearrange("p g c -> p (g c)"), z_ps[:, 2, :], ACT.Gelu)\
                    .then_inc(S.zv, 1)

            def period(t):
                if not t.last:
                    copy_hT(t.after(1))
                if not t.first:
                    square_x1(t.after(-1))
                act.wait_ge(S.diff, t.n + 1)
                nc.scalar.activation(diffT[:, :, :], diff_ps[:, :, :], ACT.Copy).then_inc(S.diffT, 1)
                if not (t.last or t.after(1).last):
                    square_x(t.after(2))
                if not t.last:
                    take_p(t.after(1))
                    take_u(t.after(1))
                if not t.first:
                    copy_h2T(t.after(-1))
                if not t.last:
                    take_v(t.after(1))

            square_x(Tile(0))
            copy_hT(Tile(0))
            square_x(Tile(0, 1))
            take_p(Tile(0))
            take_u(Tile(0))
            take_v(Tile(0))
            periods(act, period)
            square_x1(Tile(0, TILES - 1))
            copy_h2T(Tile(0, TILES - 1))

        @block.vector
        def _(dve):
            def norm_x(t):
                kind = int(t.sample)
                dve.wait_ge(S.sumsq, t.n + 1)
                nc.vector.tensor_scalar(mean[:, :], sumsq[:, :], 1.0 / D, EPS, ALU.mult, ALU.add).then_inc(S.mean, 1)
                dve.wait_ge(S.rstd, t.n + 1)
                wait(dve, S.hT_ps, t.n)
                nc.vector.scalar_tensor_tensor(out=h[:, :], in0=x[t.s][:, :], scalar=rstd[:, :],
                                               in1=mods[:, kind, SCALE1, :], op0=ALU.mult, op1=ALU.mult)\
                    .then_inc(S.h_scaled, 1)
                dve.wait_ge(S.h_scaled, t.n + 1)
                nc.vector.tensor_tensor(h[:, :], h[:, :], mods[:, kind, SHIFT1, :], ALU.add).then_inc(S.h, 1)

            def mean_x1(t):
                dve.wait_ge(S.sumsq2, t.n + 1)
                nc.vector.tensor_scalar(mean2[:, :], sumsq2[:, :], 1.0 / D, EPS, ALU.mult, ALU.add)\
                    .then_inc(S.mean2, 1)

            def norm_x1(t):
                kind = int(t.sample)
                dve.wait_ge(S.rstd2, t.n + 1)
                wait(dve, S.h2T_ps, t.n)
                nc.vector.scalar_tensor_tensor(out=h2[:, :], in0=x1[t.s][:, :], scalar=rstd2[:, :],
                                               in1=mods[:, kind, SCALE2, :], op0=ALU.mult, op1=ALU.mult)\
                    .then_inc(S.h2_scaled, 1)
                dve.wait_ge(S.h2_scaled, t.n + 1)
                nc.vector.tensor_tensor(h2[:, :], h2[:, :], mods[:, kind, SHIFT2, :], ALU.add).then_inc(S.h2, 1)

            def norm_v(t):
                dve.wait_ge(S.zv, t.n + 1)
                nc.vector.tensor_tensor(vsq[:, :, :], v[:, :, :], v[:, :, :], ALU.mult).then_inc(S.v_squared, 1)
                dve.wait_ge(S.v_squared, t.n + 1)
                nc.vector.tensor_reduce(vsum[:, :], vsq[:, :, :], AX.X, ALU.add).then_inc(S.v_summed, 1)
                dve.wait_ge(S.v_summed, t.n + 1)
                nc.vector.tensor_scalar(vsum[:, :], vsum[:, :], 1.0 / P, EPS, ALU.mult, ALU.add).then_inc(S.vmean, 1)
                dve.wait_ge(S.vrstd, t.n + 1)
                nc.vector.tensor_tensor(v[:, :, :], v[:, :, :], vrstd[:, :].rearrange("p (g c) -> p g c", c=1)
                                        .to_broadcast([P, GROUPS, P]), ALU.mult).then_inc(S.v_scaled, 1)
                dve.wait_ge(S.v_scaled, t.n + 1)
                nc.vector.tensor_tensor(v[:, :, :], v[:, :, :],
                                        gmlp_g_sb[:, :].rearrange("p (g c) -> p g c", g=GROUPS), ALU.mult)\
                    .then_inc(S.vn, 1)

            def mix_gmlp(t):
                dve.wait_ge(S.gmlp_ps, t.n + 1)
                nc.vector.tensor_tensor(sT[:, :, :], sT_ps, bs[:, int(t.sample), :, :], ALU.add)\
                    .then_inc(S.s_biased, 1)
                dve.wait_ge(S.s_biased, t.n + 1)
                dve.wait_ge(S.zu, t.n + 1)
                nc.vector.tensor_tensor(mixT[:, 4:8, :], uT[:, :, :], sT[:, :, :], ALU.mult).then_inc(S.gmlp_mixed, 1)

            def mix_pool(t):
                dve.wait_ge(S.pool, t.n + 1)
                nc.vector.tensor_tensor(mixT[:, 0:4, :], pool_ps, pool_scale_sb[:, :]
                                        .rearrange("p (g c) -> p g c", c=1).to_broadcast([P, GROUPS, P]), ALU.mult)\
                    .then_inc(S.pool_mixed, 1)

            def add_mix(t):
                dve.wait_ge(S.mix, t.n + 1)
                nc.vector.tensor_tensor(gated[:, :], mix_ps[:, :, :].rearrange("p a n -> p (a n)"),
                                        mods[:, int(t.sample), GATE1, :], ALU.mult).then_inc(S.mix_read, 1)
                dve.wait_ge(S.mix_read, t.n + 1)
                dve.wait_ge(r_loaded[t.s], (t.half + 1) * 16)
                nc.vector.tensor_tensor(x1[t.s][:, :], x1[t.s][:, :], gated[:, :], ALU.add).then_inc(S.x1_ready, 1)

            def period(t):
                if not t.first:
                    add_mix(t.after(-1))
                mix_gmlp(t)
                if not t.first:
                    mean_x1(t.after(-1))
                mix_pool(t)
                if not t.first:
                    norm_x1(t.after(-1))
                if not (t.last or t.after(1).last):
                    norm_x(t.after(2))
                if not t.last:
                    norm_v(t.after(1))

            dve.wait_ge(S.mods_in, 16)
            norm_x(Tile(0))
            dve.wait_ge(S.ws_ps, 1)
            nc.vector.tensor_copy(wmT[:, 0, :, :], z_ps[:, 0, :].rearrange("p (g t) -> p g t", g=GROUPS))\
                .then_inc(S.ws_sb, 1)
            nc.vector.tensor_copy(wmT[:, 1, :, :], z_ps[:, 1, :].rearrange("p (g t) -> p g t", g=GROUPS))\
                .then_inc(S.ws_sb, 1)
            norm_x(Tile(0, 1))
            dve.wait_ge(S.consts, CONSTS)
            nc.vector.tensor_copy(bs[:, 1, :, :].rearrange("p h (b i) -> p h b i", b=STREAMS),
                                  bs[:, 0, :, 0:STEP].rearrange("p h (b i) -> p h b i", b=1)
                                  .to_broadcast([P, GROUPS, STREAMS, STEP])).then_inc(S.bs_rep, 1)
            norm_v(Tile(0))
            dve.wait_ge(S.bs_rep, 1)
            dve.wait_ge(S.w_out_in, 32)
            dve.wait_ge(S.mods_sample, 16)
            periods(dve, period)
            add_mix(Tile(0, TILES - 1))
            mean_x1(Tile(0, TILES - 1))
            norm_x1(Tile(0, TILES - 1))

        @block.tensor
        def _(pe):
            def transpose_h(t):
                pe.wait_ge(S.h, t.n + 1)
                if not (isinstance(t.n, int) and t.n < 3):
                    pe.wait_ge(S.h2T, (t.n - 2) * 2)
                for k in range(KD):
                    last = nc.tensor.transpose(t_ps[:, k, :], h[:, k * P:(k + 1) * P], ident[:, :])
                last.then_inc(S.hT_ps, 1)

            def project(t, b):
                if b == 0:
                    pe.wait_ge(S.hT, t.n * 2 + 2)
                wait(pe, (S.zp, S.zu, S.zv)[b], t.n)
                for k in range(KD):
                    if b != 1:
                        last = nc.tensor.matmul(z_ps[:, b, :], hT[:, k, :], w_in_sb[:, k, b * HALF:(b + 1) * HALF],
                                                start=k == 0, stop=k == KD - 1)
                if b == 1:
                    for g in range(GROUPS):
                        chan = slice(HALF + g * P, HALF + (g + 1) * P)
                        for k in range(KD):
                            last = nc.tensor.matmul(z_ps[:, 1, g * P:(g + 1) * P], w_in_sb[:, k, chan], hT[:, k, :],
                                                    start=k == 0, stop=k == KD - 1)
                last.then_inc(S.z_ps, 1)

            def difference(t):
                pe.wait_ge(S.zp, t.n + 1)
                wait(pe, S.diffT, t.n)
                now, before, rows = BAND_NEXT, bands[:, BAND_BEFORE], p[1 - t.s]
                if t.sample:
                    now, before, rows = BAND_SAMPLE, bands[0:STREAMS * HIST, BAND_HIST], hist
                if t.first:
                    now = BAND_FIRST
                for g in range(GROUPS):
                    chan = slice(g * P, (g + 1) * P)
                    last = nc.tensor.matmul(diff_ps[:, g, :], p[t.s][:, chan], bands[:, now, g, :],
                                            start=True, stop=t.first)
                    if not t.first:
                        last = nc.tensor.matmul(diff_ps[:, g, :], rows[:, chan], before[:, g, :],
                                                start=False, stop=True)
                last.then_inc(S.diff, 1)

            def mix_tokens(t):
                pe.wait_ge(S.vn, t.n + 1)
                wait(pe, S.mix_read, t.n)
                for g in range(GROUPS):
                    last = nc.tensor.matmul(sT_ps[:, g, :], v[:, g, :], wmT[:, int(t.sample), g, :],
                                            start=True, stop=True)
                last.then_inc(S.gmlp_ps, 1)

            def mix_channels(t):
                pe.wait_ge(S.diffT, t.n + 1)
                for g in range(GROUPS):
                    last = nc.tensor.matmul(pool_ps[:, g, :], pool_w_sb[:, g, :], diffT[:, g, :],
                                            start=True, stop=True)
                last.then_inc(S.pool, 1)

            def transpose_h2(t):
                pe.wait_ge(S.h2, t.n + 1)
                if t.last or t.after(1).last:
                    pe.wait_ge(S.hT, TILES * 2)
                else:
                    pe.wait_ge(S.hT, (t.n + 3) * 2)
                if t.last:
                    pe.wait_ge(S.h2T, t.n * 2)
                for k in range(KD):
                    last = nc.tensor.transpose(t_ps[:, k, :], h2[:, k * P:(k + 1) * P], ident[:, :])
                last.then_inc(S.h2T_ps, 1)

            def project_out(t):
                pe.wait_ge(S.gmlp_mixed, t.n + 1)
                pe.wait_ge(S.pool_mixed, t.n + 1)
                for b in range(2):
                    for k in range(KD):
                        last = nc.tensor.matmul(mix_ps[:, b, :], mixT[:, k, :], w_out_sb[:, k, b * HALF:(b + 1) * HALF],
                                                start=k == 0, stop=k == KD - 1)
                last.then_inc(S.mix, 1)

            def period(t):
                if not t.last:
                    transpose_h(t.after(1))
                difference(t)
                mix_tokens(t)
                if not t.last:
                    project(t.after(1), 0)
                mix_channels(t)
                if not t.last:
                    project(t.after(1), 1)
                if not t.first:
                    transpose_h2(t.after(-1))
                if not t.last:
                    project(t.after(1), 2)
                project_out(t)

            pe.wait_ge(S.early, EARLY)
            for kind in range(2):
                for g in range(GROUPS):
                    last = nc.tensor.transpose(z_ps[:, kind, g * P:(g + 1) * P], ws[:, kind, g, :], ident[:, :])
            last.then_inc(S.ws_ps, 1)
            transpose_h(Tile(0))
            pe.wait_ge(S.ws_sb, 2)
            for b in range(3):
                project(Tile(0), b)
            pe.wait_ge(S.wm, 1)
            pe.wait_ge(S.consts, CONSTS)
            pe.wait_ge(S.w_out_in, 32)
            periods(pe, period)
            transpose_h2(Tile(0, TILES - 1))


def routing(nc, ctx, wq, keys, ident_in, h2T_tiles, gate_blocks):
    S = sems(nc, ctx, "route", "passed consts wq0 wq1 wq2 wq3 iota h2 keys_ps keysT q_ps q qT_ps qT scores "
                               "scores_used shifted exp gate_ready ranked keyed slotsT_ps slotsT left right_hot "
                               "gated_vector gated_pool place_ps placed out0 out1 dve pool")
    HP = HEADS * 2
    WIDE, NARROW = 4, 12
    NW = WIDE * TOPK
    SUMS = NW + NARROW * 4
    with ExitStack() as mem:
        wq_sb = [sbuf(nc, mem, f"wq_sb{b}", [P, KD, HALF]) for b in range(4)]
        keysT = sbuf(nc, mem, "keysT", [P, HP, NKEYS])
        ident = sbuf(nc, mem, "ident_c", [P, P])
        h2T = sbuf(nc, mem, "h2T", [P, KD, P])
        q = sbuf(nc, mem, "q", [P, 4, P])
        qT = sbuf(nc, mem, "qT", [P, HP, P])
        work = sbuf(nc, mem, "work", [P, HP * NKEYS])
        best = sbuf(nc, mem, "best", [P, HP, TOPK])
        best_at = sbuf(nc, mem, "best_at", [P, HP, TOPK], U32)
        best_key = sbuf(nc, mem, "best_key", [P, HP, TOPK], BF16)
        pair = sbuf(nc, mem, "pair", [P, HEADS, TOPK])
        pair_at = sbuf(nc, mem, "pair_at", [P, HEADS, TOPK], U32)
        soft = sbuf(nc, mem, "soft", [P, HEADS, TOPK])
        digits = sbuf(nc, mem, "digits", [P, 4, HEADS, TOPK], U32)
        narrow = sbuf(nc, mem, "narrow", [P, HEADS, TOPK])
        ranks = sbuf(nc, mem, "ranks", [P, 2, HEADS, TOPK])
        rank = sbuf(nc, mem, "rank", [P, 2, HEADS, TOPK], BF16)
        hit = sbuf(nc, mem, "hit", [P, 2, HEADS, TOPK, TOPK], BF16)
        total = sbuf(nc, mem, "total", [P, HEADS])
        slots = sbuf(nc, mem, "slots", [P, 3, HEADS, TOPK])
        keyT = sbuf(nc, mem, "keyT", [P, 2, P], BF16)
        gateT = sbuf(nc, mem, "gateT", [P, P])
        LEFTS = 4
        left = [sbuf(nc, mem, f"left{s}", [P, BATCH, NKEYS]) for s in range(LEFTS)]
        right_hot = [sbuf(nc, mem, f"right_hot{s}", [P, NKEYS, BATCH], BF16) for s in range(2)]
        right = [sbuf(nc, mem, f"right{s}", [P, BATCH, NKEYS]) for s in range(2)]
        dense = [sbuf(nc, mem, f"dense{s}", [P, NKEYS, BLOCK]) for s in range(2)]
        iota_rank = sbuf(nc, mem, "iota_rank", [P, TOPK, TOPK], BF16)
        iota_key = sbuf(nc, mem, "iota_key", [P, NKEYS], BF16)
        iota_keys = sbuf(nc, mem, "iota_keys", [P, NKEYS, BATCH], BF16)
        s_ps = psum(nc, mem, "s_ps", [P, HP, NKEYS])
        q_ps = psum(nc, mem, "q_ps", [P, HALF])
        x_ps = psum(nc, mem, "x_ps", [P, 4, P])
        place_ps = psum(nc, mem, "place_ps", [P, 2, 4, NKEYS])
        wq_loaded = [S.wq0, S.wq1, S.wq2, S.wq3]
        stored = [S.out0, S.out1]
        BATCHES = P // BATCH
        key4 = best_key[:, :, :].rearrange("p (h s) k -> p h s k", s=2)
        block = mem.enter_context(nc.Block())

        def on_vector(b):
            return b % 4 == 3
        ON_POOL = sum(not on_vector(b) for b in range(BATCHES))

        def gated(eng, b):
            return eng.tensor_tensor(
                right[b % 2][:, :, :], right_hot[b % 2][:, :, :].rearrange("p i t -> p t i"),
                gateT[:, b * BATCH:(b + 1) * BATCH].rearrange("p (t o) -> p t o", o=1)
                .to_broadcast([P, BATCH, NKEYS]), ALU.mult)

        def wait_for_gated(eng, t, b):
            if on_vector(b):
                eng.wait_ge(S.gated_vector, t * (BATCHES - ON_POOL) + sum(on_vector(n) for n in range(b + 1)))
            else:
                eng.wait_ge(S.gated_pool, t * ON_POOL + sum(not on_vector(n) for n in range(b + 1)))

        def wait_for_placed(eng, t, b, buffers):
            wait(eng, S.place_ps, t * (BATCHES * 2) + max(b + 1 - buffers, 0) * 2)

        def periods(eng, choose, place):
            choose(0, True)
            for t in (1,):
                choose(t, True)
                place(t - 1)
            with eng.Fori(2, TILES - 1) as t:
                choose(t, True)
                place(t - 1)
            choose(TILES - 1, False)
            place(TILES - 2)
            place(TILES - 1)

        @block.sync
        def _(sp):
            sp.dma_start(work[:, :].rearrange("k (n c) -> k n c", n=HP), keys.rearrange("h s k c -> k (h s) c"))\
                .then_inc(S.consts, 16)
            sp.dma_start(ident[:, :], ident_in).then_inc(S.consts, 16)
            sp.dma_start(h2T[:, :, :].rearrange("p k t -> p (k t)"), h2T_tiles[0, :, :]).then_inc(S.h2, 16)
            for b in range(4):
                sp.dma_start(wq_sb[b][:, :, :], wq[:, b * HALF:(b + 1) * HALF].rearrange("(k p) n -> p k n", p=P))\
                    .then_inc(wq_loaded[b], 16)

            def load_h2(t):
                sp.wait_ge(S.q_ps, t * 4)
                sp.dma_start(h2T[:, :, :].rearrange("p k t -> p (k t)"),
                             h2T_tiles[bass.ds(t, 1), :, :].rearrange("a p d -> p (a d)")).then_inc(S.h2, 16)

            def store(t):
                for half in range(2):
                    sp.wait_ge(S.placed, t * 32 + 2 + 16 * (half + 1))
                    sp.dma_start(gate_blocks[bass.ds(t * 2 + half, 1), :, :, :].rearrange("a p i j -> p (a i j)"),
                                 dense[half][:, :, :].rearrange("p i j -> p (i j)")).then_inc(stored[half], 16)
            load_h2(1)
            load_h2(2)
            with sp.Fori(1, TILES - 2) as t:
                load_h2(t + 2)
                store(t - 1)
            for t in range(TILES - 3, TILES):
                store(t)
            for half in range(2):
                sp.wait_ge(stored[half], TILES * 16)

        @block.gpsimd
        def _(pool):
            own = Order(pool, S.pool)
            PER_TILE = 8
            pool.iota(iota_rank[:, :, :], pattern=[[1, TOPK], [0, TOPK]], base=0, channel_multiplier=0,
                      allow_small_or_imprecise_dtypes=True).then_inc(S.iota, 1)
            pool.iota(iota_key[:, :], pattern=[[1, NKEYS]], base=0, channel_multiplier=0,
                      allow_small_or_imprecise_dtypes=True).then_inc(S.iota, 1)
            pool.iota(iota_keys[:, :, :], pattern=[[1, NKEYS], [0, BATCH]], base=0, channel_multiplier=0,
                      allow_small_or_imprecise_dtypes=True).then_inc(S.iota, 1)

            def place(t):
                own.loop(t * PER_TILE)
                for s in range(2):
                    pool.wait_ge(S.ranked, t * 2 + s + 1)
                    if s == 0:
                        wait(pool, S.slotsT_ps, t)
                    own.then(nc.gpsimd.tensor_tensor(
                        hit[:, s], hit[:, s], key4[:, :, s, :].rearrange("p h (a o) -> p h a o", o=1)
                        .to_broadcast([P, HEADS, TOPK, TOPK]), ALU.mult))
                    for n in (8, 4, 2):
                        own.then(nc.gpsimd.tensor_tensor(hit[:, s, :, 0:n, :], hit[:, s, :, 0:n, :],
                                                         hit[:, s, :, n:2 * n, :], ALU.add))
                    nc.gpsimd.tensor_tensor(slots[:, s, :, :], hit[:, s, :, 0, :], hit[:, s, :, 1, :], ALU.add)\
                        .then_inc(S.keyed, 1)
                assert own.n == PER_TILE
                pool.wait_ge(S.slotsT, t * 2 + 2)
                for b in range(BATCHES):
                    if not on_vector(b):
                        wait_for_placed(pool, t, b, 2)
                        pool.wait_ge(S.right_hot, t * BATCHES + b + 1)
                        gated(nc.gpsimd, b).then_inc(S.gated_pool, 1)
            periods(pool, lambda t, more: None, place)

        @block.scalar
        def _(act):
            act.sem_inc(S.placed, 2)
            act.wait_ge(S.keys_ps, 1)
            nc.scalar.activation(keysT[:, :, :], s_ps[:, :, :], ACT.Copy).then_inc(S.keysT, 1)

            def queries(t):
                for b in range(4):
                    n = t * 4 + b
                    act.wait_ge(S.q_ps, n + 1)
                    wait(act, S.qT_ps, n)
                    nc.scalar.activation(q[:, :, :].rearrange("p a c -> p (a c)"), q_ps[:, :], ACT.Copy)\
                        .then_inc(S.q, 1)
                    act.wait_ge(S.qT_ps, n + 1)
                    wait(act, S.scores, t * 4)
                    nc.scalar.activation(qT[:, b * 4:b * 4 + 4, :], x_ps[:, :, :], ACT.Copy).then_inc(S.qT, 1)

            def choose(t, more):
                if more:
                    queries(t + 1)
                if not isinstance(t, int) or t > 0:
                    act.wait_ge(S.slotsT_ps, t)
                    nc.scalar.activation(keyT[:, :, :], x_ps[:, 0:2, :], ACT.Copy).then_inc(S.slotsT, 1)
                    nc.scalar.activation(gateT[:, :], x_ps[:, 2, :], ACT.Copy).then_inc(S.slotsT, 1)
                act.wait_ge(S.shifted, t + 1)
                nc.scalar.activation(soft[:, :, :], soft[:, :, :], ACT.Exp).then_inc(S.exp, 1)

            def place(t):
                if isinstance(t, int) and t == TILES - 1:
                    act.wait_ge(S.slotsT_ps, t + 1)
                    nc.scalar.activation(keyT[:, :, :], x_ps[:, 0:2, :], ACT.Copy).then_inc(S.slotsT, 1)
                    nc.scalar.activation(gateT[:, :], x_ps[:, 2, :], ACT.Copy).then_inc(S.slotsT, 1)
                for half in range(2):
                    wait(act, stored[half], t * 16)
                    for g in range(16):
                        act.wait_ge(S.place_ps, t * 32 + half * 16 + g + 1)
                        nc.scalar.activation(dense[half][:, :, g * 4:g * 4 + 4].rearrange("p i t -> p t i"),
                                             place_ps[:, g % 2, :, :], ACT.Copy).then_inc(S.placed, 1)
            queries(0)
            periods(act, choose, place)

        @block.vector
        def _(dve):
            own = Order(dve, S.dve)
            PER_TILE = 135
            dve.wait_ge(S.iota, 3)
            dve.wait_ge(S.keysT, 1)
            best4 = best[:, :, :].rearrange("p (h s) k -> p h s k", s=2)
            sums = work[:, 0:HEADS * SUMS].rearrange("p (h n) -> p h n", h=HEADS)
            work3 = work[:, :].rearrange("p (n k) -> p n k", n=HP)
            low, high = slice(0, 8), slice(8, 16)

            def two_lists(t):
                for n in range(HP):
                    if n % 4 == 0:
                        dve.wait_ge(S.scores, t * 4 + n // 4 + 1)
                        dve.sem_inc(S.passed, 1)
                    own.mark(nc.vector.max(best[:, n, low], s_ps[:, n, :]))
                own.settle()
                dve.sem_inc(S.passed, 1)
                for n in range(HP):
                    own.mark(nc.vector.max_index(best_at[:, n, low], best[:, n, low], s_ps[:, n, :]))
                    own.mark(nc.vector.match_replace(work3[:, n, :], best[:, n, low], s_ps[:, n, :], NEG))
                own.settle()
                nc.vector.memset(total[:, :], 0.0).then_inc(S.scores_used, 1)
                for n in range(HP):
                    own.mark(nc.vector.max(best[:, n, high], work3[:, n, :]))
                own.settle()
                dve.sem_inc(S.passed, 1)
                for n in range(HP):
                    own.mark(nc.vector.max_index(best_at[:, n, high], best[:, n, high], work3[:, n, :]))
                own.settle()
                wait(dve, S.keyed, t * 2)
                own.then(nc.vector.tensor_copy(best_key[:, :, :], best_at[:, :, :]))

            def best_pairs(t):
                first, second = best4[:, :, 0, :], best4[:, :, 1, :]
                for at, a, nb in ((slice(0, NW), slice(0, WIDE), TOPK), (slice(NW, SUMS), slice(WIDE, TOPK), 4)):
                    na = a.stop - a.start
                    own.mark(nc.vector.tensor_tensor(
                        sums[:, :, at].rearrange("p h (a b) -> p h a b", a=na),
                        first[:, :, a].rearrange("p h (a o) -> p h a o", o=1).to_broadcast([P, HEADS, na, nb]),
                        second[:, :, 0:nb].rearrange("p h (o b) -> p h o b", o=1).to_broadcast([P, HEADS, na, nb]),
                        ALU.add))
                own.settle()
                dve.sem_inc(S.passed, 1)
                for part in (low, high):
                    for h in range(HEADS):
                        own.mark(nc.vector.max(pair[:, h, part], sums[:, h]))
                    own.settle()
                    dve.sem_inc(S.passed, 1)
                    for h in range(HEADS):
                        own.mark(nc.vector.max_index(pair_at[:, h, part], pair[:, h, part], sums[:, h]))
                    own.settle()
                    dve.sem_inc(S.passed, 1)
                    if part is low:
                        for h in range(HEADS):
                            own.mark(nc.vector.match_replace(sums[:, h], pair[:, h, low], sums[:, h], NEG))
                        own.settle()
                        dve.sem_inc(S.passed, 1)

            def chosen_ranks(t):
                nc.vector.tensor_tensor(soft[:, :, :], pair[:, :, :],
                                        pair[:, :, 0:1].to_broadcast([P, HEADS, TOPK]), ALU.subtract)\
                    .then_inc(S.shifted, 1)
                for n, (op, by) in enumerate(((ALU.logical_shift_right, 4), (ALU.bitwise_and, 15),
                                              (ALU.logical_shift_right, 2), (ALU.bitwise_and, 3))):
                    own.mark(nc.vector.tensor_scalar(digits[:, n], pair_at[:, :, :], by, None, op))
                own.mark(nc.vector.tensor_scalar(narrow[:, :, :], pair_at[:, :, :], NW, None, ALU.is_ge))
                own.settle()
                own.then(nc.vector.tensor_tensor(ranks[:, :], digits[:, 2:4], digits[:, 0:2], ALU.subtract))
                own.then(nc.vector.tensor_tensor(
                    ranks[:, :], ranks[:, :], narrow[:, :, :].rearrange("p (o h) k -> p o h k", o=1)
                    .to_broadcast([P, 2, HEADS, TOPK]), ALU.mult))
                own.then(nc.vector.tensor_tensor(ranks[:, :], ranks[:, :], digits[:, 0:2], ALU.add))
                own.mark(nc.vector.scalar_tensor_tensor(
                    out=rank[:, 0], in0=narrow[:, :, :], scalar=-float(NW // 4 - WIDE), in1=ranks[:, 0],
                    op0=ALU.mult, op1=ALU.add))
                own.then(nc.vector.tensor_copy(rank[:, 1], ranks[:, 1]))
                for s in range(2):
                    nc.vector.tensor_tensor(
                        hit[:, s], rank[:, s].rearrange("p h (o k) -> p h o k", o=1)
                        .to_broadcast([P, HEADS, TOPK, TOPK]),
                        iota_rank[:, :, :].rearrange("p (o a) k -> p o a k", o=1)
                        .to_broadcast([P, HEADS, TOPK, TOPK]), ALU.is_equal).then_inc(S.ranked, 1)

            def choose(t, more):
                own.loop(t * PER_TILE)
                two_lists(t)
                best_pairs(t)
                chosen_ranks(t)
                if isinstance(t, int) and t == 0:
                    softmax(t)

            def softmax(t):
                dve.wait_ge(S.exp, t + 1)
                own.then(nc.vector.tensor_reduce(total[:, :], soft[:, :, :], AX.X, ALU.add))
                own.then(nc.vector.reciprocal(total[:, :], total[:, :]))
                nc.vector.tensor_tensor(slots[:, 2, :, :], soft[:, :, :],
                                        total[:, :].rearrange("p (h o) -> p h o", o=1)
                                        .to_broadcast([P, HEADS, TOPK]), ALU.mult).then_inc(S.gate_ready, 1)
                assert own.n == PER_TILE, own.n

            def place(t):
                dve.wait_ge(S.slotsT, t * 2 + 2)

                def right_rows(b):
                    if b >= 2:
                        wait_for_gated(dve, t, b - 2)
                    nc.vector.tensor_tensor(
                        right_hot[b % 2][:, :, :], keyT[:, 1, b * BATCH:(b + 1) * BATCH]
                        .rearrange("p (o t) -> p o t", o=1).to_broadcast([P, NKEYS, BATCH]),
                        iota_keys[:, :, :], ALU.is_equal).then_inc(S.right_hot, 1)

                right_rows(0)
                for b in range(BATCHES):
                    if b + 1 < BATCHES:
                        right_rows(b + 1)
                    wait_for_placed(dve, t, b, LEFTS)
                    nc.vector.tensor_tensor(
                        left[b % LEFTS][:, :, :], keyT[:, 0, b * BATCH:(b + 1) * BATCH]
                        .rearrange("p (t o) -> p t o", o=1).to_broadcast([P, BATCH, NKEYS]),
                        iota_key[:, :].rearrange("p (o i) -> p o i", o=1).to_broadcast([P, BATCH, NKEYS]),
                        ALU.is_equal).then_inc(S.left, 1)
                    if on_vector(b):
                        wait_for_placed(dve, t, b, 2)
                        dve.wait_ge(S.right_hot, t * BATCHES + b + 1)
                        gated(nc.vector, b).then_inc(S.gated_vector, 1)
                if not (isinstance(t, int) and t == TILES - 1):
                    softmax(t + 1)
            periods(dve, choose, place)

        @block.tensor
        def _(pe):
            pe.wait_ge(S.consts, 32)
            for n in range(HP):
                last = nc.tensor.transpose(s_ps[:, n, :], work[:, n * P:(n + 1) * P], ident[:, :])
            last.then_inc(S.keys_ps, 1)

            def queries(t):
                pe.wait_ge(S.h2, t * 16 + 16)

                def product(b):
                    if isinstance(t, int) and t == 0:
                        pe.wait_ge(wq_loaded[b], 16)
                    wait(pe, S.q, t * 4 + b)
                    for k in range(KD):
                        last = nc.tensor.matmul(q_ps[:, :], h2T[:, k, :], wq_sb[b][:, k, :],
                                                start=k == 0, stop=k == KD - 1)
                    last.then_inc(S.q_ps, 1)

                def turn(b):
                    pe.wait_ge(S.q, t * 4 + b + 1)
                    wait(pe, S.qT, t * 4 + b)
                    for n in range(4):
                        last = nc.tensor.transpose(x_ps[:, n, :], q[:, n, :], ident[:, :])
                    last.then_inc(S.qT_ps, 1)
                for b in range(4):
                    product(b)
                    turn(b)

            def scores(t):
                pe.wait_ge(S.qT, t * 4 + 4)
                wait(pe, S.scores_used, t)
                for n in range(HP):
                    last = nc.tensor.matmul(s_ps[:, n, :], qT[:, n, :], keysT[:, n, :], start=True, stop=True)
                    if n % 4 == 3:
                        last.then_inc(S.scores, 1)

            def turn_slots(t):
                pe.wait_ge(S.keyed, t * 2 + 2)
                pe.wait_ge(S.gate_ready, t + 1)
                for n in range(3):
                    last = nc.tensor.transpose(x_ps[:, n, :], slots[:, n, :, :].rearrange("p h k -> p (h k)"),
                                               ident[:, :])
                last.then_inc(S.slotsT_ps, 1)

            def choose(t, more):
                if more:
                    queries(t + 1)
                    pe.wait_ge(S.qT, t * 4 + 8)
                if not isinstance(t, int) or t > 0:
                    turn_slots(t - 1)
                if more:
                    scores(t + 1)

            def place(t):
                if isinstance(t, int) and t == TILES - 1:
                    turn_slots(t)
                for b in range(BATCHES):
                    n = t * BATCHES + b
                    pe.wait_ge(S.left, n + 1)
                    wait_for_gated(pe, t, b)
                    for g in range(2):
                        pe.wait_ge(S.placed, n * 2 + g + 1)
                        for j in range(4):
                            last = nc.tensor.matmul(place_ps[:, g, j, :], right[b % 2][:, g * 4 + j, :],
                                                    left[b % LEFTS][:, g * 4 + j, :], start=True, stop=True)
                        last.then_inc(S.place_ps, 1)
            pe.wait_ge(S.keysT, 1)
            queries(0)
            scores(0)
            periods(pe, choose, place)


def experts(nc, ctx, u_table, v_table, g_final, ident_in, mod_rows, x1_rows, h2T_tiles, gate_blocks, y_prompt,
            y_sample):
    S = sems(nc, ctx, "exp", "passed consts zero h0 h1 h2 h_hi h_lo u0 u1 gates vld uT_ps uT_hi uT_lo act_ps gelu "
                             "m m_hi m_lo v_hi v_lo y_ps y_free g_last gate2_0 gate2_1 x1_0 x1_1 x1_2 x1_3 weighted summed "
                             "sumsq mean rstd final stored")
    EXPERTS = NKEYS * NKEYS
    EB = EXPERTS // P
    PAIRS = EB // 2
    TOKENS = TILES * P
    GROUP = TOKENS // 3
    OUTPUTS = 2 * TILES
    with ExitStack() as mem:
        ff = sbuf(nc, mem, "ff", [P, TILES, D])
        ident = sbuf(nc, mem, "ident_d", [P, P])
        h_hi = sbuf(nc, mem, "h_hi", [P, KD, TOKENS], F32R)
        h_lo = sbuf(nc, mem, "h_lo", [P, KD, TOKENS], F32R)
        u = [sbuf(nc, mem, f"u_raw{s}", [P, D]) for s in range(2)]
        v = sbuf(nc, mem, "v_raw", [P, D])
        uT_hi = [sbuf(nc, mem, f"uT_hi{s}", [P, KD, P], F32R) for s in range(2)]
        uT_lo = [sbuf(nc, mem, f"uT_lo{s}", [P, KD, P], F32R) for s in range(2)]
        gates = sbuf(nc, mem, "gates", [P, BLOCKS, 2, BLOCK])
        g = sbuf(nc, mem, "g", [P, TOKENS])
        m_hi = [sbuf(nc, mem, f"m_hi{s}", [P, TOKENS], F32R) for s in range(3)]
        m_lo = [sbuf(nc, mem, f"m_lo{s}", [P, TOKENS], F32R) for s in range(3)]
        v_hi = [sbuf(nc, mem, f"v_hi{s}", [P, D], F32R) for s in range(3)]
        v_lo = [sbuf(nc, mem, f"v_lo{s}", [P, D], F32R) for s in range(3)]
        g_last = sbuf(nc, mem, "g_last", [P, D])
        power = sbuf(nc, mem, "power_d", [P, 1])
        sumsq = sbuf(nc, mem, "sumsq_d", [P, TILES])
        mean = sbuf(nc, mem, "mean_d", [P, TILES])
        rstd = sbuf(nc, mem, "rstd_d", [P, TILES])
        h_raw = [ff[:, t, :] for t in range(TILES)]
        h_loaded = [S.h0, S.h1, S.h2]
        gates_flat = gates[:, :, :, :].rearrange("p n i j -> p (n i j)")
        x1 = [u[0][:, :], u[1][:, :], gates_flat[:, 0:D], gates_flat[:, D:2 * D]]
        gate2 = [v[:, :], g[:, 0:D]]
        squares = uT_hi[1][:, :, :].rearrange("p k t -> p (k t)")
        uT_ps = psum(nc, mem, "uT_ps", [P, KD, P])
        a_ps = [psum(nc, mem, f"a_ps{n}", [P, HALF]) for n in range(3)]
        y_ps = [psum(nc, mem, f"y_ps{n}", [P, HALF]) for n in range(3)]
        block = mem.enter_context(nc.Block())

        def buffer(j, parity):
            return 2 if j else parity

        def pairs(eng, first, pair, last):
            first()
            with eng.Fori(0, PAIRS // 2 - 1) as i:
                pair(i * 2 + 1, 1)
                pair(i * 2 + 2, 0)
            last()

        @block.sync
        def _(sp):
            sp.dma_start(ident[:, :], ident_in).then_inc(S.consts, 16)
            sp.dma_start(u[0][:, :], u_table[0:P, :]).then_inc(S.u0, 16)
            for t in range(TILES):
                sp.dma_start(h_raw[t], h2T_tiles[t, :, :]).then_inc(h_loaded[t // 3], 16)
            sp.dma_start(g_last[:, :], g_final.partition_broadcast(P)).then_inc(S.g_last, 16)
            u_loaded = [S.u0, S.u1]

            def load_u(e, s):
                wait(sp, S.uT_ps, e)
                sp.dma_start(u[s][:, :], u_table[bass.ds(e * P, P), :]).then_inc(u_loaded[s], 16)

            def load_v(e):
                wait(sp, S.v_lo, e)
                sp.dma_start(v[:, :], v_table[bass.ds(e * P, P), :]).then_inc(S.vld, 16)

            def store(t):
                if t < PROMPT_TILES:
                    dst = y_prompt[0, t * P:(t + 1) * P, :]
                else:
                    dst = y_sample.rearrange("b t d -> (b t) d")
                sp.wait_ge(S.final, t + 1)
                sp.dma_start(dst, ff[:, t, :]).then_inc(S.stored, 16)

            def load(c, more=True):
                load_u(c * 2 + 1, 1)
                load_v(c * 2)
                if more:
                    load_u(c * 2 + 2, 0)
                load_v(c * 2 + 1)
            load(0)
            with sp.Fori(1, PAIRS - 1) as c:
                load(c)
            load(PAIRS - 1, more=False)

            def load_x1(t):
                sp.dma_start(x1[t % 4], x1_rows[t, :, :]).then_inc(x1_loaded[t % 4], 16)
            x1_loaded = [S.x1_0, S.x1_1, S.x1_2, S.x1_3]
            sp.wait_ge(S.uT_ps, EB + 1)
            load_x1(0)
            load_x1(1)
            sp.wait_ge(S.v_lo, EB)
            sp.dma_start(gate2[0], mod_rows[0, GATE2, :, :]).then_inc(S.gate2_0, 16)
            sp.wait_ge(S.m, EB * 3)
            load_x1(2)
            load_x1(3)
            sp.wait_ge(S.m_lo, EB * 3)
            sp.dma_start(gate2[1], mod_rows[1, GATE2, :, :]).then_inc(S.gate2_1, 16)
            for t in range(TILES):
                if t + 4 < TILES:
                    sp.wait_ge(S.summed, t + 1)
                    load_x1(t + 4)
                if t >= 2:
                    store(t - 2)
            store(TILES - 2)
            store(TILES - 1)
            sp.wait_ge(S.stored, TILES * 16)

        @block.gpsimd
        def _(pool):
            pool.memset(power[:, :], -0.5).then_inc(S.zero, 1)

            def split_v(c, parity, j):
                e = c * 2 + j
                pool.wait_ge(S.v_hi, e + 1)
                nc.gpsimd.tensor_tensor(v_lo[buffer(j, parity)][:, :], v[:, :],
                                        v_hi[buffer(j, parity)][:, :].bitcast(F32), ALU.subtract)\
                    .then_inc(S.v_lo, 1)

            def load_gates(c):
                pool.sem_inc(S.passed, 1)
                pool.dma_start(gates[:, :, :, :],
                               gate_blocks[:, :, bass.ds(c * 2, 2), :].rearrange("n p i j -> p n (i j)"))\
                    .then_inc(S.gates, 16)

            def pair(c, parity, more=True):
                split_v(c, parity, 0)
                split_v(c, parity, 1)
                if more:
                    pool.wait_ge(S.m, c * 6 + 6)
                    load_gates(c + 1)
            load_gates(0)
            pool.wait_ge(S.h_lo, TILES)
            pool.memset(ff[:, :, :], 0.0).then_inc(S.zero, 1)
            pairs(pool, lambda: pair(0, 0), pair, lambda: pair(PAIRS - 1, 1, more=False))

            pool.wait_ge(S.gate2_0, 16)
            pool.wait_ge(S.gate2_1, 16)
            pool.wait_ge(S.zero, 2)
            for t in range(TILES + 1):
                if t < TILES:
                    pool.wait_ge(S.y_free, 3 + (PAIRS - 1) * OUTPUTS + t * 2 + 2)
                    pool.tensor_tensor(ff[:, t, :], ff[:, t, :], gate2[int(t == TILES - 1)], ALU.mult)\
                        .then_inc(S.weighted, 1)
                if t:
                    pool.wait_ge(S.mean, t)
                    pool.tensor_tensor(rstd[:, t - 1:t], mean[:, t - 1:t], power[:, :], ALU.pow).then_inc(S.rstd, 1)

        @block.scalar
        def _(act):
            def split_h(n):
                act.wait_ge(h_loaded[n], 48)
                for t in range(n * 3, n * 3 + 3):
                    nc.scalar.activation(h_hi[:, :, t * P:(t + 1) * P], h_raw[t].rearrange("p (k t) -> p k t", k=KD),
                                         ACT.Copy).then_inc(S.h_hi, 1)

            def uT(e, s):
                act.wait_ge(S.uT_ps, e + 2)
                wait(act, S.act_ps, e * 3 - 3)
                for n in range(2):
                    nc.scalar.activation(uT_hi[s][:, n * 4:n * 4 + 4, :], uT_ps[:, n * 4:n * 4 + 4, :], ACT.Copy)\
                        .then_inc(S.uT_hi, 1)

            def split_v(c, parity, j):
                e = c * 2 + j
                act.wait_ge(S.vld, e * 16 + 16)
                if j:
                    wait(act, S.y_ps, c * OUTPUTS)
                nc.scalar.activation(v_hi[buffer(j, parity)][:, :], v[:, :], ACT.Copy).then_inc(S.v_hi, 1)

            def weigh(c, parity, j):
                e = c * 2 + j
                wait(act, S.m_lo, e * 3)
                for n in range(3):
                    act.wait_ge(S.act_ps, e * 3 + n + 1)
                    nc.scalar.activation(g[:, n * GROUP:(n + 1) * GROUP], a_ps[n][:, 0:GROUP], ACT.Gelu)\
                        .then_inc(S.gelu, 1)
                act.wait_ge(S.m, e * 3 + 3)
                nc.scalar.activation(m_hi[buffer(j, parity)][:, :], g[:, :], ACT.Copy).then_inc(S.m_hi, 1)

            def pair(c, parity, more=True):
                uT(c * 2 + 1, 1)
                split_v(c, parity, 0)
                weigh(c, parity, 0)
                if more:
                    uT(c * 2 + 2, 0)
                split_v(c, parity, 1)
                weigh(c, parity, 1)
            act.wait_ge(S.uT_ps, 2)
            for n in range(2):
                nc.scalar.activation(uT_hi[0][:, n * 4:n * 4 + 4, :], uT_ps[:, n * 4:n * 4 + 4, :], ACT.Copy)\
                    .then_inc(S.uT_hi, 1)
            for n in range(3):
                split_h(n)
            pairs(act, lambda: pair(0, 0), pair, lambda: pair(PAIRS - 1, 1, more=False))

            for t in range(TILES):
                act.wait_ge(S.summed, t + 1)
                if t:
                    act.wait_ge(S.mean, t)
                nc.scalar.activation(squares, ff[:, t, :], ACT.Square, accum_out=sumsq[:, t:t + 1]).then_inc(S.sumsq, 1)

        @block.vector
        def _(dve):
            dve.sem_inc(S.y_free, 3)

            def uT(e, s):
                for n in range(2):
                    dve.wait_ge(S.uT_hi, e * 2 + n + 1)
                    part = slice(n * 4, n * 4 + 4)
                    nc.vector.tensor_tensor(uT_lo[s][:, part, :], uT_ps[:, part, :], uT_hi[s][:, part, :].bitcast(F32),
                                            ALU.subtract).then_inc(S.uT_lo, 1)

            def weigh(c, j, n):
                dve.wait_ge(S.gelu, (c * 2 + j) * 3 + n + 1)
                dve.wait_ge(S.gates, c * 16 + 16)
                part = g[:, n * GROUP:(n + 1) * GROUP].rearrange("p (n j) -> p n j", j=BLOCK)
                per = GROUP // BLOCK
                nc.vector.tensor_tensor(part, part, gates[:, n * per:(n + 1) * per, j, :], ALU.mult).then_inc(S.m, 1)

            def rest(c, j, parity, n):
                b = buffer(j, parity)
                dve.wait_ge(S.m_hi, c * 2 + j + 1)
                part = slice(n * GROUP, (n + 1) * GROUP)
                nc.vector.tensor_tensor(m_lo[b][:, part], g[:, part], m_hi[b][:, part].bitcast(F32), ALU.subtract)\
                    .then_inc(S.m_lo, 1)

            def collect(c, between):
                for n in range(OUTPUTS):
                    dve.wait_ge(S.y_ps, c * OUTPUTS + n + 1)
                    part = ff[:, n // 2, (n % 2) * HALF:(n % 2 + 1) * HALF]
                    nc.vector.tensor_tensor(part, part, y_ps[n % 3][:, :], ALU.add).then_inc(S.y_free, 1)
                    if n in between:
                        between[n]()

            def pair(c, parity, more=True, before=True):
                uT(c * 2 + 1, 1)
                steps = {}
                for n in range(3):
                    steps[1 + n] = lambda n=n: weigh(c, 0, n)
                    steps[7 + n] = lambda n=n: rest(c, 0, parity, n)
                if before:
                    collect(c - 1, steps)
                else:
                    for n in sorted(steps):
                        steps[n]()
                if more:
                    uT(c * 2 + 2, 0)
                for n in range(3):
                    weigh(c, 1, n)
                for n in range(3):
                    rest(c, 1, parity, n)
            uT(0, 0)
            for t in range(TILES):
                dve.wait_ge(S.h_hi, t + 1)
                tok = slice(t * P, (t + 1) * P)
                nc.vector.tensor_tensor(h_lo[:, :, tok], h_raw[t].rearrange("p (k t) -> p k t", k=KD),
                                        h_hi[:, :, tok].bitcast(F32), ALU.subtract).then_inc(S.h_lo, 1)

            def first_pair():
                pair(0, 0, before=False)
                dve.wait_ge(S.zero, 2)
            pairs(dve, first_pair, pair, lambda: pair(PAIRS - 1, 1, more=False))

            def add_x1(t):
                dve.wait_ge(S.weighted, t + 1)
                dve.wait_ge((S.x1_0, S.x1_1, S.x1_2, S.x1_3)[t % 4], t // 4 * 16 + 16)
                nc.vector.tensor_tensor(ff[:, t, :], ff[:, t, :], x1[t % 4], ALU.add).then_inc(S.summed, 1)

            def mean_of(t):
                dve.wait_ge(S.sumsq, t + 1)
                nc.vector.tensor_scalar(mean[:, t:t + 1], sumsq[:, t:t + 1], 1.0 / D, EPS, ALU.mult, ALU.add)\
                    .then_inc(S.mean, 1)

            def normed(t):
                if t == 0:
                    dve.wait_ge(S.g_last, 16)
                dve.wait_ge(S.rstd, t + 1)
                nc.vector.scalar_tensor_tensor(out=ff[:, t, :], in0=ff[:, t, :], scalar=rstd[:, t:t + 1], in1=g_last[:, :],
                                               op0=ALU.mult, op1=ALU.mult).then_inc(S.final, 1)

            def finish(t):
                if 1 <= t <= TILES:
                    add_x1(t - 1)
                if 2 <= t <= TILES + 1:
                    mean_of(t - 2)
                if 3 <= t:
                    normed(t - 3)
            collect(PAIRS - 1, {t * 2 + 1: lambda t=t: finish(t) for t in range(TILES)})
            for t in range(TILES, TILES + 3):
                finish(t)

        @block.tensor
        def _(pe):
            pe.sem_inc(S.uT_ps, 1)
            pe.wait_ge(S.consts, 16)
            u_loaded = [S.u0, S.u1]

            def transpose_u(e, c, s):
                pe.wait_ge(u_loaded[s], c * 16 + 16)
                wait(pe, S.uT_lo, e * 2)
                for k in range(KD):
                    last = nc.tensor.transpose(uT_ps[:, k, :], u[s][:, k * P:(k + 1) * P], ident[:, :])
                last.then_inc(S.uT_ps, 1)

            def first_product(e, s):
                pe.wait_ge(S.uT_lo, e * 2 + 2)
                for n in range(3):
                    if isinstance(e, int) and e == 0:
                        pe.wait_ge(S.h_lo, n * 3 + 3)
                    wait(pe, S.gelu, e * 3 - 2 + n)
                    tok = slice(n * GROUP, (n + 1) * GROUP)
                    for k in range(KD):
                        for m, (lhs, rhs) in enumerate(((uT_lo, h_hi), (uT_hi, h_lo), (uT_hi, h_hi))):
                            last = nc.tensor.matmul(a_ps[n][:, 0:GROUP], lhs[s][:, k, :], rhs[:, k, tok],
                                                    start=k == 0 and m == 0, stop=k == KD - 1 and m == 2)
                    last.then_inc(S.act_ps, 1)

            def second_product(c, parity):
                pe.wait_ge(S.m_lo, c * 6 + 6)
                pe.wait_ge(S.v_lo, c * 2 + 2)
                for n in range(OUTPUTS):
                    tok = slice(n // 2 * P, (n // 2 + 1) * P)
                    col = slice((n % 2) * HALF, (n % 2 + 1) * HALF)
                    pe.wait_ge(S.y_free, c * OUTPUTS + n + 1)
                    for j in range(2):
                        b = buffer(j, parity)
                        for m, (lhs, rhs) in enumerate(((m_lo, v_hi), (m_hi, v_lo), (m_hi, v_hi))):
                            last = nc.tensor.matmul(y_ps[n % 3][:, :], lhs[b][:, tok], rhs[b][:, col],
                                                    start=j == 0 and m == 0, stop=j == 1 and m == 2)
                    last.then_inc(S.y_ps, 1)

            def pair(c, parity, more=True, before=True):
                transpose_u(c * 2 + 1, c, 1)
                first_product(c * 2, 0)
                if before:
                    second_product(c - 1, 1 - parity)
                if more:
                    transpose_u(c * 2 + 2, c + 1, 0)
                first_product(c * 2 + 1, 1)
            transpose_u(0, 0, 0)
            pairs(pe, lambda: pair(0, 0, before=False), pair, lambda: pair(PAIRS - 1, 1, more=False))
            second_product(PAIRS - 1, 1)


def program(nc, a, outs):
    y_prompt, y_sample, pool_prompt_out, pool_sample_out, v_sample_out = outs
    with ExitStack() as ctx:
        mod_rows = nc.dram_tensor("mod_rows", (2, MODS, P, D), F32, kind="Internal").ap()
        x1_rows = nc.dram_tensor("x1_rows", (TILES, P, D), F32, kind="Internal").ap()
        h2T_tiles = nc.dram_tensor("h2T_tiles", (TILES, P, D), F32, kind="Internal").ap()
        gate_blocks = nc.dram_tensor("gate_blocks", (BLOCKS, P, NKEYS, BLOCK), F32, kind="Internal").ap()
        with nc.sbuf_tensor("w_in_sb", [P, KD, ZW], F32) as w_in_sb:
            modulation(nc, ctx, a["c_prompt"], a["c_sample"], a["w_ada"][0], a["b_ada"][0], a["g_norm1"][0],
                       a["g_norm2"][0], a["selector"], a["identity"], a["w_in"][0], w_in_sb, mod_rows)
            mixing(nc, ctx, a["x_prompt"], a["x_sample"], a["cache_pool"], w_in_sb, a["pool_w"][0],
                   a["pool_scale"][0], a["gmlp_norm_g"][0], a["gmlp_ws"][0], a["gmlp_bs"][0], a["w_out"][0],
                   a["identity"], a["bands"], mod_rows, x1_rows, h2T_tiles, pool_prompt_out, pool_sample_out,
                   v_sample_out)
        routing(nc, ctx, a["peer_wq"][0], a["peer_keys"][0], a["identity"], h2T_tiles, gate_blocks)
        experts(nc, ctx, a["peer_u"][0], a["peer_v"][0], a["g_final"], a["identity"], mod_rows, x1_rows, h2T_tiles,
                gate_blocks, y_prompt, y_sample)


_INS = ['x_prompt', 'x_sample', 'cache_pool', 'c_prompt', 'c_sample', 'w_ada', 'b_ada', 'g_norm1', 'w_in', 'pool_w',
        'pool_scale', 'gmlp_norm_g', 'gmlp_ws', 'gmlp_bs', 'w_out', 'g_norm2', 'peer_wq', 'peer_keys', 'peer_u',
        'peer_v', 'g_final']
_OUTS = [(1, 1024, 1024), (8, 16, 1024), (1, 1, 15, 512), (1, 8, 15, 512), (1, 8, 16, 512)]


def _constants():
    import numpy as np
    selector = np.zeros((1 + STREAMS, 2, P), np.float32)
    selector[0, 0, :] = 1
    for t in range(P):
        selector[1 + t // STEP, 1, t] = 1
    bands = np.zeros((P, 5, GROUPS, P), np.float32)
    for g in range(GROUPS):
        w = 2 << g
        for t in range(P):
            for j in range(P):
                back = t - j
                if 0 <= back < w:
                    bands[j, 0, g, t] = 1 / min(t + 1, w)
                    bands[j, 1, g, t] = 1 / w
                    if j // STEP == t // STEP:
                        bands[j, 2, g, t] = 1 / w
                if back + P < w:
                    bands[j, 3, g, t] = 1 / w
                if j < STREAMS * HIST and j // HIST == t // STEP and t % STEP - (j % HIST - HIST) < w:
                    bands[j, 4, g, t] = 1 / w
            bands[t, 0:3, g, t] -= 1
    return {"identity": np.eye(P, dtype=np.float32), "selector": selector, "bands": bands}


def kernel(**inputs):
    import numpy as _np
    import concourse.bacc as _bacc
    from concourse.bass_utils import run_bass_kernel_spmd as _run

    nc = _bacc.Bacc("TRN2", target_bir_lowering=False, num_devices=1)
    arrays, args = {}, {}
    given = {name: _np.ascontiguousarray(inputs[name]) for name in _INS}
    given.update(_constants())
    for name, a in given.items():
        arrays[f"in_{name}"] = a
        args[name] = nc.dram_tensor(f"in_{name}", a.shape, F32, kind="ExternalInput").ap()
    outs = [nc.dram_tensor(f"out_{i}", shape, F32, kind="ExternalOutput").ap() for i, shape in enumerate(_OUTS)]
    program(nc, args, outs)
    r = _run(nc, [arrays], core_ids=[0])
    return tuple(r.results[0][f"out_{i}"] for i in range(len(_OUTS)))
```

```python
import concourse.bass as bass
from concourse import mybir
from contextlib import ExitStack

F32 = mybir.dt.float32
F32R = mybir.dt.float32r
BF16 = mybir.dt.bfloat16
U32 = mybir.dt.uint32
ALU = mybir.AluOpType
ACT = mybir.ActivationFunctionType
AX = mybir.AxisListType

P = 128
D = 1024
KD = D // P
HALF = 512
PROMPT_TILES = 8
TILES = 9
STREAMS, STEP = 8, 16
HIST = 15
ZW = 1536
GROUPS = 4
HEADS = 8
TOPK = 16
NKEYS = 128
BLOCK = 64
BLOCKS = TILES * P // BLOCK
BATCH = 8
NEG = -3.0e38
EPS = 1e-6
MODS = 6
SHIFT1, SCALE1, GATE1, SHIFT2, SCALE2, GATE2 = range(MODS)
SHARED = KD * ZW
WQ_SHARED = SHARED // (KD * HALF)


class Order:

    def __init__(self, eng, sem):
        self.eng, self.sem, self.base, self.n = eng, sem, 0, 0

    def loop(self, base):
        self.base, self.n = base, 0

    def mark(self, ins):
        ins.then_inc(self.sem, 1)
        self.n += 1

    def settle(self):
        self.eng.wait_ge(self.sem, self.base + self.n)

    def then(self, ins):
        self.mark(ins)
        self.settle()


def sems(nc, ctx, stage, names):
    made = {n: ctx.enter_context(nc.semaphore(f"{stage}_{n}")) for n in names.split()}
    return type("Sems", (), made)


def input_weights(shared):
    return shared[:, :].rearrange("p (k n) -> p k n", k=KD)


def query_weights(shared, b):
    return shared[:, b * KD * HALF:(b + 1) * KD * HALF].rearrange("p (k n) -> p k n", k=KD)


def expert_memory(shared):
    ff = shared[:, 0:TILES * D].rearrange("p (t d) -> p t d", t=TILES)
    u0, u1, v = (shared[:, (TILES + n) * D:(TILES + n + 1) * D] for n in range(3))
    return ff, [u0, u1], v


def wait(eng, sem, value):
    if not isinstance(value, int) or value > 0:
        eng.wait_ge(sem, value)


def sbuf(nc, ctx, name, shape, dtype=F32):
    return ctx.enter_context(nc.sbuf_tensor(name, shape, dtype))


def psum(nc, ctx, name, shape, dtype=F32):
    return ctx.enter_context(nc.psum_tensor(name, shape, dtype))


def modulation(nc, ctx, c_prompt, c_sample, w_ada, b_ada, g1, g2, ident_in, w_in, shared, mod_rows):
    S = sems(nc, ctx, "mod", "c_in ident bias norm_g silu cT_ps cT w0 w1 w2 rows_ps rows scaled stored w_in")
    NC = 1 + STREAMS
    CHUNKS = MODS * D // HALF
    w_in_sb = input_weights(shared)
    with ExitStack() as mem:
        c_rows = sbuf(nc, mem, "c_rows", [NC, D])
        c_silu = sbuf(nc, mem, "c_silu", [NC, D])
        cT = sbuf(nc, mem, "cT", [P, KD, 16])
        ident = sbuf(nc, mem, "ident_a", [P, P])
        bias = sbuf(nc, mem, "bias", [NC, MODS * D])
        norm_g = sbuf(nc, mem, "norm_g", [NC, 2, D])
        w = [sbuf(nc, mem, f"w_ada{s}", [P, KD, HALF]) for s in range(3)]
        rows = sbuf(nc, mem, "mod_rows_sb", [NC, MODS, D])
        cT_ps = psum(nc, mem, "cT_ps", [P, KD, 16])
        rows_ps = [psum(nc, mem, f"rows_ps{s}", [NC, HALF]) for s in range(2)]
        w_loaded = [S.w0, S.w1, S.w2]
        w_view = w_ada.rearrange("(k p) n -> p k n", p=P)
        block = mem.enter_context(nc.Block())

        @block.sync
        def _(sp):
            sp.dma_start(c_rows[0:1, :], c_prompt).then_inc(S.c_in, 16)
            sp.dma_start(c_rows[1:NC, :], c_sample).then_inc(S.c_in, 16)
            sp.dma_start(ident[:, :], ident_in).then_inc(S.ident, 16)
            for c in range(CHUNKS):
                if c >= 3:
                    sp.wait_ge(S.rows_ps, c - 2)
                sp.dma_start(w[c % 3][:, :, :], w_view[:, :, c * HALF:(c + 1) * HALF]).then_inc(w_loaded[c % 3], 16)
                if c == 0:
                    sp.dma_start(bias[:, :], b_ada.partition_broadcast(NC)).then_inc(S.bias, 16)
                    sp.dma_start(norm_g[:, 0, :], g1.partition_broadcast(NC)).then_inc(S.norm_g, 16)
                    sp.dma_start(norm_g[:, 1, :], g2.partition_broadcast(NC)).then_inc(S.norm_g, 16)
                if c >= CHUNKS - KD:
                    k = c - (CHUNKS - KD)
                    sp.dma_start(w_in_sb[:, k, :], w_in[k * P:(k + 1) * P, :]).then_inc(S.w_in, 16)
            sp.wait_ge(S.w_in, 16 * KD)

        @block.scalar
        def _(act):
            act.wait_ge(S.c_in, 32)
            nc.scalar.activation(c_silu[:, :], c_rows[:, :], ACT.Silu).then_inc(S.silu, 1)
            for m in range(MODS):
                if m in (SCALE1, SCALE2):
                    act.wait_ge(S.scaled, 2 * (m // 3) + 2)
                else:
                    act.wait_ge(S.rows, 2 * m + 2)
                act.dma_start(mod_rows[:, m, :], rows[:, m, :]).then_inc(S.stored, 16)
            act.wait_ge(S.stored, 16 * MODS)

        @block.vector
        def _(dve):
            dve.wait_ge(S.cT_ps, 1)
            nc.vector.tensor_copy(cT[:, :, 0:NC], cT_ps[:, :, 0:NC]).then_inc(S.cT, 1)
            dve.wait_ge(S.bias, 16)
            dve.wait_ge(S.norm_g, 32)
            for c in range(CHUNKS):
                m, half = c // 2, slice(c % 2 * HALF, (c % 2 + 1) * HALF)
                dve.wait_ge(S.rows_ps, c + 1)
                nc.vector.tensor_tensor(rows[:, m, half], rows_ps[c % 2][:, :], bias[:, c * HALF:(c + 1) * HALF],
                                        ALU.add).then_inc(S.rows, 1)
                if m in (SCALE1, SCALE2):
                    dve.wait_ge(S.rows, c + 1)
                    nc.vector.scalar_tensor_tensor(out=rows[:, m, half], in0=rows[:, m, half], scalar=1.0,
                                                   in1=norm_g[:, m // 3, half], op0=ALU.add, op1=ALU.mult)\
                        .then_inc(S.scaled, 1)

        @block.tensor
        def _(pe):
            pe.wait_ge(S.ident, 16)
            pe.wait_ge(S.silu, 1)
            for k in range(KD):
                last = nc.tensor.transpose(cT_ps[:, k, 0:NC], c_silu[:, k * P:(k + 1) * P], ident[0:NC, 0:NC])
            last.then_inc(S.cT_ps, 1)
            pe.wait_ge(S.cT, 1)
            for c in range(CHUNKS):
                pe.wait_ge(w_loaded[c % 3], (c // 3 + 1) * 16)
                if c >= 2:
                    pe.wait_ge(S.rows, c - 1)
                for k in range(KD):
                    last = nc.tensor.matmul(rows_ps[c % 2][:, :], cT[:, k, 0:NC], w[c % 3][:, k, :],
                                            start=k == 0, stop=k == KD - 1)
                last.then_inc(S.rows_ps, 1)


class Tile:

    def __init__(self, j, offset=0):
        self.j, self.offset = j, offset
        self.n = j * 2 + offset
        self.half = j + offset // 2
        self.s = offset % 2
        known = isinstance(j, int)
        self.first = known and self.n == 0
        self.last = self.sample = known and self.n == TILES - 1

    def after(self, k):
        return Tile(self.j, self.offset + k)


def mixing(nc, ctx, x_prompt, x_sample, cache_pool, pool_w, pool_scale, gmlp_g, gmlp_ws, gmlp_bs, w_out, wq,
           ident_in, bands_in, shared, mod_rows, x1_rows, h2T_tiles, pool_prompt_out, pool_sample_out, v_sample_out):
    S = sems(nc, ctx, "mix", "passed consts early mods_in mods_sample w_out_in x0 x1 r0 r1 ws_ps ws_sb wm bs_rep zero "
                             "sumsq mean rstd h_scaled h hT_ps hT z_ps zp zu zv v_squared v_summed vmean vrstd "
                             "v_scaled vn diff diffT pool pool_mixed gmlp_ps s_biased gmlp_mixed mix mix_read "
                             "x1_ready sumsq2 mean2 rstd2 h2_scaled h2 h2T_ps h2T x1_out0 x1_out1 h2T_out outs wq")
    x_loaded, r_loaded = [S.x0, S.x1], [S.r0, S.r1]
    w_in_sb = input_weights(shared)
    x1_stored = [S.x1_out0, S.x1_out1]
    with ExitStack() as mem:
        w_out_sb = sbuf(nc, mem, "w_out_sb", [P, KD, D])
        mods = sbuf(nc, mem, "mods", [P, 2, 5, D])
        ident = sbuf(nc, mem, "ident_b", [P, P])
        bands = sbuf(nc, mem, "bands", [P, 5, GROUPS, P])
        BAND_FIRST, BAND_NEXT, BAND_SAMPLE, BAND_BEFORE, BAND_HIST = range(5)
        hist = sbuf(nc, mem, "hist", [STREAMS * HIST, HALF])
        pool_w_sb = sbuf(nc, mem, "pool_w_sb", [P, GROUPS, P])
        pool_scale_sb = sbuf(nc, mem, "pool_scale_sb", [P, GROUPS])
        gmlp_g_sb = sbuf(nc, mem, "gmlp_g_sb", [P, HALF])
        ws = sbuf(nc, mem, "ws", [P, 2, GROUPS, P])
        wmT = sbuf(nc, mem, "wmT", [P, 2, GROUPS, P])
        bs = sbuf(nc, mem, "bs", [P, 2, GROUPS, P])
        power = sbuf(nc, mem, "power", [P, GROUPS])
        x = [sbuf(nc, mem, f"x_in{s}", [P, D]) for s in range(2)]
        squares = sbuf(nc, mem, "squares", [P, D], BF16)
        squares2 = sbuf(nc, mem, "squares2", [P, D], BF16)
        sumsq = sbuf(nc, mem, "sumsq", [P, 1])
        mean = sbuf(nc, mem, "mean", [P, 1])
        rstd = sbuf(nc, mem, "rstd", [P, 1])
        sumsq2 = sbuf(nc, mem, "sumsq2", [P, 1])
        mean2 = sbuf(nc, mem, "mean2", [P, 1])
        rstd2 = sbuf(nc, mem, "rstd2", [P, 1])
        h = sbuf(nc, mem, "h", [P, D])
        hT = sbuf(nc, mem, "hT", [P, KD, P])
        p = [sbuf(nc, mem, f"p{s}", [P, HALF]) for s in range(2)]
        uT = sbuf(nc, mem, "uT", [P, GROUPS, P])
        v = sbuf(nc, mem, "v", [P, GROUPS, P])
        vsq = sbuf(nc, mem, "vsq", [P, GROUPS, P])
        vsum = sbuf(nc, mem, "vsum", [P, GROUPS])
        vrstd = sbuf(nc, mem, "vrstd", [P, GROUPS])
        sT = sbuf(nc, mem, "sT", [P, GROUPS, P])
        diffT = sbuf(nc, mem, "diffT", [P, GROUPS, P])
        mixT = sbuf(nc, mem, "mixT", [P, KD, P])
        x1 = [sbuf(nc, mem, f"x1_in{s}", [P, D]) for s in range(2)]
        gated = sbuf(nc, mem, "gated_mix", [P, D])
        h2 = sbuf(nc, mem, "h2", [P, D])
        h2T = sbuf(nc, mem, "h2T_b", [P, KD, P])
        t_ps = psum(nc, mem, "t_ps", [P, KD, P])
        z_ps = psum(nc, mem, "z_ps", [P, 3, HALF])
        mix_ps = psum(nc, mem, "mix_ps", [P, 2, HALF])
        diff_ps = psum(nc, mem, "diff_ps", [P, GROUPS, P])
        sT_ps = mix_ps[:, 0, :].rearrange("p (g t) -> p g t", g=GROUPS)
        pool_ps = mix_ps[:, 1, :].rearrange("p (g t) -> p g t", g=GROUPS)
        EARLY = 16 * (2 + STREAMS)
        CONSTS = 16 * 6
        block = mem.enter_context(nc.Block())

        def periods(eng, period):
            period(Tile(0, 0))
            period(Tile(0, 1))
            with eng.Fori(1, 3) as j:
                period(Tile(j, 0))
                period(Tile(j, 1))
            for t in range(6, TILES):
                period(Tile(3, t - 6))

        @block.sync
        def _(sp):
            def src(t):
                if t.sample:
                    return x_sample.rearrange("b t d -> (b t) d")
                return x_prompt[0, bass.ds(t.n * P, P), :]

            def load_x(t):
                wait(sp, S.h, t.n - 1)
                sp.dma_start(x[t.s][:, :], src(t)).then_inc(x_loaded[t.s], 16)

            def load_residual(t):
                wait(sp, x1_stored[t.s], t.half * 16)
                sp.dma_start(x1[t.s][:, :], src(t)).then_inc(r_loaded[t.s], 16)

            sp.dma_start(x[0][:, :], src(Tile(0))).then_inc(x_loaded[0], 16)
            sp.dma_start(mods[:, 0, 0:2, :].rearrange("p m n -> p (m n)"),
                         mod_rows[0, 0:2, :].rearrange("m n -> (m n)").partition_broadcast(P)).then_inc(S.mods_in, 16)
            sp.dma_start(ident[:, :], ident_in).then_inc(S.early, 16)
            sp.dma_start(ws[:, 0, :, :], gmlp_ws.rearrange("h i j -> i h j")).then_inc(S.early, 16)
            sp.wait_ge(S.zero, 1)
            for b in range(STREAMS):
                span = slice(b * STEP, (b + 1) * STEP)
                sp.dma_start(ws[span, 1, :, span], gmlp_ws[:, 0:STEP, 0:STEP].rearrange("h i j -> i h j"))\
                    .then_inc(S.early, 16)
            sp.dma_start(x[1][:, :], src(Tile(0, 1))).then_inc(x_loaded[1], 16)
            c = S.consts
            sp.dma_start(bs[:, 0, :, :].rearrange("p h i -> p (h i)"),
                         gmlp_bs.rearrange("h i -> (h i)").partition_broadcast(P)).then_inc(c, 16)
            sp.dma_start(gmlp_g_sb[:, :], gmlp_g.partition_broadcast(P)).then_inc(c, 16)
            sp.dma_start(pool_w_sb[:, :, :], pool_w.rearrange("g c d -> c g d")).then_inc(c, 16)
            sp.dma_start(pool_scale_sb[:, :], pool_scale.rearrange("(g c) -> c g", g=GROUPS),
                         allow_slow_non_contiguous=True).then_inc(c, 16)
            sp.dma_start(bands[:, :, :, :], bands_in).then_inc(c, 16)
            sp.dma_start(hist[:, :], cache_pool.rearrange("l b r c -> (l b r) c")).then_inc(c, 16)
            sp.dma_start(w_out_sb[:, :, :], w_out.rearrange("(k p) n -> p k n", p=P)).then_inc(S.w_out_in, 16)
            sp.dma_start(mods[:, 0, 2:5, :].rearrange("p m n -> p (m n)"),
                         mod_rows[0, 2:5, :].rearrange("m n -> (m n)").partition_broadcast(P)).then_inc(S.w_out_in, 16)
            sp.dma_start(x1[0][:, :], src(Tile(0))).then_inc(r_loaded[0], 16)
            sp.dma_start(x1[1][:, :], src(Tile(0, 1))).then_inc(r_loaded[1], 16)
            for b in range(STREAMS):
                sp.dma_start(mods[b * STEP:(b + 1) * STEP, 1, :, :].rearrange("p m n -> p (m n)"),
                             mod_rows[1 + b, 0:5, :].rearrange("m n -> (m n)").partition_broadcast(STEP))\
                    .then_inc(S.mods_sample, 16)

            def period(t):
                if not (t.last or t.after(1).last):
                    load_x(t.after(2))
                if not (t.first or t.last):
                    load_residual(t.after(1))
            periods(sp, period)
            sp.wait_ge(S.zp, TILES)
            sp.dma_start(pool_prompt_out[0, 0, :, :], p[1][P - HIST:P, :]).then_inc(S.outs, 16)
            for b in range(STREAMS):
                sp.dma_start(pool_sample_out[0, b, :, :], p[0][b * STEP + 1:(b + 1) * STEP, :]).then_inc(S.outs, 16)
            sp.wait_ge(S.z_ps, TILES * 3)
            for b in range(WQ_SHARED):
                sp.dma_start(query_weights(shared, b),
                             wq[:, b * HALF:(b + 1) * HALF].rearrange("(k p) n -> p k n", p=P)).then_inc(S.wq, 16)
            sp.wait_ge(S.vn, TILES)
            sp.dma_start(v_sample_out.rearrange("l b t c -> (l b t) c"), v[:, :, :].rearrange("p g c -> p (g c)"))\
                .then_inc(S.outs, 16)
            sp.wait_ge(S.wq, WQ_SHARED * 16)
            sp.wait_ge(S.outs, (STREAMS + 2) * 16)

        @block.gpsimd
        def _(pool):
            pool.memset(ws[:, 1, :, :], 0.0).then_inc(S.zero, 1)
            pool.memset(power[:, :], -0.5).then_inc(S.zero, 1)
            pool.wait_ge(S.zero, 2)

            def root(t):
                pool.wait_ge(S.mean, t.n + 1)
                pool.tensor_tensor(rstd[:, :], mean[:, :], power[:, 0:1], ALU.pow).then_inc(S.rstd, 1)

            def head_roots(t):
                pool.wait_ge(S.vmean, t.n + 1)
                pool.tensor_tensor(vrstd[:, :], vsum[:, :], power[:, :], ALU.pow).then_inc(S.vrstd, 1)

            def store_x1(t):
                pool.wait_ge(S.h2, t.n + 1)
                pool.sem_inc(S.passed, 1)
                pool.dma_start(x1_rows[bass.ds(t.n, 1), :, :].rearrange("a p d -> p (a d)"), x1[t.s][:, :])\
                    .then_inc(x1_stored[t.s], 16)

            def root_x1(t):
                pool.wait_ge(S.mean2, t.n + 1)
                pool.tensor_tensor(rstd2[:, :], mean2[:, :], power[:, 0:1], ALU.pow).then_inc(S.rstd2, 1)

            def store_h2T(t):
                pool.wait_ge(S.h2T, t.n * 2 + 2)
                pool.sem_inc(S.passed, 1)
                pool.dma_start(h2T_tiles[bass.ds(t.n, 1), :, :].rearrange("a p d -> p (a d)"),
                               h2T[:, :, :].rearrange("p k t -> p (k t)")).then_inc(S.h2T_out, 16)

            def period(t):
                if not t.first:
                    root_x1(t.after(-1))
                if not (t.last or t.after(1).last):
                    root(t.after(2))
                if not t.first:
                    store_x1(t.after(-1))
                    store_h2T(t.after(-1))
                if not t.last:
                    head_roots(t.after(1))

            root(Tile(0))
            pool.wait_ge(S.ws_sb, 2)
            pool.affine_select(out=wmT[:, :, :, :], in_=wmT[:, :, :, :], compare_op=ALU.is_ge, fill=0.0, base=0,
                               pattern=[[0, 2 * GROUPS], [1, P]], channel_multiplier=-1).then_inc(S.wm, 1)
            root(Tile(0, 1))
            head_roots(Tile(0))
            periods(pool, period)
            root_x1(Tile(0, TILES - 1))
            store_x1(Tile(0, TILES - 1))
            store_h2T(Tile(0, TILES - 1))
            pool.wait_ge(S.x1_out0, 16 * 5)
            pool.wait_ge(S.x1_out1, 16 * 4)
            pool.wait_ge(S.h2T_out, 16 * TILES)

        @block.scalar
        def _(act):
            def square_x(t):
                act.wait_ge(x_loaded[t.s], (t.half + 1) * 16)
                wait(act, S.mean, t.n)
                nc.scalar.activation(squares[:, :], x[t.s][:, :], ACT.Square, accum_out=sumsq[:, :])\
                    .then_inc(S.sumsq, 1)

            def square_x1(t):
                act.wait_ge(S.x1_ready, t.n + 1)
                wait(act, S.mean2, t.n)
                nc.scalar.activation(squares2[:, :], x1[t.s][:, :], ACT.Square, accum_out=sumsq2[:, :])\
                    .then_inc(S.sumsq2, 1)

            def copy_hT(t):
                act.wait_ge(S.hT_ps, t.n + 1)
                wait(act, S.z_ps, t.n * 3)
                for half in (slice(0, 4), slice(4, 8)):
                    nc.scalar.activation(hT[:, half, :], t_ps[:, half, :], ACT.Copy).then_inc(S.hT, 1)

            def copy_h2T(t):
                act.wait_ge(S.h2T_ps, t.n + 1)
                wait(act, S.h2T_out, t.n * 16)
                for half in (slice(0, 4), slice(4, 8)):
                    nc.scalar.activation(h2T[:, half, :], t_ps[:, half, :], ACT.Copy).then_inc(S.h2T, 1)

            def take_p(t):
                act.wait_ge(S.z_ps, t.n * 3 + 1)
                nc.scalar.activation(p[t.s][:, :], z_ps[:, 0, :], ACT.Copy).then_inc(S.zp, 1)

            def take_u(t):
                act.wait_ge(S.z_ps, t.n * 3 + 2)
                wait(act, S.gmlp_mixed, t.n)
                nc.scalar.activation(uT[:, :, :].rearrange("p g t -> p (g t)"), z_ps[:, 1, :], ACT.Gelu)\
                    .then_inc(S.zu, 1)

            def take_v(t):
                act.wait_ge(S.z_ps, t.n * 3 + 3)
                nc.scalar.activation(v[:, :, :].rearrange("p g c -> p (g c)"), z_ps[:, 2, :], ACT.Gelu)\
                    .then_inc(S.zv, 1)

            def period(t):
                if not t.last:
                    copy_hT(t.after(1))
                if not t.first:
                    square_x1(t.after(-1))
                act.wait_ge(S.diff, t.n + 1)
                nc.scalar.activation(diffT[:, :, :], diff_ps[:, :, :], ACT.Copy).then_inc(S.diffT, 1)
                if not (t.last or t.after(1).last):
                    square_x(t.after(2))
                if not t.last:
                    take_p(t.after(1))
                    take_u(t.after(1))
                if not t.first:
                    copy_h2T(t.after(-1))
                if not t.last:
                    take_v(t.after(1))

            square_x(Tile(0))
            copy_hT(Tile(0))
            square_x(Tile(0, 1))
            take_p(Tile(0))
            take_u(Tile(0))
            take_v(Tile(0))
            periods(act, period)
            square_x1(Tile(0, TILES - 1))
            copy_h2T(Tile(0, TILES - 1))

        @block.vector
        def _(dve):
            def norm_x(t):
                kind = int(t.sample)
                dve.wait_ge(S.sumsq, t.n + 1)
                nc.vector.tensor_scalar(mean[:, :], sumsq[:, :], 1.0 / D, EPS, ALU.mult, ALU.add).then_inc(S.mean, 1)
                dve.wait_ge(S.rstd, t.n + 1)
                wait(dve, S.hT_ps, t.n)
                nc.vector.scalar_tensor_tensor(out=h[:, :], in0=x[t.s][:, :], scalar=rstd[:, :],
                                               in1=mods[:, kind, SCALE1, :], op0=ALU.mult, op1=ALU.mult)\
                    .then_inc(S.h_scaled, 1)
                dve.wait_ge(S.h_scaled, t.n + 1)
                nc.vector.tensor_tensor(h[:, :], h[:, :], mods[:, kind, SHIFT1, :], ALU.add).then_inc(S.h, 1)

            def mean_x1(t):
                dve.wait_ge(S.sumsq2, t.n + 1)
                nc.vector.tensor_scalar(mean2[:, :], sumsq2[:, :], 1.0 / D, EPS, ALU.mult, ALU.add)\
                    .then_inc(S.mean2, 1)

            def norm_x1(t):
                kind = int(t.sample)
                dve.wait_ge(S.rstd2, t.n + 1)
                wait(dve, S.h2T_ps, t.n)
                nc.vector.scalar_tensor_tensor(out=h2[:, :], in0=x1[t.s][:, :], scalar=rstd2[:, :],
                                               in1=mods[:, kind, SCALE2, :], op0=ALU.mult, op1=ALU.mult)\
                    .then_inc(S.h2_scaled, 1)
                dve.wait_ge(S.h2_scaled, t.n + 1)
                nc.vector.tensor_tensor(h2[:, :], h2[:, :], mods[:, kind, SHIFT2, :], ALU.add).then_inc(S.h2, 1)

            def norm_v(t):
                dve.wait_ge(S.zv, t.n + 1)
                nc.vector.tensor_tensor(vsq[:, :, :], v[:, :, :], v[:, :, :], ALU.mult).then_inc(S.v_squared, 1)
                dve.wait_ge(S.v_squared, t.n + 1)
                nc.vector.tensor_reduce(vsum[:, :], vsq[:, :, :], AX.X, ALU.add).then_inc(S.v_summed, 1)
                dve.wait_ge(S.v_summed, t.n + 1)
                nc.vector.tensor_scalar(vsum[:, :], vsum[:, :], 1.0 / P, EPS, ALU.mult, ALU.add).then_inc(S.vmean, 1)
                dve.wait_ge(S.vrstd, t.n + 1)
                nc.vector.tensor_tensor(v[:, :, :], v[:, :, :], vrstd[:, :].rearrange("p (g c) -> p g c", c=1)
                                        .to_broadcast([P, GROUPS, P]), ALU.mult).then_inc(S.v_scaled, 1)
                dve.wait_ge(S.v_scaled, t.n + 1)
                nc.vector.tensor_tensor(v[:, :, :], v[:, :, :],
                                        gmlp_g_sb[:, :].rearrange("p (g c) -> p g c", g=GROUPS), ALU.mult)\
                    .then_inc(S.vn, 1)

            def mix_gmlp(t):
                dve.wait_ge(S.gmlp_ps, t.n + 1)
                nc.vector.tensor_tensor(sT[:, :, :], sT_ps, bs[:, int(t.sample), :, :], ALU.add)\
                    .then_inc(S.s_biased, 1)
                dve.wait_ge(S.s_biased, t.n + 1)
                dve.wait_ge(S.zu, t.n + 1)
                nc.vector.tensor_tensor(mixT[:, 4:8, :], uT[:, :, :], sT[:, :, :], ALU.mult).then_inc(S.gmlp_mixed, 1)

            def mix_pool(t):
                dve.wait_ge(S.pool, t.n + 1)
                nc.vector.tensor_tensor(mixT[:, 0:4, :], pool_ps, pool_scale_sb[:, :]
                                        .rearrange("p (g c) -> p g c", c=1).to_broadcast([P, GROUPS, P]), ALU.mult)\
                    .then_inc(S.pool_mixed, 1)

            def add_mix(t):
                dve.wait_ge(S.mix, t.n + 1)
                nc.vector.tensor_tensor(gated[:, :], mix_ps[:, :, :].rearrange("p a n -> p (a n)"),
                                        mods[:, int(t.sample), GATE1, :], ALU.mult).then_inc(S.mix_read, 1)
                dve.wait_ge(S.mix_read, t.n + 1)
                dve.wait_ge(r_loaded[t.s], (t.half + 1) * 16)
                nc.vector.tensor_tensor(x1[t.s][:, :], x1[t.s][:, :], gated[:, :], ALU.add).then_inc(S.x1_ready, 1)

            def period(t):
                if not t.first:
                    add_mix(t.after(-1))
                mix_gmlp(t)
                if not t.first:
                    mean_x1(t.after(-1))
                mix_pool(t)
                if not t.first:
                    norm_x1(t.after(-1))
                if not (t.last or t.after(1).last):
                    norm_x(t.after(2))
                if not t.last:
                    norm_v(t.after(1))

            dve.wait_ge(S.mods_in, 16)
            norm_x(Tile(0))
            dve.wait_ge(S.ws_ps, 1)
            nc.vector.tensor_copy(wmT[:, 0, :, :], z_ps[:, 0, :].rearrange("p (g t) -> p g t", g=GROUPS))\
                .then_inc(S.ws_sb, 1)
            nc.vector.tensor_copy(wmT[:, 1, :, :], z_ps[:, 1, :].rearrange("p (g t) -> p g t", g=GROUPS))\
                .then_inc(S.ws_sb, 1)
            norm_x(Tile(0, 1))
            dve.wait_ge(S.consts, CONSTS)
            nc.vector.tensor_copy(bs[:, 1, :, :].rearrange("p h (b i) -> p h b i", b=STREAMS),
                                  bs[:, 0, :, 0:STEP].rearrange("p h (b i) -> p h b i", b=1)
                                  .to_broadcast([P, GROUPS, STREAMS, STEP])).then_inc(S.bs_rep, 1)
            norm_v(Tile(0))
            dve.wait_ge(S.bs_rep, 1)
            dve.wait_ge(S.w_out_in, 32)
            dve.wait_ge(S.mods_sample, 16 * STREAMS)
            periods(dve, period)
            add_mix(Tile(0, TILES - 1))
            mean_x1(Tile(0, TILES - 1))
            norm_x1(Tile(0, TILES - 1))

        @block.tensor
        def _(pe):
            def transpose_h(t):
                pe.wait_ge(S.h, t.n + 1)
                if not (isinstance(t.n, int) and t.n < 3):
                    pe.wait_ge(S.h2T, (t.n - 2) * 2)
                for k in range(KD):
                    last = nc.tensor.transpose(t_ps[:, k, :], h[:, k * P:(k + 1) * P], ident[:, :])
                last.then_inc(S.hT_ps, 1)

            def project(t, b):
                if b == 0:
                    pe.wait_ge(S.hT, t.n * 2 + 2)
                wait(pe, (S.zp, S.zu, S.zv)[b], t.n)
                for k in range(KD):
                    if b != 1:
                        last = nc.tensor.matmul(z_ps[:, b, :], hT[:, k, :], w_in_sb[:, k, b * HALF:(b + 1) * HALF],
                                                start=k == 0, stop=k == KD - 1)
                if b == 1:
                    for g in range(GROUPS):
                        chan = slice(HALF + g * P, HALF + (g + 1) * P)
                        for k in range(KD):
                            last = nc.tensor.matmul(z_ps[:, 1, g * P:(g + 1) * P], w_in_sb[:, k, chan], hT[:, k, :],
                                                    start=k == 0, stop=k == KD - 1)
                last.then_inc(S.z_ps, 1)

            def difference(t):
                pe.wait_ge(S.zp, t.n + 1)
                wait(pe, S.diffT, t.n)
                now, before, rows = BAND_NEXT, bands[:, BAND_BEFORE], p[1 - t.s]
                if t.sample:
                    now, before, rows = BAND_SAMPLE, bands[0:STREAMS * HIST, BAND_HIST], hist
                if t.first:
                    now = BAND_FIRST
                for g in range(GROUPS):
                    chan = slice(g * P, (g + 1) * P)
                    last = nc.tensor.matmul(diff_ps[:, g, :], p[t.s][:, chan], bands[:, now, g, :],
                                            start=True, stop=t.first)
                    if not t.first:
                        last = nc.tensor.matmul(diff_ps[:, g, :], rows[:, chan], before[:, g, :],
                                                start=False, stop=True)
                last.then_inc(S.diff, 1)

            def mix_tokens(t):
                pe.wait_ge(S.vn, t.n + 1)
                wait(pe, S.mix_read, t.n)
                for g in range(GROUPS):
                    last = nc.tensor.matmul(sT_ps[:, g, :], v[:, g, :], wmT[:, int(t.sample), g, :],
                                            start=True, stop=True)
                last.then_inc(S.gmlp_ps, 1)

            def mix_channels(t):
                pe.wait_ge(S.diffT, t.n + 1)
                for g in range(GROUPS):
                    last = nc.tensor.matmul(pool_ps[:, g, :], pool_w_sb[:, g, :], diffT[:, g, :],
                                            start=True, stop=True)
                last.then_inc(S.pool, 1)

            def transpose_h2(t):
                pe.wait_ge(S.h2, t.n + 1)
                if t.last or t.after(1).last:
                    pe.wait_ge(S.hT, TILES * 2)
                else:
                    pe.wait_ge(S.hT, (t.n + 3) * 2)
                if t.last:
                    pe.wait_ge(S.h2T, t.n * 2)
                for k in range(KD):
                    last = nc.tensor.transpose(t_ps[:, k, :], h2[:, k * P:(k + 1) * P], ident[:, :])
                last.then_inc(S.h2T_ps, 1)

            def project_out(t):
                pe.wait_ge(S.gmlp_mixed, t.n + 1)
                pe.wait_ge(S.pool_mixed, t.n + 1)
                for b in range(2):
                    for k in range(KD):
                        last = nc.tensor.matmul(mix_ps[:, b, :], mixT[:, k, :], w_out_sb[:, k, b * HALF:(b + 1) * HALF],
                                                start=k == 0, stop=k == KD - 1)
                last.then_inc(S.mix, 1)

            def period(t):
                if not t.last:
                    transpose_h(t.after(1))
                difference(t)
                mix_tokens(t)
                if not t.last:
                    project(t.after(1), 0)
                mix_channels(t)
                if not t.last:
                    project(t.after(1), 1)
                if not t.first:
                    transpose_h2(t.after(-1))
                if not t.last:
                    project(t.after(1), 2)
                project_out(t)

            pe.wait_ge(S.early, EARLY)
            for kind in range(2):
                for g in range(GROUPS):
                    last = nc.tensor.transpose(z_ps[:, kind, g * P:(g + 1) * P], ws[:, kind, g, :], ident[:, :])
            last.then_inc(S.ws_ps, 1)
            transpose_h(Tile(0))
            pe.wait_ge(S.ws_sb, 2)
            for b in range(3):
                project(Tile(0), b)
            pe.wait_ge(S.wm, 1)
            pe.wait_ge(S.consts, CONSTS)
            pe.wait_ge(S.w_out_in, 32)
            periods(pe, period)
            transpose_h2(Tile(0, TILES - 1))


def routing(nc, ctx, wq, keys, u_table, v_table, ident_in, shared, h2T_tiles, gate_blocks):
    S = sems(nc, ctx, "route", "passed consts wq experts_in iota h2 keys_ps keysT q_ps q qT_ps qT scores "
                               "scores_used shifted exp gate_ready keyed slotsT_ps slotsT left_hot left "
                               "right_hot right place_ps placed out0 out1 dve")
    HP = HEADS * 2
    WIDE, NARROW = 4, 12
    NW = WIDE * TOPK
    SUMS = NW + NARROW * 4
    with ExitStack() as mem:
        wq_sb = [query_weights(shared, b) for b in range(WQ_SHARED)] + \
                [sbuf(nc, mem, "wq_sb", [P, KD, HALF])[:, :, :]]
        keysT = sbuf(nc, mem, "keysT", [P, HP, NKEYS])
        ident = sbuf(nc, mem, "ident_c", [P, P])
        h2T = sbuf(nc, mem, "h2T", [P, KD, P])
        q = sbuf(nc, mem, "q", [P, 4, P])
        qT = sbuf(nc, mem, "qT", [P, HP, P])
        work = sbuf(nc, mem, "work", [P, HP * NKEYS])
        best = sbuf(nc, mem, "best", [P, HP, TOPK])
        best_at = sbuf(nc, mem, "best_at", [P, HP, TOPK], U32)
        best_key = sbuf(nc, mem, "best_key", [P, HP, TOPK], BF16)
        pair = sbuf(nc, mem, "pair", [P, HEADS, TOPK])
        pair_at = sbuf(nc, mem, "pair_at", [P, HEADS, TOPK], U32)
        soft = sbuf(nc, mem, "soft", [P, HEADS, TOPK])
        digits = sbuf(nc, mem, "digits", [P, 4, HEADS, TOPK], U32)
        narrow = sbuf(nc, mem, "narrow", [P, HEADS, TOPK])
        ranks = sbuf(nc, mem, "ranks", [P, 2, HEADS, TOPK])
        rank = sbuf(nc, mem, "rank", [P, 2, HEADS, TOPK], BF16)
        hit = sbuf(nc, mem, "hit", [P, HP, TOPK, TOPK], BF16)
        total = sbuf(nc, mem, "total", [P, HEADS])
        slots = sbuf(nc, mem, "slots", [P, 3, HEADS, TOPK])
        keyT = sbuf(nc, mem, "keyT", [P, 2, P], BF16)
        gateT = sbuf(nc, mem, "gateT", [P, P])
        left_hot = [sbuf(nc, mem, f"left_hot{s}", [P, NKEYS, BATCH], BF16) for s in range(2)]
        left = [sbuf(nc, mem, f"left{s}", [P, BATCH, NKEYS]) for s in range(2)]
        right_hot = [sbuf(nc, mem, f"right_hot{s}", [P, NKEYS, BATCH], BF16) for s in range(2)]
        right = [sbuf(nc, mem, f"right{s}", [P, BATCH, NKEYS]) for s in range(2)]
        dense = [sbuf(nc, mem, f"dense{s}", [P, NKEYS, BLOCK]) for s in range(2)]
        iota_rank = sbuf(nc, mem, "iota_rank", [P, TOPK, TOPK], BF16)
        iota_keys = sbuf(nc, mem, "iota_keys", [P, NKEYS, BATCH], BF16)
        s_ps = psum(nc, mem, "s_ps", [P, HP, NKEYS])
        q_ps = psum(nc, mem, "q_ps", [P, HALF])
        x_ps = psum(nc, mem, "x_ps", [P, 4, P])
        place_ps = psum(nc, mem, "place_ps", [P, 2, 4, NKEYS])
        stored = [S.out0, S.out1]
        BATCHES = P // BATCH
        key4 = best_key[:, :, :].rearrange("p (h s) k -> p h s k", s=2)
        block = mem.enter_context(nc.Block())

        def wait_for_placed(eng, t, b):
            wait(eng, S.place_ps, t * (BATCHES * 2) + max(b - 1, 0) * 2)

        def periods(eng, period):
            period(0, None, 1)
            period(1, 0, 2)
            with eng.Fori(2, TILES - 1) as t:
                period(t, t - 1, t + 1)
            period(TILES - 1, TILES - 2, None)
            period(None, TILES - 1, None)

        @block.sync
        def _(sp):
            sp.dma_start(work[:, :].rearrange("k (n c) -> k n c", n=HP), keys.rearrange("h s k c -> k (h s) c"))\
                .then_inc(S.consts, 16)
            sp.dma_start(ident[:, :], ident_in).then_inc(S.consts, 16)
            sp.dma_start(h2T[:, :, :].rearrange("p k t -> p (k t)"), h2T_tiles[0, :, :]).then_inc(S.h2, 16)
            sp.dma_start(wq_sb[3], wq[:, 3 * HALF:4 * HALF].rearrange("(k p) n -> p k n", p=P)).then_inc(S.wq, 16)

            def load_h2(t):
                sp.wait_ge(S.q_ps, t * 4)
                sp.dma_start(h2T[:, :, :].rearrange("p k t -> p (k t)"),
                             h2T_tiles[bass.ds(t, 1), :, :].rearrange("a p d -> p (a d)")).then_inc(S.h2, 16)

            def store(t):
                for half in range(2):
                    sp.wait_ge(S.placed, t * 32 + 2 + 16 * (half + 1))
                    sp.dma_start(gate_blocks[bass.ds(t * 2 + half, 1), :, :, :].rearrange("a p i j -> p (a i j)"),
                                 dense[half][:, :, :].rearrange("p i j -> p (i j)")).then_inc(stored[half], 16)
            load_h2(1)
            load_h2(2)
            with sp.Fori(1, TILES - 2) as t:
                load_h2(t + 2)
                store(t - 1)
            store(TILES - 3)
            sp.wait_ge(S.q_ps, TILES * 4)
            ff, u, v = expert_memory(shared)
            for dst, src in ((u[0], u_table[0:P, :]), (u[1], u_table[P:2 * P, :]), (v, v_table[0:P, :])):
                sp.dma_start(dst, src).then_inc(S.experts_in, 16)
            for t in range(TILES):
                sp.dma_start(ff[:, t, :], h2T_tiles[t, :, :]).then_inc(S.experts_in, 16)
            store(TILES - 2)
            store(TILES - 1)
            sp.wait_ge(S.experts_in, (3 + TILES) * 16)
            for half in range(2):
                sp.wait_ge(stored[half], TILES * 16)

        @block.gpsimd
        def _(pool):
            pool.iota(iota_rank[:, :, :], pattern=[[1, TOPK], [0, TOPK]], base=0, channel_multiplier=0,
                      allow_small_or_imprecise_dtypes=True).then_inc(S.iota, 1)
            pool.iota(iota_keys[:, :, :], pattern=[[1, NKEYS], [0, BATCH]], base=0, channel_multiplier=0,
                      allow_small_or_imprecise_dtypes=True).then_inc(S.iota, 1)

            def place(t):
                pool.wait_ge(S.slotsT, t * 2 + 2)
                for b in range(BATCHES):
                    wait_for_placed(pool, t, b)
                    pool.wait_ge(S.right_hot, t * BATCHES + b + 1)
                    nc.gpsimd.tensor_tensor(
                        right[b % 2][:, :, :], right_hot[b % 2][:, :, :].rearrange("p i t -> p t i"),
                        gateT[:, b * BATCH:(b + 1) * BATCH].rearrange("p (t o) -> p t o", o=1)
                        .to_broadcast([P, BATCH, NKEYS]), ALU.mult).then_inc(S.right, 1)

            def period(choose, placed, prepare):
                if placed is not None:
                    place(placed)
            periods(pool, period)

        @block.scalar
        def _(act):
            act.sem_inc(S.placed, 2)
            act.wait_ge(S.keys_ps, 1)
            nc.scalar.activation(keysT[:, :, :], s_ps[:, :, :], ACT.Copy).then_inc(S.keysT, 1)

            def take_q(t, b):
                n = t * 4 + b
                act.wait_ge(S.q_ps, n + 1)
                wait(act, S.qT_ps, n)
                nc.scalar.activation(q[:, :, :].rearrange("p a c -> p (a c)"), q_ps[:, :], ACT.Copy).then_inc(S.q, 1)

            def take_qT(t, b):
                act.wait_ge(S.qT_ps, t * 4 + b + 1)
                wait(act, S.scores, t * 4)
                nc.scalar.activation(qT[:, b * 4:b * 4 + 4, :], x_ps[:, :, :], ACT.Copy).then_inc(S.qT, 1)

            def take_slots(t):
                act.wait_ge(S.slotsT_ps, t + 1)
                nc.scalar.activation(keyT[:, :, :], x_ps[:, 0:2, :], ACT.Copy).then_inc(S.slotsT, 1)
                nc.scalar.activation(gateT[:, :], x_ps[:, 2, :], ACT.Copy).then_inc(S.slotsT, 1)

            def left_rows(t, b):
                act.wait_ge(S.left_hot, t * BATCHES + b + 1)
                wait_for_placed(act, t, b)
                nc.scalar.activation(left[b % 2][:, :, :], left_hot[b % 2][:, :, :].rearrange("p i t -> p t i"),
                                     ACT.Copy).then_inc(S.left, 1)

            def take_gates(t, b):
                half = b * 2 // BATCHES
                if b * 2 % BATCHES == 0:
                    wait(act, stored[half], t * 16)
                for g in range(2):
                    act.wait_ge(S.place_ps, (t * BATCHES + b) * 2 + g + 1)
                    at = b * BATCH % BLOCK + g * 4
                    nc.scalar.activation(dense[half][:, :, at:at + 4].rearrange("p i t -> p t i"),
                                         place_ps[:, g, :, :], ACT.Copy).then_inc(S.placed, 1)

            def period(choose, placed, prepare):
                if prepare is not None:
                    take_q(prepare, 0)
                if placed is not None:
                    take_slots(placed)
                if prepare is not None:
                    take_qT(prepare, 0)
                    take_q(prepare, 1)
                for b in range(BATCHES):
                    if placed is not None:
                        left_rows(placed, b)
                        if b:
                            take_gates(placed, b - 1)
                    if prepare is not None and b in (4, 8):
                        take_q(prepare, b // 4 + 1)
                    if prepare is not None and b in (1, 5, 9):
                        take_qT(prepare, b // 4 + 1)
                    if choose is not None and b == 12:
                        act.wait_ge(S.shifted, choose + 1)
                        nc.scalar.activation(soft[:, :, :], soft[:, :, :], ACT.Exp).then_inc(S.exp, 1)
                if placed is not None:
                    take_gates(placed, BATCHES - 1)
            for b in range(4):
                take_q(0, b)
                take_qT(0, b)
            periods(act, period)

        @block.vector
        def _(dve):
            own = Order(dve, S.dve)
            PER_TILE = 141
            dve.wait_ge(S.iota, 2)
            dve.wait_ge(S.keysT, 1)
            best4 = best[:, :, :].rearrange("p (h s) k -> p h s k", s=2)
            sums = work[:, 0:HEADS * SUMS].rearrange("p (h n) -> p h n", h=HEADS)
            work3 = work[:, :].rearrange("p (n k) -> p n k", n=HP)
            low, high = slice(0, 8), slice(8, 16)

            def two_lists(t, rows):
                for n in range(HP):
                    if n % 4 == 0:
                        dve.wait_ge(S.scores, t * 4 + n // 4 + 1)
                        dve.sem_inc(S.passed, 1)
                    own.mark(nc.vector.max(best[:, n, low], s_ps[:, n, :]))
                own.settle()
                dve.sem_inc(S.passed, 1)
                for n in range(HP):
                    own.mark(nc.vector.max_index(best_at[:, n, low], best[:, n, low], s_ps[:, n, :]))
                    own.mark(nc.vector.match_replace(work3[:, n, :], best[:, n, low], s_ps[:, n, :], NEG))
                rows(0)
                own.settle()
                nc.vector.memset(total[:, :], 0.0).then_inc(S.scores_used, 1)
                for n in range(HP):
                    own.mark(nc.vector.max(best[:, n, high], work3[:, n, :]))
                rows(1)
                own.settle()
                dve.sem_inc(S.passed, 1)
                for n in range(HP):
                    own.mark(nc.vector.max_index(best_at[:, n, high], best[:, n, high], work3[:, n, :]))
                rows(2)
                own.settle()
                own.mark(nc.vector.tensor_copy(best_key[:, :, :], best_at[:, :, :]))
                rows(3)
                own.settle()

            def best_pairs(t, rows):
                first, second = best4[:, :, 0, :], best4[:, :, 1, :]
                for at, a, nb in ((slice(0, NW), slice(0, WIDE), TOPK), (slice(NW, SUMS), slice(WIDE, TOPK), 4)):
                    na = a.stop - a.start
                    own.mark(nc.vector.tensor_tensor(
                        sums[:, :, at].rearrange("p h (a b) -> p h a b", a=na),
                        first[:, :, a].rearrange("p h (a o) -> p h a o", o=1).to_broadcast([P, HEADS, na, nb]),
                        second[:, :, 0:nb].rearrange("p h (o b) -> p h o b", o=1).to_broadcast([P, HEADS, na, nb]),
                        ALU.add))
                rows(4)
                own.settle()
                dve.sem_inc(S.passed, 1)
                for n, part in enumerate((low, high)):
                    for h in range(HEADS):
                        own.mark(nc.vector.max(pair[:, h, part], sums[:, h]))
                    rows(5 + n * 3)
                    own.settle()
                    dve.sem_inc(S.passed, 1)
                    for h in range(HEADS):
                        own.mark(nc.vector.max_index(pair_at[:, h, part], pair[:, h, part], sums[:, h]))
                    rows(6 + n * 3)
                    own.settle()
                    dve.sem_inc(S.passed, 1)
                    if part is low:
                        for h in range(HEADS):
                            own.mark(nc.vector.match_replace(sums[:, h], pair[:, h, low], sums[:, h], NEG))
                        rows(7)
                        own.settle()
                        dve.sem_inc(S.passed, 1)

            def chosen_ranks(t, rows):
                nc.vector.tensor_tensor(soft[:, :, :], pair[:, :, :],
                                        pair[:, :, 0:1].to_broadcast([P, HEADS, TOPK]), ALU.subtract)\
                    .then_inc(S.shifted, 1)
                for n, (op, by) in enumerate(((ALU.logical_shift_right, 4), (ALU.bitwise_and, 15),
                                              (ALU.logical_shift_right, 2), (ALU.bitwise_and, 3))):
                    own.mark(nc.vector.tensor_scalar(digits[:, n], pair_at[:, :, :], by, None, op))
                own.mark(nc.vector.tensor_scalar(narrow[:, :, :], pair_at[:, :, :], NW, None, ALU.is_ge))
                rows(10)
                own.settle()
                own.mark(nc.vector.tensor_tensor(ranks[:, :], digits[:, 2:4], digits[:, 0:2], ALU.subtract))
                rows(11)
                own.settle()
                own.mark(nc.vector.tensor_tensor(
                    ranks[:, :], ranks[:, :], narrow[:, :, :].rearrange("p (o h) k -> p o h k", o=1)
                    .to_broadcast([P, 2, HEADS, TOPK]), ALU.mult))
                rows(12)
                own.settle()
                own.mark(nc.vector.tensor_tensor(ranks[:, :], ranks[:, :], digits[:, 0:2], ALU.add))
                rows(13)
                own.settle()
                own.mark(nc.vector.scalar_tensor_tensor(
                    out=rank[:, 0], in0=narrow[:, :, :], scalar=-float(NW // 4 - WIDE), in1=ranks[:, 0],
                    op0=ALU.mult, op1=ALU.add))
                own.mark(nc.vector.tensor_copy(rank[:, 1], ranks[:, 1]))
                rows(14)
                own.settle()
                own.mark(nc.vector.tensor_tensor(
                    hit[:, :, :, :], rank[:, :].rearrange("p s h (o k) -> p (s h) o k", o=1)
                    .to_broadcast([P, HP, TOPK, TOPK]),
                    iota_rank[:, :, :].rearrange("p (o a) k -> p o a k", o=1)
                    .to_broadcast([P, HP, TOPK, TOPK]), ALU.is_equal))
                rows(15)
                own.settle()
                for s in range(2):
                    own.mark(nc.vector.tensor_tensor(
                        hit[:, s * HEADS:(s + 1) * HEADS], hit[:, s * HEADS:(s + 1) * HEADS],
                        key4[:, :, s, :].rearrange("p h (a o) -> p h a o", o=1)
                        .to_broadcast([P, HEADS, TOPK, TOPK]), ALU.mult))
                own.settle()
                for n in (8, 4, 2):
                    own.then(nc.vector.tensor_tensor(hit[:, :, 0:n, :], hit[:, :, 0:n, :], hit[:, :, n:2 * n, :],
                                                     ALU.add))
                nc.vector.tensor_tensor(slots[:, 0:2, :, :].rearrange("p s h k -> p (s h) k"), hit[:, :, 0, :],
                                        hit[:, :, 1, :], ALU.add).then_inc(S.keyed, 1)

            def softmax(t):
                dve.wait_ge(S.exp, t + 1)
                own.then(nc.vector.tensor_reduce(total[:, :], soft[:, :, :], AX.X, ALU.add))
                own.then(nc.vector.reciprocal(total[:, :], total[:, :]))
                nc.vector.tensor_tensor(slots[:, 2, :, :], soft[:, :, :],
                                        total[:, :].rearrange("p (h o) -> p h o", o=1)
                                        .to_broadcast([P, HEADS, TOPK]), ALU.mult).then_inc(S.gate_ready, 1)
                assert own.n == PER_TILE, own.n

            def hot_rows(t, b):
                keys_iota = iota_keys[:, :, :]
                if b == 0:
                    dve.wait_ge(S.slotsT, t * 2 + 2)

                def key(n):
                    return keyT[:, n, b * BATCH:(b + 1) * BATCH].rearrange("p (o t) -> p o t", o=1)\
                        .to_broadcast([P, NKEYS, BATCH])
                wait(dve, S.right, t * BATCHES + max(b - 1, 0))
                nc.vector.tensor_tensor(right_hot[b % 2][:, :, :], key(1), keys_iota, ALU.is_equal)\
                    .then_inc(S.right_hot, 1)
                wait(dve, S.left, t * BATCHES + max(b - 1, 0))
                nc.vector.tensor_tensor(left_hot[b % 2][:, :, :], key(0), keys_iota, ALU.is_equal)\
                    .then_inc(S.left_hot, 1)

            def period(choose, placed, prepare):
                def rows(b):
                    if placed is not None:
                        hot_rows(placed, b)

                if choose is not None:
                    own.loop(choose * PER_TILE)
                    two_lists(choose, rows)
                    best_pairs(choose, rows)
                    chosen_ranks(choose, rows)
                    softmax(choose)
                else:
                    for b in range(BATCHES):
                        rows(b)
            periods(dve, period)

        @block.tensor
        def _(pe):
            pe.wait_ge(S.consts, 32)
            for n in range(HP):
                last = nc.tensor.transpose(s_ps[:, n, :], work[:, n * P:(n + 1) * P], ident[:, :])
            last.then_inc(S.keys_ps, 1)

            def product(t, b, steps=range(KD)):
                if 0 in steps:
                    if b == 0:
                        pe.wait_ge(S.h2, t * 16 + 16)
                    if isinstance(t, int) and t == 0 and b == 3:
                        pe.wait_ge(S.wq, 16)
                    wait(pe, S.q, t * 4 + b)
                for k in steps:
                    last = nc.tensor.matmul(q_ps[:, :], h2T[:, k, :], wq_sb[b][:, k, :],
                                            start=k == 0, stop=k == KD - 1)
                if KD - 1 in steps:
                    last.then_inc(S.q_ps, 1)

            def turn(t, b):
                pe.wait_ge(S.q, t * 4 + b + 1)
                wait(pe, S.qT, t * 4 + b)
                for n in range(4):
                    last = nc.tensor.transpose(x_ps[:, n, :], q[:, n, :], ident[:, :])
                last.then_inc(S.qT_ps, 1)

            def scores(t, b):
                pe.wait_ge(S.qT, t * 4 + b + 1)
                if b == 0:
                    wait(pe, S.scores_used, t)
                for n in range(b * 4, b * 4 + 4):
                    last = nc.tensor.matmul(s_ps[:, n, :], qT[:, n, :], keysT[:, n, :], start=True, stop=True)
                last.then_inc(S.scores, 1)

            def turn_slots(t):
                pe.wait_ge(S.keyed, t + 1)
                pe.wait_ge(S.gate_ready, t + 1)
                for n in range(3):
                    last = nc.tensor.transpose(x_ps[:, n, :], slots[:, n, :, :].rearrange("p h k -> p (h k)"),
                                               ident[:, :])
                last.then_inc(S.slotsT_ps, 1)

            def place(t, b):
                n = t * BATCHES + b
                pe.wait_ge(S.left, n + 1)
                pe.wait_ge(S.right, n + 1)
                for g in range(2):
                    pe.wait_ge(S.placed, n * 2 + g + 1)
                    for j in range(4):
                        last = nc.tensor.matmul(place_ps[:, g, j, :], right[b % 2][:, g * 4 + j, :],
                                                left[b % 2][:, g * 4 + j, :], start=True, stop=True)
                    last.then_inc(S.place_ps, 1)

            def period(choose, placed, prepare):
                if prepare is not None:
                    product(prepare, 0)
                if placed is not None:
                    turn_slots(placed)
                if prepare is not None:
                    product(prepare, 1, range(0, 5))
                    if placed is not None:
                        pe.wait_ge(S.slotsT, placed * 2 + 2)
                    turn(prepare, 0)
                    product(prepare, 1, range(5, KD))
                for b in range(BATCHES):
                    if placed is not None:
                        place(placed, b)
                    if prepare is not None:
                        if b < 8:
                            product(prepare, 2 + b // 4, range(b % 4 * 2, b % 4 * 2 + 2))
                        if b in (0, 4, 8):
                            turn(prepare, b // 4 + 1)
                        if b in range(9, 13):
                            scores(prepare, b - 9)
            pe.wait_ge(S.keysT, 1)
            for b in range(4):
                product(0, b, range(0, 2))
                if b:
                    turn(0, b - 1)
                product(0, b, range(2, KD))
                if b:
                    scores(0, b - 1)
            turn(0, 3)
            scores(0, 3)
            periods(pe, period)


def experts(nc, ctx, u_table, v_table, g_final, ident_in, shared, mod_rows, x1_rows, gate_blocks, y_prompt,
            y_sample):
    S = sems(nc, ctx, "exp", "passed consts zero h_hi h_lo u0 u1 gates vld uT_ps uT_hi uT_lo act_ps gelu "
                             "m m_hi m_lo v_hi v_lo y_ps y_free g_last gate2_0 gate2_1 x1_0 x1_1 x1_2 x1_3 weighted summed "
                             "sumsq mean rstd final stored")
    EXPERTS = NKEYS * NKEYS
    EB = EXPERTS // P
    PAIRS = EB // 2
    TOKENS = TILES * P
    GROUP = TOKENS // 3
    OUTPUTS = 2 * TILES
    with ExitStack() as mem:
        ff, u, v = expert_memory(shared)
        ident = sbuf(nc, mem, "ident_d", [P, P])
        h_hi = sbuf(nc, mem, "h_hi", [P, KD, TOKENS], F32R)
        h_lo = sbuf(nc, mem, "h_lo", [P, KD, TOKENS], F32R)
        uT_hi = [sbuf(nc, mem, f"uT_hi{s}", [P, KD, P], F32R) for s in range(2)]
        uT_lo = [sbuf(nc, mem, f"uT_lo{s}", [P, KD, P], F32R) for s in range(2)]
        gates = sbuf(nc, mem, "gates", [P, BLOCKS, 2, BLOCK])
        g = sbuf(nc, mem, "g", [P, TOKENS])
        m_hi = [sbuf(nc, mem, f"m_hi{s}", [P, TOKENS], F32R) for s in range(3)]
        m_lo = [sbuf(nc, mem, f"m_lo{s}", [P, TOKENS], F32R) for s in range(3)]
        v_hi = [sbuf(nc, mem, f"v_hi{s}", [P, D], F32R) for s in range(3)]
        v_lo = [sbuf(nc, mem, f"v_lo{s}", [P, D], F32R) for s in range(3)]
        g_last = sbuf(nc, mem, "g_last", [P, D])
        power = sbuf(nc, mem, "power_d", [P, 1])
        sumsq = sbuf(nc, mem, "sumsq_d", [P, TILES])
        mean = sbuf(nc, mem, "mean_d", [P, TILES])
        rstd = sbuf(nc, mem, "rstd_d", [P, TILES])
        h_raw = [ff[:, t, :] for t in range(TILES)]
        gates_flat = gates[:, :, :, :].rearrange("p n i j -> p (n i j)")
        x1 = [u[0][:, :], u[1][:, :], gates_flat[:, 0:D], gates_flat[:, D:2 * D]]
        gate2 = [v[:, :], g[:, 0:D]]
        squares = uT_hi[1][:, :, :].rearrange("p k t -> p (k t)")
        uT_ps = psum(nc, mem, "uT_ps", [P, KD, P])
        a_ps = [psum(nc, mem, f"a_ps{n}", [P, HALF]) for n in range(3)]
        y_ps = [psum(nc, mem, f"y_ps{n}", [P, HALF]) for n in range(3)]
        block = mem.enter_context(nc.Block())

        def buffer(j, parity):
            return 2 if j else parity

        def pairs(eng, first, pair, last):
            first()
            with eng.Fori(0, PAIRS // 2 - 1) as i:
                pair(i * 2 + 1, 1)
                pair(i * 2 + 2, 0)
            last()

        @block.sync
        def _(sp):
            sp.dma_start(ident[:, :], ident_in).then_inc(S.consts, 16)
            for loaded in (S.u0, S.u1, S.vld):
                sp.sem_inc(loaded, 16)
            sp.dma_start(g_last[:, :], g_final.partition_broadcast(P)).then_inc(S.g_last, 16)
            u_loaded = [S.u0, S.u1]

            def load_u(e, s):
                wait(sp, S.uT_ps, e)
                sp.dma_start(u[s][:, :], u_table[bass.ds(e * P, P), :]).then_inc(u_loaded[s], 16)

            def load_v(e):
                wait(sp, S.v_lo, e)
                sp.dma_start(v[:, :], v_table[bass.ds(e * P, P), :]).then_inc(S.vld, 16)

            def store(t):
                if t < PROMPT_TILES:
                    dst = y_prompt[0, t * P:(t + 1) * P, :]
                else:
                    dst = y_sample.rearrange("b t d -> (b t) d")
                sp.wait_ge(S.final, t + 1)
                sp.dma_start(dst, ff[:, t, :]).then_inc(S.stored, 16)

            def load(c, more=True):
                load_u(c * 2 + 1, 1)
                load_v(c * 2)
                if more:
                    load_u(c * 2 + 2, 0)
                load_v(c * 2 + 1)
            load_u(2, 0)
            load_v(1)
            with sp.Fori(1, PAIRS - 1) as c:
                load(c)
            load(PAIRS - 1, more=False)

            def load_x1(t):
                sp.dma_start(x1[t % 4], x1_rows[t, :, :]).then_inc(x1_loaded[t % 4], 16)
            x1_loaded = [S.x1_0, S.x1_1, S.x1_2, S.x1_3]
            sp.wait_ge(S.uT_ps, EB + 1)
            load_x1(0)
            load_x1(1)
            sp.wait_ge(S.v_lo, EB)
            sp.dma_start(gate2[0], mod_rows[0, GATE2, :].partition_broadcast(P)).then_inc(S.gate2_0, 16)
            sp.wait_ge(S.m, EB * 3)
            load_x1(2)
            load_x1(3)
            sp.wait_ge(S.m_lo, EB * 3)
            for b in range(STREAMS):
                sp.dma_start(gate2[1][b * STEP:(b + 1) * STEP, :], mod_rows[1 + b, GATE2, :].partition_broadcast(STEP))\
                    .then_inc(S.gate2_1, 16)
            for t in range(TILES):
                if t + 4 < TILES:
                    sp.wait_ge(S.summed, t + 1)
                    load_x1(t + 4)
                if t >= 2:
                    store(t - 2)
            store(TILES - 2)
            store(TILES - 1)
            sp.wait_ge(S.stored, TILES * 16)

        @block.gpsimd
        def _(pool):
            pool.memset(power[:, :], -0.5).then_inc(S.zero, 1)

            def split_v(c, parity, j):
                e = c * 2 + j
                pool.wait_ge(S.v_hi, e + 1)
                nc.gpsimd.tensor_tensor(v_lo[buffer(j, parity)][:, :], v[:, :],
                                        v_hi[buffer(j, parity)][:, :].bitcast(F32), ALU.subtract)\
                    .then_inc(S.v_lo, 1)

            def load_gates(c):
                pool.sem_inc(S.passed, 1)
                pool.dma_start(gates[:, :, :, :],
                               gate_blocks[:, :, bass.ds(c * 2, 2), :].rearrange("n p i j -> p n (i j)"))\
                    .then_inc(S.gates, 16)

            def pair(c, parity, more=True):
                split_v(c, parity, 0)
                split_v(c, parity, 1)
                if more:
                    pool.wait_ge(S.m, c * 6 + 6)
                    load_gates(c + 1)
            load_gates(0)
            pool.wait_ge(S.h_lo, TILES)
            pool.memset(ff[:, :, :], 0.0).then_inc(S.zero, 1)
            pairs(pool, lambda: pair(0, 0), pair, lambda: pair(PAIRS - 1, 1, more=False))

            pool.wait_ge(S.gate2_0, 16)
            pool.wait_ge(S.gate2_1, 16 * STREAMS)
            pool.wait_ge(S.zero, 2)
            for t in range(TILES + 1):
                if t < TILES:
                    pool.wait_ge(S.y_free, 3 + (PAIRS - 1) * OUTPUTS + t * 2 + 2)
                    pool.tensor_tensor(ff[:, t, :], ff[:, t, :], gate2[int(t == TILES - 1)], ALU.mult)\
                        .then_inc(S.weighted, 1)
                if t:
                    pool.wait_ge(S.mean, t)
                    pool.tensor_tensor(rstd[:, t - 1:t], mean[:, t - 1:t], power[:, :], ALU.pow).then_inc(S.rstd, 1)

        @block.scalar
        def _(act):
            def split_h(n):
                for t in range(n * 3, n * 3 + 3):
                    nc.scalar.activation(h_hi[:, :, t * P:(t + 1) * P], h_raw[t].rearrange("p (k t) -> p k t", k=KD),
                                         ACT.Copy).then_inc(S.h_hi, 1)

            def uT(e, s):
                act.wait_ge(S.uT_ps, e + 2)
                wait(act, S.act_ps, e * 3 - 3)
                for n in range(2):
                    nc.scalar.activation(uT_hi[s][:, n * 4:n * 4 + 4, :], uT_ps[:, n * 4:n * 4 + 4, :], ACT.Copy)\
                        .then_inc(S.uT_hi, 1)

            def split_v(c, parity, j):
                e = c * 2 + j
                act.wait_ge(S.vld, e * 16 + 16)
                if j:
                    wait(act, S.y_ps, c * OUTPUTS)
                nc.scalar.activation(v_hi[buffer(j, parity)][:, :], v[:, :], ACT.Copy).then_inc(S.v_hi, 1)

            def weigh(c, parity, j):
                e = c * 2 + j
                wait(act, S.m_lo, e * 3)
                for n in range(3):
                    act.wait_ge(S.act_ps, e * 3 + n + 1)
                    nc.scalar.activation(g[:, n * GROUP:(n + 1) * GROUP], a_ps[n][:, 0:GROUP], ACT.Gelu)\
                        .then_inc(S.gelu, 1)
                act.wait_ge(S.m, e * 3 + 3)
                nc.scalar.activation(m_hi[buffer(j, parity)][:, :], g[:, :], ACT.Copy).then_inc(S.m_hi, 1)

            def pair(c, parity, more=True):
                uT(c * 2 + 1, 1)
                split_v(c, parity, 0)
                weigh(c, parity, 0)
                if more:
                    uT(c * 2 + 2, 0)
                split_v(c, parity, 1)
                weigh(c, parity, 1)
            act.wait_ge(S.uT_ps, 2)
            for n in range(2):
                nc.scalar.activation(uT_hi[0][:, n * 4:n * 4 + 4, :], uT_ps[:, n * 4:n * 4 + 4, :], ACT.Copy)\
                    .then_inc(S.uT_hi, 1)
            for n in range(3):
                split_h(n)
            pairs(act, lambda: pair(0, 0), pair, lambda: pair(PAIRS - 1, 1, more=False))

            for t in range(TILES):
                act.wait_ge(S.summed, t + 1)
                if t:
                    act.wait_ge(S.mean, t)
                nc.scalar.activation(squares, ff[:, t, :], ACT.Square, accum_out=sumsq[:, t:t + 1]).then_inc(S.sumsq, 1)

        @block.vector
        def _(dve):
            dve.sem_inc(S.y_free, 3)

            def uT(e, s):
                for n in range(2):
                    dve.wait_ge(S.uT_hi, e * 2 + n + 1)
                    part = slice(n * 4, n * 4 + 4)
                    nc.vector.tensor_tensor(uT_lo[s][:, part, :], uT_ps[:, part, :], uT_hi[s][:, part, :].bitcast(F32),
                                            ALU.subtract).then_inc(S.uT_lo, 1)

            def weigh(c, j, n):
                dve.wait_ge(S.gelu, (c * 2 + j) * 3 + n + 1)
                dve.wait_ge(S.gates, c * 16 + 16)
                part = g[:, n * GROUP:(n + 1) * GROUP].rearrange("p (n j) -> p n j", j=BLOCK)
                per = GROUP // BLOCK
                nc.vector.tensor_tensor(part, part, gates[:, n * per:(n + 1) * per, j, :], ALU.mult).then_inc(S.m, 1)

            def rest(c, j, parity, n):
                b = buffer(j, parity)
                dve.wait_ge(S.m_hi, c * 2 + j + 1)
                part = slice(n * GROUP, (n + 1) * GROUP)
                nc.vector.tensor_tensor(m_lo[b][:, part], g[:, part], m_hi[b][:, part].bitcast(F32), ALU.subtract)\
                    .then_inc(S.m_lo, 1)

            def collect(c, between):
                for n in range(OUTPUTS):
                    dve.wait_ge(S.y_ps, c * OUTPUTS + n + 1)
                    part = ff[:, n // 2, (n % 2) * HALF:(n % 2 + 1) * HALF]
                    nc.vector.tensor_tensor(part, part, y_ps[n % 3][:, :], ALU.add).then_inc(S.y_free, 1)
                    if n in between:
                        between[n]()

            def pair(c, parity, more=True, before=True):
                uT(c * 2 + 1, 1)
                steps = {}
                for n in range(3):
                    steps[1 + n] = lambda n=n: weigh(c, 0, n)
                    steps[7 + n] = lambda n=n: rest(c, 0, parity, n)
                if before:
                    collect(c - 1, steps)
                else:
                    for n in sorted(steps):
                        steps[n]()
                if more:
                    uT(c * 2 + 2, 0)
                for n in range(3):
                    weigh(c, 1, n)
                for n in range(3):
                    rest(c, 1, parity, n)
            uT(0, 0)
            for t in range(TILES):
                dve.wait_ge(S.h_hi, t + 1)
                tok = slice(t * P, (t + 1) * P)
                nc.vector.tensor_tensor(h_lo[:, :, tok], h_raw[t].rearrange("p (k t) -> p k t", k=KD),
                                        h_hi[:, :, tok].bitcast(F32), ALU.subtract).then_inc(S.h_lo, 1)

            def first_pair():
                pair(0, 0, before=False)
                dve.wait_ge(S.zero, 2)
            pairs(dve, first_pair, pair, lambda: pair(PAIRS - 1, 1, more=False))

            def add_x1(t):
                dve.wait_ge(S.weighted, t + 1)
                dve.wait_ge((S.x1_0, S.x1_1, S.x1_2, S.x1_3)[t % 4], t // 4 * 16 + 16)
                nc.vector.tensor_tensor(ff[:, t, :], ff[:, t, :], x1[t % 4], ALU.add).then_inc(S.summed, 1)

            def mean_of(t):
                dve.wait_ge(S.sumsq, t + 1)
                nc.vector.tensor_scalar(mean[:, t:t + 1], sumsq[:, t:t + 1], 1.0 / D, EPS, ALU.mult, ALU.add)\
                    .then_inc(S.mean, 1)

            def normed(t):
                if t == 0:
                    dve.wait_ge(S.g_last, 16)
                dve.wait_ge(S.rstd, t + 1)
                nc.vector.scalar_tensor_tensor(out=ff[:, t, :], in0=ff[:, t, :], scalar=rstd[:, t:t + 1], in1=g_last[:, :],
                                               op0=ALU.mult, op1=ALU.mult).then_inc(S.final, 1)

            def finish(t):
                if 1 <= t <= TILES:
                    add_x1(t - 1)
                if 2 <= t <= TILES + 1:
                    mean_of(t - 2)
                if 3 <= t:
                    normed(t - 3)
            collect(PAIRS - 1, {t * 2 + 1: lambda t=t: finish(t) for t in range(TILES)})
            for t in range(TILES, TILES + 3):
                finish(t)

        @block.tensor
        def _(pe):
            pe.sem_inc(S.uT_ps, 1)
            pe.wait_ge(S.consts, 16)
            u_loaded = [S.u0, S.u1]

            def transpose_u(e, c, s):
                pe.wait_ge(u_loaded[s], c * 16 + 16)
                wait(pe, S.uT_lo, e * 2)
                for k in range(KD):
                    last = nc.tensor.transpose(uT_ps[:, k, :], u[s][:, k * P:(k + 1) * P], ident[:, :])
                last.then_inc(S.uT_ps, 1)

            def first_product(e, s):
                pe.wait_ge(S.uT_lo, e * 2 + 2)
                for n in range(3):
                    if isinstance(e, int) and e == 0:
                        pe.wait_ge(S.h_lo, n * 3 + 3)
                    wait(pe, S.gelu, e * 3 - 2 + n)
                    tok = slice(n * GROUP, (n + 1) * GROUP)
                    for k in range(KD):
                        for m, (lhs, rhs) in enumerate(((uT_lo, h_hi), (uT_hi, h_lo), (uT_hi, h_hi))):
                            last = nc.tensor.matmul(a_ps[n][:, 0:GROUP], lhs[s][:, k, :], rhs[:, k, tok],
                                                    start=k == 0 and m == 0, stop=k == KD - 1 and m == 2)
                    last.then_inc(S.act_ps, 1)

            def second_product(c, parity):
                pe.wait_ge(S.m_lo, c * 6 + 6)
                pe.wait_ge(S.v_lo, c * 2 + 2)
                for n in range(OUTPUTS):
                    tok = slice(n // 2 * P, (n // 2 + 1) * P)
                    col = slice((n % 2) * HALF, (n % 2 + 1) * HALF)
                    pe.wait_ge(S.y_free, c * OUTPUTS + n + 1)
                    for j in range(2):
                        b = buffer(j, parity)
                        for m, (lhs, rhs) in enumerate(((m_lo, v_hi), (m_hi, v_lo), (m_hi, v_hi))):
                            last = nc.tensor.matmul(y_ps[n % 3][:, :], lhs[b][:, tok], rhs[b][:, col],
                                                    start=j == 0 and m == 0, stop=j == 1 and m == 2)
                    last.then_inc(S.y_ps, 1)

            def pair(c, parity, more=True, before=True):
                transpose_u(c * 2 + 1, c, 1)
                first_product(c * 2, 0)
                if before:
                    second_product(c - 1, 1 - parity)
                if more:
                    transpose_u(c * 2 + 2, c + 1, 0)
                first_product(c * 2 + 1, 1)
            transpose_u(0, 0, 0)
            pairs(pe, lambda: pair(0, 0, before=False), pair, lambda: pair(PAIRS - 1, 1, more=False))
            second_product(PAIRS - 1, 1)


def program(nc, a, outs):
    y_prompt, y_sample, pool_prompt_out, pool_sample_out, v_sample_out = outs
    with ExitStack() as ctx:
        mod_rows = nc.dram_tensor("mod_rows", (1 + STREAMS, MODS, D), F32, kind="Internal").ap()
        x1_rows = nc.dram_tensor("x1_rows", (TILES, P, D), F32, kind="Internal").ap()
        h2T_tiles = nc.dram_tensor("h2T_tiles", (TILES, P, D), F32, kind="Internal").ap()
        gate_blocks = nc.dram_tensor("gate_blocks", (BLOCKS, P, NKEYS, BLOCK), F32, kind="Internal").ap()
        shared = ctx.enter_context(nc.sbuf_tensor("shared", [P, SHARED], F32))
        modulation(nc, ctx, a["c_prompt"], a["c_sample"], a["w_ada"][0], a["b_ada"][0], a["g_norm1"][0],
                   a["g_norm2"][0], a["identity"], a["w_in"][0], shared, mod_rows)
        mixing(nc, ctx, a["x_prompt"], a["x_sample"], a["cache_pool"], a["pool_w"][0],
               a["pool_scale"][0], a["gmlp_norm_g"][0], a["gmlp_ws"][0], a["gmlp_bs"][0], a["w_out"][0],
               a["peer_wq"][0], a["identity"], a["bands"], shared, mod_rows, x1_rows, h2T_tiles, pool_prompt_out,
               pool_sample_out, v_sample_out)
        routing(nc, ctx, a["peer_wq"][0], a["peer_keys"][0], a["peer_u"][0], a["peer_v"][0], a["identity"], shared,
                h2T_tiles, gate_blocks)
        experts(nc, ctx, a["peer_u"][0], a["peer_v"][0], a["g_final"], a["identity"], shared, mod_rows, x1_rows,
                gate_blocks, y_prompt, y_sample)


_INS = ['x_prompt', 'x_sample', 'cache_pool', 'c_prompt', 'c_sample', 'w_ada', 'b_ada', 'g_norm1', 'w_in', 'pool_w',
        'pool_scale', 'gmlp_norm_g', 'gmlp_ws', 'gmlp_bs', 'w_out', 'g_norm2', 'peer_wq', 'peer_keys', 'peer_u',
        'peer_v', 'g_final']
_OUTS = [(1, 1024, 1024), (8, 16, 1024), (1, 1, 15, 512), (1, 8, 15, 512), (1, 8, 16, 512)]


def _constants():
    import numpy as np
    bands = np.zeros((P, 5, GROUPS, P), np.float32)
    for g in range(GROUPS):
        w = 2 << g
        for t in range(P):
            for j in range(P):
                back = t - j
                if 0 <= back < w:
                    bands[j, 0, g, t] = 1 / min(t + 1, w)
                    bands[j, 1, g, t] = 1 / w
                    if j // STEP == t // STEP:
                        bands[j, 2, g, t] = 1 / w
                if back + P < w:
                    bands[j, 3, g, t] = 1 / w
                if j < STREAMS * HIST and j // HIST == t // STEP and t % STEP - (j % HIST - HIST) < w:
                    bands[j, 4, g, t] = 1 / w
            bands[t, 0:3, g, t] -= 1
    return {"identity": np.eye(P, dtype=np.float32), "bands": bands}


def kernel(**inputs):
    import numpy as _np
    import concourse.bacc as _bacc
    from concourse.bass_utils import run_bass_kernel_spmd as _run

    nc = _bacc.Bacc("TRN2", target_bir_lowering=False, num_devices=1)
    arrays, args = {}, {}
    given = {name: _np.ascontiguousarray(inputs[name]) for name in _INS}
    given.update(_constants())
    for name, a in given.items():
        arrays[f"in_{name}"] = a
        args[name] = nc.dram_tensor(f"in_{name}", a.shape, F32, kind="ExternalInput").ap()
    outs = [nc.dram_tensor(f"out_{i}", shape, F32, kind="ExternalOutput").ap() for i, shape in enumerate(_OUTS)]
    program(nc, args, outs)
    r = _run(nc, [arrays], core_ids=[0])
    return tuple(r.results[0][f"out_{i}"] for i in range(len(_OUTS)))
```
